# Optimizing a Trainium2 kernel written in Bass

```python
import jax, jax.numpy as jnp
from jax import lax
import numpy as np

D_MODEL = 1024
BATCH = 1
SEQ = 256
DEPTH = 2

GRID_W = 64
HEAD_DIM = 64
Q_BLOCK = 128
NORM_EPS = 1e-6
NEG_INF = -1e30
ROPE_THETA = 500000.0
PARTIAL_ROPE_DIM = HEAD_DIM // 4
GQA_Q_HEADS = 8
GQA_KV_HEADS = 2
GQA_GROUP = GQA_Q_HEADS // GQA_KV_HEADS
AXIAL_THETA = 10000.0
MLA_HEADS = 8
MLA_Q_RANK = 256
MLA_KV_RANK = 128
MLA_NOPE_DIM = 64
MLA_ROPE_DIM = 32
MLA_V_DIM = 64
MLA_ROPE_THETA = 10000.0
AB_SPLITS = (GQA_Q_HEADS * HEAD_DIM,
             GQA_Q_HEADS * HEAD_DIM + GQA_KV_HEADS * HEAD_DIM,
             GQA_Q_HEADS * HEAD_DIM + 2 * GQA_KV_HEADS * HEAD_DIM,
             GQA_Q_HEADS * HEAD_DIM + 2 * GQA_KV_HEADS * HEAD_DIM + MLA_Q_RANK,
             GQA_Q_HEADS * HEAD_DIM + 2 * GQA_KV_HEADS * HEAD_DIM + MLA_Q_RANK + MLA_KV_RANK)
AB_IN_WIDTH = AB_SPLITS[-1] + MLA_ROPE_DIM
AB_OUT_WIDTH = GQA_Q_HEADS * HEAD_DIM + MLA_HEADS * MLA_V_DIM
DIL_CONFIGS = ((128, 1), (512, 4), (2048, 16))
DIL_GROUPS = len(DIL_CONFIGS)
DIL_HEADS = 8
DIL_IN_WIDTH = DIL_GROUPS * 3 * DIL_HEADS * HEAD_DIM
DIL_OUT_WIDTH = DIL_HEADS * HEAD_DIM
D_FF = 3584
N_EXPERTS = 8
TOP_K = 2
D_FF_EXPERT = 3584
MOE_BLOCK = 256
PLE_DIM = 256
N_EVEN = (DEPTH + 1) // 2
N_ODD = DEPTH // 2

kernel_name = 'hybrid_gqa_mla_dilated_moe_encoder'

def rms_norm(x, g):
    xf = x.astype(jnp.float32)
    y = xf * lax.rsqrt(jnp.mean(xf * xf, axis=-1, keepdims=True) + NORM_EPS)
    return (y * g.astype(jnp.float32)).astype(x.dtype)

def rotary_tables(pos, dim, theta):
    exponent = jnp.arange(0, dim, 2, dtype=jnp.float32) / dim
    inv_freq = jnp.power(jnp.float32(theta), -exponent)
    ang = pos.astype(jnp.float32)[:, None] * inv_freq[None, :]
    return jnp.cos(ang), jnp.sin(ang)

def apply_rotary(x, cos, sin):
    half = x.shape[-1] // 2
    shape = (cos.shape[0],) + (1,) * (x.ndim - 3) + (half,)
    c = cos.reshape(shape)
    s_ = sin.reshape(shape)
    xf = x.astype(jnp.float32)
    x1, x2 = xf[..., :half], xf[..., half:]
    return jnp.concatenate([x1 * c - x2 * s_, x2 * c + x1 * s_], axis=-1).astype(x.dtype)

def axial_rotary(x, row_cs, col_cs):
    half = x.shape[-1] // 2
    return jnp.concatenate([apply_rotary(x[..., :half], *row_cs),
                            apply_rotary(x[..., half:], *col_cs)], axis=-1)

def dense_blocked_attention(q, k, v, scale):
    b, s, hk, g, dk = q.shape
    nblk = s // Q_BLOCK
    qb = jnp.moveaxis(q.reshape(b, nblk, Q_BLOCK, hk, g, dk), 1, 0)

    def one_block(qblk):
        sc = jnp.einsum('bqhgd,bkhd->bhgqk', qblk, k, preferred_element_type=jnp.float32) * scale
        probs = jax.nn.softmax(sc, axis=-1)
        return jnp.einsum('bhgqk,bkhe->bqhge', probs.astype(v.dtype), v)

    o = lax.map(one_block, qb)
    return jnp.moveaxis(o, 0, 1).reshape(b, s, hk, g, v.shape[-1])

def dilated_window_attention(q, k, v, dilation, half, scale):
    b, s, h, dh = q.shape
    L = s // dilation
    nb = -(-L // half)
    Lp = nb * half
    z = b * dilation

    def residues(x):
        e = x.shape[-1]
        return x.reshape(b, L, dilation, h, e).transpose(0, 2, 1, 3, 4).reshape(z, L, h, e)

    def windows(x):
        e = x.shape[-1]
        xp = jnp.pad(residues(x), ((0, 0), (half, Lp - L + half), (0, 0), (0, 0)))
        xp = xp.reshape(z, nb + 2, half, h, e)
        return jnp.concatenate([xp[:, :-2], xp[:, 1:-1], xp[:, 2:]], axis=2)

    qs = jnp.pad(residues(q), ((0, 0), (0, Lp - L), (0, 0), (0, 0))).reshape(z, nb, half, h, dh)
    kw = windows(k)
    vw = windows(v)
    qi = jnp.arange(nb)[:, None] * half + jnp.arange(half)[None, :]
    ki = jnp.arange(nb)[:, None] * half - half + jnp.arange(3 * half)[None, :]
    mask = ((jnp.abs(qi[:, :, None] - ki[:, None, :]) <= half)
            & (ki[:, None, :] >= 0) & (ki[:, None, :] < L))
    sc = jnp.einsum('znqhd,znkhd->znhqk', qs, kw, preferred_element_type=jnp.float32) * scale
    sc = jnp.where(mask[None, :, None], sc, NEG_INF)
    m = jnp.max(sc, axis=-1, keepdims=True)
    pexp = jnp.exp(sc - m)
    l = jnp.sum(pexp, axis=-1, keepdims=True)
    o = jnp.einsum('znhqk,znkhd->znqhd', (pexp / l).astype(v.dtype), vw)
    lse = jnp.swapaxes((m + jnp.log(l))[..., 0], 2, 3)

    def unresidue(y):
        e = y.shape[-1]
        y = y.reshape(b, dilation, Lp, h, e)[:, :, :L]
        return y.transpose(0, 2, 1, 3, 4).reshape(b, s, h, e)

    o = unresidue(o.reshape(z, Lp, h, dh))
    lse = unresidue(lse.reshape(z, Lp, h, 1))[..., 0]
    return o, lse

def mixer_gqa_mla(a, w_in, gqa_qn, gqa_kn, mla_qn, w_uq, mla_kvn, w_ukv, w_out, row_cs, col_cs, mla_cs):
    b, s, _ = a.shape
    zin = a @ w_in
    q_a, k_a, v_a, c_q, c_kv, k_r = jnp.split(zin, AB_SPLITS, axis=-1)
    q_a = rms_norm(q_a.reshape(b, s, GQA_KV_HEADS, GQA_GROUP, HEAD_DIM), gqa_qn)
    k_a = rms_norm(k_a.reshape(b, s, GQA_KV_HEADS, HEAD_DIM), gqa_kn)
    v_a = v_a.reshape(b, s, GQA_KV_HEADS, HEAD_DIM)
    q_a = axial_rotary(q_a, row_cs, col_cs)
    k_a = axial_rotary(k_a, row_cs, col_cs)
    o_a = dense_blocked_attention(q_a, k_a, v_a, HEAD_DIM ** -0.5).reshape(b, s, GQA_Q_HEADS * HEAD_DIM)
    q_m = (rms_norm(c_q, mla_qn) @ w_uq).reshape(b, s, MLA_HEADS, MLA_NOPE_DIM + MLA_ROPE_DIM)
    q_m = jnp.concatenate([q_m[..., :MLA_NOPE_DIM], apply_rotary(q_m[..., MLA_NOPE_DIM:], *mla_cs)], axis=-1)
    kv = (rms_norm(c_kv, mla_kvn) @ w_ukv).reshape(b, s, MLA_HEADS, MLA_NOPE_DIM + MLA_V_DIM)
    k_rope = apply_rotary(k_r.reshape(b, s, 1, MLA_ROPE_DIM), *mla_cs)
    k_m = jnp.concatenate([kv[..., :MLA_NOPE_DIM],
                           jnp.broadcast_to(k_rope, (b, s, MLA_HEADS, MLA_ROPE_DIM))], axis=-1)
    v_m = kv[..., MLA_NOPE_DIM:]
    o_m = dense_blocked_attention(q_m[:, :, :, None, :], k_m, v_m,
                                  (MLA_NOPE_DIM + MLA_ROPE_DIM) ** -0.5).reshape(b, s, MLA_HEADS * MLA_V_DIM)
    return jnp.concatenate([o_a, o_m], axis=-1) @ w_out

def mixer_dilated(a, w_qkv, w_out, part_cs):
    b, s, _ = a.shape
    zin = (a @ w_qkv).reshape(b, s, DIL_GROUPS, 3, DIL_HEADS, HEAD_DIM)

    def partial_rope(x):
        return jnp.concatenate([apply_rotary(x[..., :PARTIAL_ROPE_DIM], *part_cs),
                                x[..., PARTIAL_ROPE_DIM:]], axis=-1)

    q = partial_rope(zin[:, :, :, 0])
    k = partial_rope(zin[:, :, :, 1])
    v = zin[:, :, :, 2]
    outs, lses = [], []
    for gi, (window, dilation) in enumerate(DIL_CONFIGS):
        o_g, lse_g = dilated_window_attention(q[:, :, gi], k[:, :, gi], v[:, :, gi],
                                              dilation, window // (2 * dilation), HEAD_DIM ** -0.5)
        outs.append(o_g)
        lses.append(lse_g)
    alpha = jax.nn.softmax(jnp.stack(lses, axis=0), axis=0)
    o = jnp.sum(alpha[..., None] * jnp.stack(outs, axis=0).astype(jnp.float32), axis=0).astype(a.dtype)
    return o.reshape(b, s, DIL_OUT_WIDTH) @ w_out

def swiglu(a, w_gate, w_up, w_down):
    return (jax.nn.silu(a @ w_gate) * (a @ w_up)) @ w_down

def moe_swiglu(a, w_router, w_gate, w_up, w_down):
    b, s, d = a.shape
    n = b * s
    nk = n * TOP_K
    af = a.reshape(n, d)
    logits = jnp.einsum('nd,de->ne', af, w_router, preferred_element_type=jnp.float32)
    top_logits, top_idx = lax.top_k(logits, TOP_K)
    gates = jax.nn.softmax(top_logits, axis=-1)
    flat_e = top_idx.reshape(nk).astype(jnp.int32)
    flat_tok = jnp.arange(nk, dtype=jnp.int32) // TOP_K
    flat_g = gates.reshape(nk)
    order = jnp.argsort(flat_e)
    sorted_e = flat_e[order]
    counts = jnp.bincount(flat_e, length=N_EXPERTS).astype(jnp.int32)
    padded = (counts + MOE_BLOCK - 1) // MOE_BLOCK * MOE_BLOCK
    end_pad = jnp.cumsum(padded)
    start_pad = end_pad - padded
    start_unp = jnp.cumsum(counts) - counts
    dest = start_pad[sorted_e] + jnp.arange(nk, dtype=jnp.int32) - start_unp[sorted_e]
    n_slots = nk + N_EXPERTS * MOE_BLOCK
    n_blk = n_slots // MOE_BLOCK
    slot_tok = jnp.zeros((n_slots,), jnp.int32).at[dest].set(flat_tok[order])
    slot_gate = jnp.zeros((n_slots,), jnp.float32).at[dest].set(flat_g[order])
    blk_start = jnp.arange(n_blk, dtype=jnp.int32) * MOE_BLOCK
    blk_e = jnp.minimum(jnp.searchsorted(end_pad, blk_start, side='right'), N_EXPERTS - 1)
    xs = af[slot_tok].reshape(n_blk, MOE_BLOCK, d)

    def expert_block(args):
        xb, e = args
        return (jax.nn.silu(xb @ w_gate[e]) * (xb @ w_up[e])) @ w_down[e]

    ys = lax.map(expert_block, (xs, blk_e)).reshape(n_slots, d)
    out = jnp.zeros((n, d), jnp.float32).at[slot_tok].add(ys.astype(jnp.float32) * slot_gate[:, None])
    return out.astype(a.dtype).reshape(b, s, d)

def setup_inputs(seed: int = 0) -> dict:
    key = jax.random.key(seed)
    ks = list(jax.random.split(key, 32))
    counter = [0]

    def nk():
        counter[0] += 1
        return ks[counter[0] - 1]

    def w(shape, fan_in):
        return jax.random.normal(nk(), shape, jnp.float32) * (fan_in ** -0.5)

    def g(shape):
        return 1.0 + 0.05 * jax.random.normal(nk(), shape, jnp.float32)

    D = D_MODEL
    return {
        'x': jax.random.normal(nk(), (BATCH, SEQ, D), jnp.float32),
        'p': jax.random.normal(nk(), (DEPTH, BATCH, SEQ, PLE_DIM), jnp.float32),
        'mix_pre_g': g((DEPTH, D)),
        'mix_post_g': g((DEPTH, D)),
        'ffn_pre_g': g((DEPTH, D)),
        'ffn_post_g': g((DEPTH, D)),
        'ple_w_proj': w((DEPTH, PLE_DIM, D), PLE_DIM),
        'ple_gate_norm_g': g((DEPTH, D)),
        'ple_w_gate': w((DEPTH, D, D), D),
        'ple_post_g': g((DEPTH, D)),
        'ab_w_in': w((N_EVEN, D, AB_IN_WIDTH), D),
        'gqa_q_norm_g': g((N_EVEN, HEAD_DIM)),
        'gqa_k_norm_g': g((N_EVEN, HEAD_DIM)),
        'mla_q_norm_g': g((N_EVEN, MLA_Q_RANK)),
        'mla_w_uq': w((N_EVEN, MLA_Q_RANK, MLA_HEADS * (MLA_NOPE_DIM + MLA_ROPE_DIM)), MLA_Q_RANK),
        'mla_kv_norm_g': g((N_EVEN, MLA_KV_RANK)),
        'mla_w_ukv': w((N_EVEN, MLA_KV_RANK, MLA_HEADS * (MLA_NOPE_DIM + MLA_V_DIM)), MLA_KV_RANK),
        'ab_w_out': w((N_EVEN, AB_OUT_WIDTH, D), AB_OUT_WIDTH),
        'ffn_w_gate': w((N_EVEN, D, D_FF), D),
        'ffn_w_up': w((N_EVEN, D, D_FF), D),
        'ffn_w_down': w((N_EVEN, D_FF, D), D_FF),
        'dil_w_qkv': w((N_ODD, D, DIL_IN_WIDTH), D),
        'dil_w_out': w((N_ODD, DIL_OUT_WIDTH, D), DIL_OUT_WIDTH),
        'moe_w_router': w((N_ODD, D, N_EXPERTS), D),
        'moe_w_gate': w((N_ODD, N_EXPERTS, D, D_FF_EXPERT), D),
        'moe_w_up': w((N_ODD, N_EXPERTS, D, D_FF_EXPERT), D),
        'moe_w_down': w((N_ODD, N_EXPERTS, D_FF_EXPERT, D), D_FF_EXPERT),
    }

def reference(x, p, mix_pre_g, mix_post_g, ffn_pre_g, ffn_post_g, ple_w_proj, ple_gate_norm_g,
              ple_w_gate, ple_post_g, ab_w_in, gqa_q_norm_g, gqa_k_norm_g, mla_q_norm_g, mla_w_uq,
              mla_kv_norm_g, mla_w_ukv, ab_w_out, ffn_w_gate, ffn_w_up, ffn_w_down, dil_w_qkv,
              dil_w_out, moe_w_router, moe_w_gate, moe_w_up, moe_w_down):
    s = x.shape[1]
    rows = s // GRID_W
    t = jnp.arange(s, dtype=jnp.int32)
    row_pos = jnp.repeat(jnp.arange(rows, dtype=jnp.int32), GRID_W)
    col_pos = jnp.tile(jnp.arange(GRID_W, dtype=jnp.int32), rows)
    row_cs = rotary_tables(row_pos, HEAD_DIM // 2, AXIAL_THETA)
    col_cs = rotary_tables(col_pos, HEAD_DIM // 2, AXIAL_THETA)
    mla_cs = rotary_tables(t, MLA_ROPE_DIM, MLA_ROPE_THETA)
    part_cs = rotary_tables(t, PARTIAL_ROPE_DIM, ROPE_THETA)

    h = x
    for i in range(DEPTH):
        j = i // 2
        a = rms_norm(h, mix_pre_g[i])
        if i % 2 == 0:
            m = mixer_gqa_mla(a, ab_w_in[j], gqa_q_norm_g[j], gqa_k_norm_g[j], mla_q_norm_g[j],
                              mla_w_uq[j], mla_kv_norm_g[j], mla_w_ukv[j], ab_w_out[j],
                              row_cs, col_cs, mla_cs)
        else:
            m = mixer_dilated(a, dil_w_qkv[j], dil_w_out[j], part_cs)
        h = h + rms_norm(m, mix_post_g[i])
        a = rms_norm(h, ffn_pre_g[i])
        if i % 2 == 0:
            f = swiglu(a, ffn_w_gate[j], ffn_w_up[j], ffn_w_down[j])
        else:
            f = moe_swiglu(a, moe_w_router[j], moe_w_gate[j], moe_w_up[j], moe_w_down[j])
        h = h + rms_norm(f, ffn_post_g[i])
        gate = jax.nn.sigmoid(rms_norm(h, ple_gate_norm_g[i]) @ ple_w_gate[i])
        e = (p[i].astype(h.dtype) @ ple_w_proj[i]) * gate
        h = h + rms_norm(e, ple_post_g[i])
    return h


_drawn_inputs = setup_inputs


def setup_inputs(seed=0):
    import zlib

    import numpy as np

    out = dict(_drawn_inputs(seed))
    spreads = {}
    factors = {}
    for name, (base, spread) in spreads.items():
        noise = np.random.default_rng([zlib.crc32(name.encode()), seed]).standard_normal(out[name].shape)
        drawn = base * np.exp(spread * noise) if base else spread * noise
        out[name] = __import__('jax').numpy.asarray(drawn.astype(out[name].dtype))
    for name, factor in factors.items():
        out[name] = (out[name] * factor).astype(out[name].dtype)
    return out
```

```python
from contextlib import ExitStack

import numpy as np

import concourse.bass as bass
from concourse import mybir

P = 128
F32 = mybir.dt.float32
I32 = mybir.dt.int32
ACT = mybir.ActivationFunctionType
ALU = mybir.AluOpType
AX_X = mybir.AxisListType.X

SEQ, D = 256, 1024
T = SEQ // P
KD = D // P
EPS = 1e-6
NEG = -1e30
HD = 64
NQ, NKV = 8, 2
ZQ, ZK, ZV, ZCQ, ZCKV, ZKR, ZW = 0, 512, 640, 768, 1024, 1152, 1184
MH, MN, MR = 8, 64, 32
MQ = MN + MR
GQA_SCALE = HD ** -0.5
MLA_SCALE = MQ ** -0.5
FF = 3584
FC = 512
NFC = FF // FC
FT = FC // P
DH, DG = 8, 3
PD, PK = 256, 2
NE = 8
BANK = 512

SLOT, RING = 4096, 7
C_IN = 0
IN_TILES = [(0, 3), (3, 3), (6, 2)]
C_UQ, C_UKV = 3, 4
C_ABOUT = 5
C_FFN = 7
N_FFN = 3 * NFC
C_PLE0 = C_FFN + N_FFN
C_QKV = C_PLE0 + 3
C_DOUT = C_QKV + 9
C_MOE = C_DOUT + 1
assert N_FFN % RING == 0


def ffn_order():
    order = [("g", 0), ("u", 0)]
    for c in range(1, NFC):
        order += [("g", c), ("u", c), ("d", c - 1)]
    return order + [("d", NFC - 1)]


FFN = ffn_order()
FFN_AT = {key: n for n, key in enumerate(FFN)}

TAB = {}
_w = 0
for _n, _c in (("ident", P), ("axC", T * HD), ("axS", T * HD), ("mlC", T * MR), ("mlS", T * MR),
               ("diC", T * 16), ("diS", T * 16), ("rev", T * NE)):
    TAB[_n] = (_w, _c)
    _w += _c
TAB_RES = _w
TAB_MOE = _w
TAB_MASK = TAB_MOE + 4 * P
TAB_ALL = TAB_MASK + T * BANK


def hybrid_encoder(nc, x, p, mix_pre_g, mix_post_g, ffn_pre_g, ffn_post_g, ple_w_proj, ple_gate_norm_g,
                   ple_w_gate, ple_post_g, ab_w_in, gqa_q_norm_g, gqa_k_norm_g, mla_q_norm_g, mla_w_uq,
                   mla_kv_norm_g, mla_w_ukv, ab_w_out, ffn_w_gate, ffn_w_up, ffn_w_down, dil_w_qkv,
                   dil_w_out, moe_w_router, moe_w_gate, moe_w_up, moe_w_down, tables, out):
    ctx = ExitStack()
    with ctx:
        def sb(name, shape, dt=F32):
            return ctx.enter_context(nc.sbuf_tensor(name, shape, dt))

        def sem(name):
            return ctx.enter_context(nc.semaphore(name))

        ps = ctx.enter_context(nc.psum_tensor("ps", [P, 8, BANK], F32))

        ring = sb("ring", [P, RING, SLOT])
        h = sb("h", [P, T, D])
        xn = sb("xn", [P, T, D])
        xT = sb("xT", [P, KD, SEQ])
        gb = sb("gb", [P, 3, D])
        tab = sb("tab", [P, TAB_RES])
        gT = sb("gT", [P, 51])
        grow = sb("grow", [P, 2, HD])
        rot = sb("rot", [P, 4, T, HD])
        wr = sb("wr", [P, KD, NE])
        eps = sb("eps", [P, 1])
        ss = sb("ss", [P, T])
        ssl = sb("ssl", [P, T])
        rstd = sb("rstd", [P, T])
        prstd = sb("prstd", [P, T])
        hss = sb("hss", [P, T, 12])
        hrs = sb("hrs", [P, T, 12])
        smax = sb("smax", [P, 3, T])
        snm = sb("snm", [P, 3, T])
        ssum = sb("ssum", [P, 3, T])
        srec = sb("srec", [P, 3, T])
        rt = sb("rt", [P, 10, T * NE])
        rs = sb("rs", [P, 8, T])
        posm = sb("posm", [P, T, NE + 1])
        gate = sb("gate", [P, T, NE + 1])
        cnt = sb("cnt", [P, 2])
        cnti = sb("cnti", [P, 1], I32)
        ARENA = 12608
        arena = sb("arena", [P, ARENA])

        used = [0]

        def carve(n, reset=None):
            if reset is not None:
                used[0] = reset
            a = used[0]
            used[0] += n
            assert used[0] <= ARENA
            return arena[:, a:a + n]

        def table(name, *dims):
            a, n = TAB[name]
            return tab[:, a:a + n]

        ident = table("ident")

        z = carve(T * ZW, 0).rearrange("p (t n) -> p t n", t=T)
        rows = carve(MH * MQ * T)
        qr = rows[:, 0:T * 512].rearrange("p (t n) -> p t n", t=T)
        kr = rows[:, T * 512:T * 768].rearrange("p (t j u n) -> p t j u n", t=T, j=NKV, u=2)
        km = rows.rearrange("p (t h n) -> p t h n", t=T, h=MH)
        qT = carve(4 * SEQ).rearrange("p (c n) -> p c n", c=4)
        kT = carve(NKV * SEQ).rearrange("p (c n) -> p c n", c=NKV)
        vm = carve(T * MH * HD).rearrange("p (t h n) -> p t h n", t=T, h=MH)
        qmT = carve(MH * SEQ).rearrange("p (h n) -> p h n", h=MH)
        kmT = carve(MH * SEQ).rearrange("p (h n) -> p h n", h=MH)
        latT = kmT[:, 0:3, :]
        qm = xn[:, :, :].rearrange("p t n -> p (t n)")[:, 0:T * MH * MQ].rearrange("p (t h n) -> p t h n", t=T, h=MH)
        mtmp = xn[:, :, :].rearrange("p t n -> p (t n)")[:, T * MH * MQ:T * D]
        probs0 = carve(3 * BANK).rearrange("p (b n) -> p b n", b=3)
        probT0 = carve(BANK)
        dq = carve(DG * 4 * SEQ, 0).rearrange("p (g c n) -> p g c n", g=DG, c=4)
        dk = carve(DG * 4 * SEQ).rearrange("p (g c n) -> p g c n", g=DG, c=4)
        dv = carve(DG * T * 512).rearrange("p (g t n) -> p g t n", g=DG, t=T)
        mask = carve(T * BANK).rearrange("p (t n) -> p t n", t=T)
        probs1 = carve(3 * BANK).rearrange("p (b n) -> p b n", b=3)
        probT1 = carve(BANK)
        dtmp = probs1
        sg = carve(FT * SEQ, 0).rearrange("p (f n) -> p f n", f=FT)
        hT = carve(2 * FT * SEQ).rearrange("p (b f n) -> p b f n", b=2, f=FT)
        xg = carve(KD * P, 0).rearrange("p (k n) -> p k n", k=KD)
        msg = carve(BANK)
        mh = carve(2 * BANK).rearrange("p (b n) -> p b n", b=2)
        mhT = carve(2 * BANK).rearrange("p (b n) -> p b n", b=2)
        ysb = carve(D)
        acc = carve(T * D).rearrange("p (t n) -> p t n", t=T)
        sel = carve(T * P).rearrange("p (t n) -> p t n", t=T)
        selg = carve(T * P).rearrange("p (t n) -> p t n", t=T)
        selT = carve(T * P).rearrange("p (t n) -> p t n", t=T)
        moetab = carve(4 * P)
        tri, ones, iota = moetab[:, 0:P], moetab[:, P:2 * P], moetab[:, 2 * P:4 * P]
        pe_rows = carve(T * PD, ARENA - 2 * T * PD).rearrange("p (t n) -> p t n", t=T)
        pT = carve(PK * SEQ).rearrange("p (k n) -> p k n", k=PK)
        small = pe_rows.rearrange("p t n -> p (t n)")[0:51, 0:P]

        tab_in = sem("tab_in")
        gain_in = sem("gain_in")
        grow_in = sem("grow_in")
        wr_in = sem("wr_in")
        x_in = sem("x_in")
        gb_in = [sem(f"gb_in{i}") for i in range(3)]
        mask_in = sem("mask_in")
        moetab_in = sem("moetab_in")
        p_in = sem("p_in")
        slot_in = [sem(f"slot_in{i}") for i in range(RING)]
        chunk_used = sem("chunk_used")
        tail_in = [sem(f"tail_in{i}") for i in range(3)]
        eps_ok = sem("eps_ok")
        acc_zero = sem("acc_zero")
        mqT_ok = sem("mqT_ok")
        mkT_ok = sem("mkT_ok")
        out_done = sem("out_done")
        dve_step = sem("dve_step")
        act_step = sem("act_step")
        gt_tr = sem("gt_tr")
        gt_ok = sem("gt_ok")
        rstd_ok = sem("rstd_ok")
        xn_ok = sem("xn_ok")
        xn_tr = sem("xn_tr")
        xT_ok = sem("xT_ok")
        y_ok = sem("y_ok")
        ysq_ok = sem("ysq_ok")
        prstd_ok = sem("prstd_ok")
        h_ok = sem("h_ok")
        z_mm = sem("z_mm")
        z_ok = sem("z_ok")
        hss_ok = sem("hss_ok")
        hrs_ok = sem("hrs_ok")
        lat_tr = sem("lat_tr")
        lat_ok = sem("lat_ok")
        up_mm = sem("up_mm")
        up_ok = sem("up_ok")
        qk_ok = sem("qk_ok")
        qk_tr = sem("qk_tr")
        qkT_ok = sem("qkT_ok")
        mrow_ok = sem("mrow_ok")
        m_tr = sem("m_tr")
        mT_ok = sem("mT_ok")
        sc_mm = sem("sc_mm")
        sc_max = sem("sc_max")
        sc_exp = sem("sc_exp")
        pr_ok = sem("pr_ok")
        pr_tr = sem("pr_tr")
        prT_ok = sem("prT_ok")
        pv_mm = sem("pv_mm")
        oT_ok = sem("oT_ok")
        f_g = sem("f_g")
        f_silu = sem("f_silu")
        f_u = sem("f_u")
        f_h = sem("f_h")
        p_tr = sem("p_tr")
        pT_ok = sem("pT_ok")
        pl_mm = sem("pl_mm")
        pl_exp = sem("pl_exp")
        dz_mm = sem("dz_mm")
        dz_ok = sem("dz_ok")
        dr_ok = sem("dr_ok")
        d_tr = sem("d_tr")
        dT_ok = sem("dT_ok")
        r_mm = sem("r_mm")
        r_ev = sem("r_ev")
        r_mask = sem("r_mask")
        r_gap = sem("r_gap")
        r_eg = sem("r_eg")
        r_pos = sem("r_pos")
        r_cnt = sem("r_cnt")
        m_sel = sem("m_sel")
        m_ga = sem("m_ga")
        m_xg = sem("m_xg")
        m_st = sem("m_st")
        m_sT = sem("m_sT")
        m_silu = sem("m_silu")
        m_h = sem("m_h")
        m_t = sem("m_t")
        m_ht = sem("m_ht")
        m_y = sem("m_y")
        m_ysb = sem("m_ysb")
        m_sc = sem("m_sc")
        m_acc = sem("m_acc")
        m_end = sem("m_end")

        def kt_rows(w):
            return w.rearrange("(k p) n -> p k n", p=P)

        chunks = []
        for a, n in IN_TILES:
            chunks.append((kt_rows(ab_w_in[0])[:, a:a + n, :], n, ZW))
        chunks.append((kt_rows(mla_w_uq[0]), 2, MH * MQ))
        chunks.append((mla_w_ukv[0].rearrange("(k p) n -> p k n", p=P), 1, MH * 2 * HD))
        for a in range(2):
            chunks.append((kt_rows(ab_w_out[0])[:, 4 * a:4 * a + 4, :], 4, D))

        def ffn_source(kind, c, wg, wu, wd):
            if kind == "d":
                return kt_rows(wd)[:, FT * c:FT * (c + 1), :], FT, D
            return kt_rows(wg if kind == "g" else wu)[:, :, FC * c:FC * (c + 1)], KD, FC

        for kind, c in FFN:
            chunks.append(ffn_source(kind, c, ffn_w_gate[0], ffn_w_up[0], ffn_w_down[0]))

        def ple_source(i):
            return [(kt_rows(ple_w_proj[i]), PK, D)] + [(kt_rows(ple_w_gate[i])[:, 4 * a:4 * a + 4, :], 4, D) for a in range(2)]

        chunks += ple_source(0)
        for c in range(9):
            chunks.append((kt_rows(dil_w_qkv[0])[:, :, FC * c:FC * (c + 1)], KD, FC))
        chunks.append((kt_rows(dil_w_out[0]), 4, D))
        assert len(chunks) == C_MOE

        def chunk(n, tiles, width):
            return ring[:, n % RING, 0:tiles * width].rearrange("p (k n) -> p k n", k=tiles)

        def arrived(eng, n, rounds=0):
            eng.wait_ge(slot_in[n % RING], 16 * (n // RING + 1) + 16 * (N_FFN // RING) * rounds)

        def load(eng, n, source, tiles, width, rounds=0):
            if n >= RING:
                eng.wait_ge(chunk_used, n - RING + 1 + N_FFN * rounds)
            eng.dma_start(chunk(n, tiles, width), source).then_inc(slot_in[n % RING], 16)

        def used(eng, n, rounds=0):
            eng.wait_ge(chunk_used, n + 1 + N_FFN * rounds)

        Y_BEFORE = [0, 1, 2, 4, 5, 7]
        Y_CHUNK = {0: C_ABOUT + 1, 1: C_FFN + N_FFN - 1, 3: C_DOUT}

        def output_ready(eng, j, t):
            if j in Y_CHUNK and t:
                used(eng, Y_CHUNK[j])
            else:
                eng.wait_ge(y_ok, Y_BEFORE[j] + t + 1)

        def first_or_used(eng, s, count, n, second):
            if second:
                used(eng, n)
            else:
                eng.wait_ge(s, count)

        def gates_ready(eng, l, t):
            if l == 0 and t:
                used(eng, C_PLE0 + 2)
            else:
                eng.wait_ge(pl_mm, 2 * l - (1 if l else 0) + t + 1)

        def rounds_before(blk):
            return NE * blk

        def hidden_used(eng, r, c):
            used(eng, C_MOE - 1 if c < 2 else C_MOE + FFN_AT["d", c - 2], r)

        def of(x, n):
            return x.unsqueeze(2).to_broadcast([P, x.shape[1], n])

        def bank(b, n=BANK):
            return ps[:, b, 0:n]

        def pair(b):
            return ps[:, b:b + 2, :].rearrange("p b n -> p (b n)")

        def flat(t):
            return xT[:, :, :].rearrange("p k n -> p (k n)")[:, t * D:(t + 1) * D]

        GAIN = {"mix": 0, "ffn": 16, "ple": 32, "mla": 48}
        PRE = [("mix", 0), ("ffn", 0), ("ple", 0), ("mix", 1), ("ffn", 1), ("ple", 1)]
        N_GQA, N_U0, N_U = NQ, NQ + MH, NQ + MH + T * DH
        S_BANK, T_BANK = (0, 1, 6), (2, 3)

        def probs(u):
            return (probs0 if u < N_U0 else probs1)[:, u % 3, :]

        def probT(u):
            return probT0 if u < N_U0 else probT1

        def oT_before(u):
            return u // 2 if u < N_U0 else N_U0 // 2 + (u - N_U0) // 4

        def o_bank(u):
            return 4 + oT_before(u) % 2

        block = ctx.enter_context(nc.Block())

        @block.sync
        def _(sp):
            sp.dma_start(h[:, :, :], x.rearrange("b (p t) d -> p t (b d)", t=T)).then_inc(x_in, 16)
            for n, (source, tiles, width) in enumerate(chunks):
                load(sp, n, source, tiles, width)

            def expert_loads(blk):
                w_gu = [w.rearrange("a e (k p) n -> (a e) p k n", p=P) for w in (moe_w_gate, moe_w_up)]
                w_d = moe_w_down.rearrange("a e (k p) n -> (a e) p k n", p=P)
                with sp.Fori(0, NE) as e:
                    for j, (kind, c) in enumerate(FFN):
                        if kind == "d":
                            source, tiles, width = w_d[e, :, FT * c:FT * (c + 1), :], FT, D
                        else:
                            source, tiles, width = w_gu[kind == "u"][e, :, :, FC * c:FC * (c + 1)], KD, FC
                        load(sp, C_MOE + j, source, tiles, width, e + rounds_before(blk))

            def tail_loads(rounds):
                for i, (source, tiles, width) in enumerate(ple_source(1)):
                    sp.wait_ge(chunk_used, C_MOE + i - RING + 1 + N_FFN * rounds)
                    sp.dma_start(chunk(C_MOE + i, tiles, width), source).then_inc(tail_in[i], 16)

            expert_loads(0)
            sp.wait_ge(r_cnt, 1)
            big = sp.value_load(cnti[0:1, 0:1])
            with sp.If(big > P):
                expert_loads(1)
                tail_loads(2 * NE)
            with sp.Else():
                tail_loads(NE)
            for t in range(T):
                sp.wait_ge(h_ok, 2 * 5 + t + 1)
                sp.dma_start(out.rearrange("b (p t) d -> p t (b d)", t=T)[:, t, :], h[:, t, :]).then_inc(out_done, 16)
            sp.wait_ge(out_done, 16 * T)

        @block.gpsimd
        def _(pool):
            def rows_of(vec, n):
                return vec.to_broadcast([P, n])

            for vec, a in ((mix_pre_g, 0), (ffn_pre_g, 16), (ple_gate_norm_g, 32)):
                pool.dma_start(small[a:a + 16, :], vec.rearrange("i (k n) -> (i k) n", n=P)).then_inc(gain_in, 16)
            pool.dma_start(small[48:50, :], mla_q_norm_g.rearrange("i (k n) -> (i k) n", n=P)).then_inc(gain_in, 16)
            pool.dma_start(small[50:51, :], mla_kv_norm_g).then_inc(gain_in, 16)
            pool.dma_start(tab[:, :], tables[:, 0:TAB_RES]).then_inc(tab_in, 16)
            pool.dma_start(grow[:, 0, :], rows_of(gqa_q_norm_g, HD)).then_inc(grow_in, 16)
            pool.dma_start(grow[:, 1, :], rows_of(gqa_k_norm_g, HD)).then_inc(grow_in, 16)
            for n, g in enumerate((mix_post_g, ffn_post_g, ple_post_g)):
                pool.dma_start(gb[:, n, :], rows_of(g[0:1, :], D)).then_inc(gb_in[n], 16)
            pool.dma_start(wr[:, :, :], kt_rows(moe_w_router[0])).then_inc(wr_in, 16)
            pool.wait_ge(oT_ok, N_U0 // 2)
            pool.dma_start(pe_rows, p[0, 0].rearrange("(p t) n -> p t n", t=T)).then_inc(p_in, 16)
            pool.wait_ge(h_ok, 2 * 3)
            pool.dma_start(mask, tables[:, TAB_MASK:TAB_ALL].rearrange("p (t n) -> p t n", t=T)).then_inc(mask_in, 16)
            for n, g in enumerate((mix_post_g, ffn_post_g, ple_post_g)):
                pool.dma_start(gb[:, n, :], rows_of(g[1:2, :], D)).then_inc(gb_in[n], 16)
            pool.wait_ge(oT_ok, N_U0 // 2 + DH // 2)
            pool.dma_start(moetab, tables[:, TAB_MOE:TAB_MASK]).then_inc(moetab_in, 16)
            pool.dma_start(pe_rows, p[1, 0].rearrange("(p t) n -> p t n", t=T)).then_inc(p_in, 16)
            pool.memset(acc, 0.0).then_inc(acc_zero, 1)

        @block.scalar
        def _(act):
            steps = [0]

            def link(ins):
                steps[0] += 1
                ins.then_inc(act_step, 1)
                act.wait_ge(act_step, steps[0])

            def copy(out, in_, scale=1.0):
                return act.activation(out, in_, ACT.Copy, scale=scale)

            def scales(out, total, width, ok, inputs_ok=None):
                link(act.activation(ssl[:, :], total, ACT.Ln, bias=eps[:, 0:1], scale=1.0 / width))
                act.activation(out, ssl[:, :], ACT.Exp, scale=-0.5).then_inc(ok, 1)

            def pre(i):
                for t in range(T):
                    if i == 0:
                        act.wait_ge(x_in, 16)
                    else:
                        act.wait_ge(h_ok, 2 * (i - 1) + t + 1)
                    q = act.activation(xn[:, t, :], h[:, t, :], ACT.Square, accum_out=ss[:, t:t + 1])
                link(q)
                scales(rstd[:, :], ss[:, :], D, rstd_ok)

            def post(j, y):
                for t in range(T):
                    output_ready(act, j, t)
                    act.activation(arena[:, t * D:(t + 1) * D], y(t), ACT.Square, accum_out=ss[:, t:t + 1]).then_inc(ysq_ok, 1)
                act.wait_ge(ysq_ok, 2 * j + 2)
                scales(prstd[:, :], ss[:, :], D, prstd_ok)

            def exps(u):
                act.wait_ge(sc_max, u + 1)
                if u < N_U0:
                    if u >= 3:
                        act.wait_ge(pr_tr, u - 2)
                    s = GQA_SCALE if u < N_GQA else MLA_SCALE
                    for t in range(T):
                        last = act.activation(probs(u)[:, t * SEQ:(t + 1) * SEQ],
                                              ps[:, S_BANK[u % 3], t * SEQ:(t + 1) * SEQ], ACT.Exp,
                                              bias=snm[:, u % 3, t:t + 1], scale=s, accum_out=ssum[:, u % 3, t:t + 1])
                else:
                    last = act.activation(probs(u), probs(u), ACT.Exp, bias=snm[:, u % 3, 0:1],
                                          accum_out=ssum[:, u % 3, 0:1])
                last.then_inc(sc_exp, 1)

            def prT(u):
                act.wait_ge(pr_tr, u + 1)
                act.wait_ge(pv_mm, u)
                copy(probT(u), bank(T_BANK[u % 2])).then_inc(prT_ok, 1)

            def attention(first, n):
                for i in range(n + 2):
                    if i < n:
                        exps(first + i)
                    if i >= 2:
                        prT(first + i - 2)

            def ple(l):
                for t in range(T):
                    gates_ready(act, l, t)
                    act.activation(xn[:, t, :], pair(4 + 2 * t), ACT.Exp, scale=-1.0).then_inc(pl_exp, 1)

            act.wait_ge(eps_ok, 1)
            pre(0)
            for t in range(T):
                first_or_used(act, z_mm, 1, 2, t)
                zb = ps[:, 3 * t:3 * t + 3, :].rearrange("p b n -> p (b n)")[:, 0:ZW]
                copy(z[:, t, :], zb).then_inc(z_ok, 1)
            act.wait_ge(z_ok, T)
            for t in range(T):
                act.activation(flat(t)[:, 0:256], z[:, t, ZCQ:ZCKV], ACT.Square, accum_out=hss[:, t, 10:11])
                q = act.activation(flat(t)[:, 256:384], z[:, t, ZCKV:ZKR], ACT.Square, accum_out=hss[:, t, 11:12])
            link(q)
            act.wait_ge(hss_ok, 1)
            for a, b, width in ((0, 10, HD), (10, 11, 256), (11, 12, 128)):
                q = act.activation(hrs[:, :, a:b], hss[:, :, a:b], ACT.Ln, bias=eps[:, 0:1], scale=1.0 / width)
            link(q)
            act.activation(hrs[:, :, :], hrs[:, :, :], ACT.Exp, scale=-0.5).then_inc(hrs_ok, 1)
            act.wait_ge(hrs_ok, 1)
            for t in range(T):
                first_or_used(act, up_mm, 1, C_UQ, t)
                copy(qm[:, t, :, :].rearrange("p h n -> p (h n)"), pair(2 * t)[:, 0:MH * MQ],
                     hrs[:, t, 10:11]).then_inc(up_ok, 1)
            act.wait_ge(qk_tr, 3)
            for t in range(T):
                first_or_used(act, up_mm, 2, C_UKV, t)
                kv = pair(4 + 2 * t).rearrange("p (h n) -> p h n", h=MH)
                copy(km[:, t, :, 0:MN], kv[:, :, 0:MN], hrs[:, t, 11:12])
                copy(vm[:, t, :, :], kv[:, :, MN:], hrs[:, t, 11:12]).then_inc(up_ok, 1)
            for b in range(4):
                act.wait_ge(m_tr, b + 1)
                copy(qmT[0:MQ, 2 * b:2 * b + 2, :].rearrange("p h n -> p (h n)"), ps[0:MQ, b, :]).then_inc(mqT_ok, 1)
            attention(0, N_U0)
            post(0, lambda t: pair(4 + 2 * t))
            pre(1)
            for c in range(NFC):
                for b in range(2):
                    first_or_used(act, f_g, c + 1, C_FFN + FFN_AT["g", c], b)
                    if c:
                        act.wait_ge(f_h, 2 * c - 1 + b)
                    act.activation(sg[:, 2 * b:2 * b + 2, :].rearrange("p f n -> p (f n)"), bank(b),
                                   ACT.Silu).then_inc(f_silu, 1)
            post(1, lambda t: pair(4 + 2 * t))
            pre(2)
            ple(0)
            post(2, lambda t: xn[:, t, :])
            pre(3)
            for c in range(9):
                g, kind = divmod(c, 3)
                for t in range(T):
                    first_or_used(act, dz_mm, c + 1, C_QKV + c, t)
                    src = bank(2 * (c % 2) + t)
                    if kind == 2:
                        copy(dv[:, g, t, :], src).then_inc(dz_ok, 1)
                    else:
                        qi = 2 * g + kind
                        if qi >= 2:
                            act.wait_ge(d_tr, 2 * qi - 2)
                        copy(xn[:, t, (qi % 2) * 512:(qi % 2) * 512 + 512], src).then_inc(dz_ok, 1)
            attention(N_U0, T * DH)
            post(3, lambda t: pair(4 + 2 * t))
            pre(4)
            act.wait_ge(r_gap, 1)
            act.activation(rs[:, 5, :], rs[:, 4, :], ACT.Exp).then_inc(r_eg, 1)

            def experts(blk):
                with act.Fori(0, NE) as e:
                    r = e + rounds_before(blk)

                    def hidden_T(c):
                        act.wait_ge(m_t, NFC * r + c + 1)
                        hidden_used(act, r, c)
                        copy(mhT[:, c % 2, :], bank(2)).then_inc(m_ht, 1)

                    for c in range(NFC):
                        used(act, C_MOE + FFN_AT["g", c], r)
                        act.wait_ge(m_h, NFC * r + c)
                        act.activation(msg, bank(0), ACT.Silu).then_inc(m_silu, 1)
                        if c:
                            hidden_T(c - 1)
                    hidden_T(NFC - 1)
                    for half in range(2):
                        if half:
                            used(act, C_MOE + N_FFN - 1, r)
                        else:
                            act.wait_ge(m_y, r + 1)
                        act.wait_ge(m_sc, 4 * r)
                        copy(ysb[:, half * BANK:(half + 1) * BANK], bank(4 + half)).then_inc(m_ysb, 1)

            act.wait_ge(r_cnt, 1)
            big = act.value_load(cnti[0:1, 0:1])
            experts(0)
            with act.If(big > P):
                experts(1)
            post(4, lambda t: acc[:, t, :])
            pre(5)
            ple(1)
            post(5, lambda t: xn[:, t, :])

        @block.vector
        def _(dve):
            steps = [0]

            def link(ins):
                steps[0] += 1
                ins.then_inc(dve_step, 1)
                dve.wait_ge(dve_step, steps[0])

            def pre(i):
                kind, l = PRE[i]
                dve.wait_ge(rstd_ok, i + 1)
                for t in range(T):
                    dve.tensor_scalar(xn[:, t, :], h[:, t, :], rstd[:, t:t + 1], None, ALU.mult).then_inc(xn_ok, 1)
                for t in range(T):
                    for half in range(2):
                        dve.wait_ge(xn_tr, 4 * i + 2 * t + half + 1)
                        a = GAIN[kind] + KD * l + 4 * half
                        dve.tensor_tensor(xT[:, 4 * half:4 * half + 4, t * P:(t + 1) * P],
                                          bank(2 * t + half).rearrange("p (k n) -> p k n", k=4),
                                          of(gT[:, a:a + 4], P), ALU.mult).then_inc(xT_ok, 1)

            def post(j, y):
                g, l = j % 3, j // 3
                dve.wait_ge(gb_in[g], 16 * (l + 1))
                for t in range(T):
                    dve.wait_ge(ysq_ok, 2 * j + t + 1)
                    q = dve.tensor_tensor(xn[:, t, :], y(t), gb[:, g, :], ALU.mult)
                link(q)
                dve.wait_ge(prstd_ok, j + 1)
                for t in range(T):
                    dve.scalar_tensor_tensor(out=h[:, t, :], in0=xn[:, t, :], scalar=prstd[:, t:t + 1],
                                             in1=h[:, t, :], op0=ALU.mult, op1=ALU.add).then_inc(h_ok, 1)

            def rotate(out, rows_, cos, sin, half, a, b):
                dve.tensor_tensor(a, rows_, cos, ALU.mult)
                lo, hi = slice(0, half), slice(half, 2 * half)
                dve.tensor_tensor(b[..., lo], rows_[..., hi], sin[..., lo], ALU.mult)
                link(dve.tensor_tensor(b[..., hi], rows_[..., lo], sin[..., hi], ALU.mult))
                return dve.tensor_tensor(out, a, b, ALU.add)

            def maxes(u):
                dve.wait_ge(sc_mm, u + 1)
                b = u % 3
                if u < N_U0:
                    s = GQA_SCALE if u < N_GQA else MLA_SCALE
                    link(dve.tensor_reduce(smax[:, b, :], bank(S_BANK[b]).rearrange("p (t n) -> p t n", t=T), AX_X, ALU.max))
                    dve.tensor_scalar(snm[:, b, :], smax[:, b, :], -s, None, ALU.mult).then_inc(sc_max, 1)
                else:
                    if u >= N_U0 + 3:
                        dve.wait_ge(pr_tr, u - 2)
                    link(dve.tensor_tensor_reduce(out=probs(u), in0=bank(S_BANK[b]), in1=mask[:, u % T, :],
                                                  scale=HD ** -0.5, scalar=-3e38, op0=ALU.add, op1=ALU.max,
                                                  accum_out=smax[:, b, 0:1]))
                    dve.tensor_scalar(snm[:, b, 0:1], smax[:, b, 0:1], -1.0, None, ALU.mult).then_inc(sc_max, 1)

            def normalise(u):
                b = u % 3
                dve.wait_ge(sc_exp, u + 1)
                n = T if u < N_U0 else 1
                link(dve.reciprocal(srec[:, b, 0:n], ssum[:, b, 0:n]))
                w = BANK // n
                for t in range(n):
                    q = dve.tensor_scalar(probs(u)[:, t * w:(t + 1) * w], probs(u)[:, t * w:(t + 1) * w],
                                          srec[:, b, t:t + 1], None, ALU.mult)
                q.then_inc(pr_ok, 1)

            def attention(first, n, per):
                for i in range(n + 4):
                    if i < n:
                        maxes(first + i)
                    if 1 <= i <= n:
                        normalise(first + i - 1)
                    if i >= 4 and (i - 4) % per == per - 1:
                        u = first + i - 4
                        dve.wait_ge(pv_mm, u + 1)
                        dve.tensor_copy(xT[:, (u - first) // per, :], bank(o_bank(u), SEQ)).then_inc(oT_ok, 1)

            def ple(l):
                dve.wait_ge(p_tr, l + 1)
                dve.tensor_copy(pT.rearrange("p k n -> p (k n)"), bank(4)).then_inc(pT_ok, 1)
                for t in range(T):
                    dve.wait_ge(pl_exp, 2 * l + t + 1)
                    link(dve.tensor_scalar(xn[:, t, :], xn[:, t, :], 1.0, None, ALU.add))
                    link(dve.reciprocal(xn[:, t, :], xn[:, t, :]))
                    dve.tensor_tensor(xn[:, t, :], pair(2 * t), xn[:, t, :], ALU.mult).then_inc(y_ok, 1)

            dve.memset(eps[:, :], EPS).then_inc(eps_ok, 1)
            dve.memset(posm[:, :, NE:], -1.0)
            dve.memset(gate[:, :, NE:], 0.0)
            dve.wait_ge(gt_tr, 1)
            link(dve.tensor_copy(gT[:, :], bank(7, 51)))
            dve.wait_ge(tab_in, 16)
            dve.wait_ge(grow_in, 32)
            axC = table("axC").rearrange("p (t n) -> p t n", t=T)
            axS = table("axS").rearrange("p (t a f n) -> p t a f n", t=T, a=2, f=2)
            for i in range(2):
                dve.tensor_tensor(rot[:, 2 * i, :, :], axC, grow[:, i:i + 1, :].to_broadcast([P, T, HD]), ALU.mult)
                rv = rot[:, 2 * i + 1, :, :].rearrange("p t (a f n) -> p t a f n", a=2, f=2)
                gv = grow[:, i, :].rearrange("p (a f n) -> p a f n", a=2, f=2)
                for t in range(T):
                    for f in range(2):
                        q = dve.tensor_tensor(rv[:, t, :, f, :], axS[:, t, :, f, :], gv[:, :, 1 - f, :], ALU.mult)
            link(q)
            pre(0)
            dve.wait_ge(z_ok, T)
            xf = xn[:, :, :].rearrange("p t n -> p (t n)")
            sq = xf[:, 0:T * ZV].rearrange("p (t n) -> p t n", t=T)
            link(dve.tensor_tensor(sq, z[:, :, 0:ZV], z[:, :, 0:ZV], ALU.mult))
            for t in range(T):
                q = dve.tensor_reduce(hss[:, t, 0:10], sq[:, t, :].rearrange("p (h n) -> p h n", h=10), AX_X, ALU.add)
            q.then_inc(hss_ok, 1)
            for t in range(T):
                dve.wait_ge(lat_tr, t + 1)
                dve.tensor_tensor(latT[:, :, t * P:(t + 1) * P], bank(6 + t, 3 * P).rearrange("p (k n) -> p k n", k=3),
                                  of(gT[:, 48:51], P), ALU.mult).then_inc(lat_ok, 1)
            dve.wait_ge(hss_ok, 1)
            sa, sb_ = probs0[:, 0, :], probs0[:, 1, :]
            for t in range(T):
                for first, heads, i in ((ZQ, NQ, 0), (ZK, NKV, 1)):
                    n = heads * HD
                    src = z[:, t, first:first + n]
                    v5 = "p (h a f n) -> p h a f n"
                    cos = rot[:, 2 * i, t:t + 1, :].to_broadcast([P, heads, HD])
                    sinv = rot[:, 2 * i + 1, t, :].rearrange("p (a f n) -> p a f n", a=2, f=2)
                    s5 = src.rearrange(v5, h=heads, a=2, f=2)
                    b5 = sb_[:, 0:n].rearrange(v5, h=heads, a=2, f=2)
                    dve.tensor_tensor(sa[:, 0:n].rearrange("p (h n) -> p h n", h=heads),
                                      src.rearrange("p (h n) -> p h n", h=heads), cos, ALU.mult)
                    for f in range(2):
                        q = dve.tensor_tensor(b5[:, :, :, f, :], s5[:, :, :, 1 - f, :],
                                              sinv[:, :, f, :].unsqueeze(1).to_broadcast([P, heads, 2, 16]), ALU.mult)
                    link(q)
                    link(dve.tensor_tensor(sa[:, 0:n], sa[:, 0:n], sb_[:, 0:n], ALU.add))
                    if t == 0 and i == 0:
                        dve.wait_ge(hrs_ok, 1)
                    a3 = sa[:, 0:n].rearrange("p (h n) -> p h n", h=heads)
                    sc = of(hrs[:, t, (0, NQ)[i]:(NQ, NQ + NKV)[i]], HD)
                    if i == 0:
                        link(dve.tensor_tensor(qr[:, t, :].rearrange("p (h n) -> p h n", h=heads), a3, sc, ALU.mult))
                    else:
                        for u in range(2):
                            q = dve.tensor_tensor(kr[:, t, :, u, :], a3, sc, ALU.mult)
                        link(q)
            dve.sem_inc(qk_ok, 1)
            for t in range(T):
                dve.wait_ge(qk_tr, t + 1)
                dve.tensor_copy(qT[:, :, t * P:(t + 1) * P], bank(t).rearrange("p (c n) -> p c n", c=4)).then_inc(qkT_ok, 1)
            dve.wait_ge(qk_tr, 3)
            dve.tensor_copy(kT.rearrange("p j n -> p (j n)"), bank(2)).then_inc(qkT_ok, 1)
            mlC = table("mlC").rearrange("p (t n) -> p t n", t=T)
            mlS = table("mlS").rearrange("p (t n) -> p t n", t=T)
            dve.wait_ge(up_ok, T)
            hb = [P, T, MH, MR]
            ma, mb = mtmp[:, 0:512].rearrange("p (t h n) -> p t h n", t=T, h=MH), probs0[:, 2, :].rearrange("p (t h n) -> p t h n", t=T, h=MH)
            link(rotate(qm[:, :, :, MN:], qm[:, :, :, MN:], mlC.unsqueeze(2).to_broadcast(hb),
                        mlS.unsqueeze(2).to_broadcast(hb), MR // 2, ma, mb))
            ka, kb = (sa[:, i * 64:(i + 1) * 64].rearrange("p (t n) -> p t n", t=T) for i in range(2))
            kro = sa[:, 128:192].rearrange("p (t n) -> p t n", t=T)
            link(rotate(kro, z[:, :, ZKR:ZW], mlC, mlS, MR // 2, ka, kb))
            dve.tensor_copy(km[:, :, :, MN:], kro.unsqueeze(2).to_broadcast(hb)).then_inc(mrow_ok, 1)
            for b in range(4):
                dve.wait_ge(m_tr, 4 + b + 1)
                dve.tensor_copy(kmT[0:MQ, 2 * b:2 * b + 2, :].rearrange("p h n -> p (h n)"), ps[0:MQ, 4 + b, :]).then_inc(mkT_ok, 1)
            attention(0, N_U0, 2)
            post(0, lambda t: pair(4 + 2 * t))
            pre(1)
            for c in range(NFC):
                for b in range(2):
                    dve.wait_ge(f_silu, 2 * c + b + 1)
                    first_or_used(dve, f_u, c + 1, C_FFN + FFN_AT["u", c], b)
                    if c >= 2:
                        used(dve, C_FFN + FFN_AT["d", c - 2])
                    dve.tensor_tensor(hT[:, c % 2, 2 * b:2 * b + 2, :].rearrange("p f n -> p (f n)"),
                                      sg[:, 2 * b:2 * b + 2, :].rearrange("p f n -> p (f n)"),
                                      bank(2 + b), ALU.mult).then_inc(f_h, 1)
            post(1, lambda t: pair(4 + 2 * t))
            pre(2)
            ple(0)
            post(2, lambda t: xn[:, t, :])
            pre(3)
            dC = table("diC").rearrange("p (t n) -> p t n", t=T).unsqueeze(2).to_broadcast([P, T, DH, 16])
            dS = table("diS").rearrange("p (t n) -> p t n", t=T).unsqueeze(2).to_broadcast([P, T, DH, 16])
            da, db = (dtmp[:, i, 0:256].rearrange("p (t h n) -> p t h n", t=T, h=DH) for i in range(2))

            def dil_T(qi):
                g, kind = divmod(qi, 2)
                for t in range(T):
                    dve.wait_ge(d_tr, 2 * qi + t + 1)
                    dve.tensor_copy((dq, dk)[kind][:, g, :, t * P:(t + 1) * P],
                                    bank(4 + 2 * (qi % 2) + t).rearrange("p (c n) -> p c n", c=4)).then_inc(dT_ok, 1)

            for c in range(9):
                g, kind = divmod(c, 3)
                if kind < 2:
                    qi = 2 * g + kind
                    dve.wait_ge(dz_ok, 2 * c + 2)
                    rw = xn[:, :, (qi % 2) * 512:(qi % 2) * 512 + 512].rearrange("p t (h n) -> p t h n", h=DH)[:, :, :, 0:16]
                    q = rotate(rw, rw, dC, dS, 8, da, db)
                    link(q)
                    dve.sem_inc(dr_ok, 1)
                if c and (c - 1) % 3 < 2:
                    dil_T(2 * ((c - 1) // 3) + (c - 1) % 3)
            dve.wait_ge(mask_in, 16)
            attention(N_U0, T * DH, 4)
            post(3, lambda t: pair(4 + 2 * t))
            pre(4)

            def R(i):
                return rt[:, i, :].rearrange("p (t n) -> p t n", t=T)

            def each(v):
                return v.unsqueeze(2).to_broadcast([P, T, NE])

            rev = table("rev").rearrange("p (t n) -> p t n", t=T)
            dve.wait_ge(r_mm, 1)
            link(dve.tensor_copy(rt[:, 0, :], bank(4, T * NE)))

            def largest(logits, top, eq, best, onehot):
                link(dve.tensor_reduce(rs[:, top, :], R(logits), AX_X, ALU.max))
                link(dve.tensor_tensor(R(eq), R(logits), each(rs[:, top, :]), ALU.is_equal))
                link(dve.tensor_tensor(R(eq), R(eq), rev, ALU.mult))
                link(dve.tensor_reduce(rs[:, best, :], R(eq), AX_X, ALU.max))
                link(dve.tensor_tensor(R(onehot), R(eq), each(rs[:, best, :]), ALU.is_equal))

            largest(0, 0, 1, 1, 2)
            link(dve.scalar_tensor_tensor(out=rt[:, 3, :], in0=rt[:, 2, :], scalar=-3e38, in1=rt[:, 0, :],
                                          op0=ALU.mult, op1=ALU.add))
            largest(3, 2, 4, 3, 5)
            dve.tensor_tensor(rs[:, 4, :], rs[:, 2, :], rs[:, 0, :], ALU.subtract).then_inc(r_gap, 1)
            dve.tensor_tensor(rt[:, 6, :], rt[:, 2, :], rt[:, 5, :], ALU.add).then_inc(r_mask, 1)
            dve.wait_ge(r_eg, 1)
            link(dve.tensor_scalar(rs[:, 6, :], rs[:, 5, :], 1.0, None, ALU.add))
            link(dve.reciprocal(rs[:, 7, :], rs[:, 6, :]))
            link(dve.tensor_tensor(rs[:, 1, :], rs[:, 5, :], rs[:, 7, :], ALU.mult))
            dve.tensor_tensor(R(7), R(2), each(rs[:, 7, :]), ALU.mult)
            link(dve.tensor_tensor(R(8), R(5), each(rs[:, 1, :]), ALU.mult))
            link(dve.tensor_tensor(gate[:, :, 0:NE], R(7), R(8), ALU.add))
            dve.wait_ge(r_pos, 1)
            dve.tensor_reduce(cnt[:, 0:1], ps[:, 5, T * NE:(T + 1) * NE], AX_X, ALU.max)
            link(dve.scalar_tensor_tensor(out=rt[:, 9, :], in0=bank(5, T * NE), scalar=1.0, in1=rt[:, 6, :],
                                          op0=ALU.add, op1=ALU.mult))
            dve.tensor_copy(cnti[:, :], cnt[:, 0:1]).then_inc(r_cnt, 1)
            link(dve.tensor_scalar(posm[:, :, 0:NE], R(9), -1.0, None, ALU.add))
            dve.wait_ge(r_cnt, 1)
            big = dve.value_load(cnti[0:1, 0:1])
            dve.wait_ge(moetab_in, 16)
            dve.wait_ge(acc_zero, 1)

            def select(blk, e, built):
                for t in range(T):
                    at, w = posm[:, t, bass.ds(e, 1)], gate[:, t, bass.ds(e, 1)]
                    io = iota[:, blk * P:(blk + 1) * P]
                    dve.tensor_scalar(sel[:, t, :], io, at, None, ALU.is_equal)
                    q = dve.tensor_scalar(selg[:, t, :], io, at, w, ALU.is_equal, ALU.mult)
                q.then_inc(m_sel, 1)

            def experts(blk):
                if blk:
                    dve.wait_ge(m_ga, 2 * NE * blk)
                    dve.wait_ge(m_st, NE * blk)
                select(blk, 0, 0)
                with dve.Fori(0, NE) as e:
                    r = e + rounds_before(blk)
                    for half in range(2):
                        dve.wait_ge(m_ga, 2 * r + half + 1)
                        used(dve, C_MOE - 1, r)
                        a = GAIN["ffn"] + KD + 4 * half
                        dve.tensor_tensor(xg[:, 4 * half:4 * half + 4, :], bank(6 + half).rearrange("p (k n) -> p k n", k=4),
                                          of(gT[:, a:a + 4], P), ALU.mult).then_inc(m_xg, 1)
                    for c in range(NFC):
                        dve.wait_ge(m_silu, NFC * r + c + 1)
                        used(dve, C_MOE + FFN_AT["u", c], r)
                        dve.wait_ge(m_t, NFC * r + max(c - 1, 0))
                        dve.tensor_tensor(mh[:, c % 2, :], msg, bank(1), ALU.mult).then_inc(m_h, 1)
                        if c == 1:
                            dve.wait_ge(m_st, r + 1)
                            dve.wait_ge(m_sc, 4 * r)
                            dve.tensor_copy(selT.rearrange("p t n -> p (t n)"), bank(3, T * P)).then_inc(m_sT, 1)
                        if c == 3:
                            select(blk, e + 1, 0)
                    for half in range(2):
                        for t in range(T):
                            dve.wait_ge(m_sc, 4 * r + 2 * half + t + 1)
                            dve.wait_ge(m_acc, 4 * r)
                            part = acc[:, t, half * BANK:(half + 1) * BANK]
                            dve.tensor_tensor(part, bank(6 + t), part, ALU.add).then_inc(m_acc, 1)
                dve.wait_ge(m_acc, 4 * NE * (blk + 1))

            experts(0)
            with dve.If(big > P):
                experts(1)
            dve.sem_inc(y_ok, 2)
            post(4, lambda t: acc[:, t, :])
            pre(5)
            ple(1)
            post(5, lambda t: xn[:, t, :])

        @block.tensor
        def _(pe):
            def mm(out_, lhsT, rhs, start, stop):
                return pe.matmul(out_, lhsT, rhs, start=start, stop=stop)

            def pre(i):
                for t in range(T):
                    pe.wait_ge(xn_ok, 2 * i + t + 1)
                    for half in range(2):
                        for k in range(4):
                            a = (4 * half + k) * P
                            q = pe.transpose(ps[:, 2 * t + half, k * P:(k + 1) * P], xn[:, t, a:a + P], ident)
                        q.then_inc(xn_tr, 1)

            def rows_by(n, tiles, width, b0, lhs, first, last, done=None, done_t=1):
                w = chunk(n, tiles, width)
                nb = -(-width // BANK)
                for t in range(T):
                    for k in range(tiles):
                        for j in range(nb):
                            a, b = j * BANK, min(width, (j + 1) * BANK)
                            q = mm(ps[:, b0 + nb * t + j, 0:b - a], lhs(k, t), w[:, k, a:b],
                                   first and k == 0, last and k == tiles - 1)
                    if done is not None and t == 0:
                        q.then_inc(done, 1)
                q.then_inc(chunk_used, 1)

            def lhs_of(base):
                return lambda k, t: xT[:, base + k, t * P:(t + 1) * P]

            def scores(u):
                b = u % 3
                if u >= 3:
                    pe.wait_ge(sc_exp, u - 2)
                if u < N_U0:
                    hh, o = u % 8, 64 * (u % 2)
                    for t in range(T):
                        cols = slice(t * P, (t + 1) * P)
                        if u < N_GQA:
                            l_, r_ = qT[o:o + 64, hh // 2, cols], kT[o:o + 64, hh // 4, :]
                        else:
                            l_, r_ = qmT[0:MQ, hh, cols], kmT[0:MQ, hh, :]
                        q = mm(ps[:, S_BANK[b], t * SEQ:(t + 1) * SEQ], l_, r_, True, True)
                else:
                    hh, t = divmod(u - N_U0, T)
                    o, own = 64 * (hh % 2), slice(t * P, (t + 1) * P)
                    for g in range(DG):
                        a, b_ = ((0, SEQ), (SEQ, SEQ + P), (SEQ + P, BANK))[g]
                        q = mm(ps[:, S_BANK[b], a:b_], dq[o:o + 64, g, hh // 2, own],
                               dk[o:o + 64, g, hh // 2, :] if g == 0 else dk[o:o + 64, g, hh // 2, own], True, True)
                q.then_inc(sc_mm, 1)

            def transposes(u):
                pe.wait_ge(pr_ok, u + 1)
                if u >= 2:
                    pe.wait_ge(prT_ok, u - 1)
                for a in range(4):
                    to = a if u >= N_U0 else 2 * (a % 2) + a // 2
                    q = pe.transpose(ps[:, T_BANK[u % 2], to * P:(to + 1) * P], probs(u)[:, a * P:(a + 1) * P], ident)
                q.then_inc(pr_tr, 1)

            def values(u):
                pe.wait_ge(prT_ok, u + 1)
                n = oT_before(u)
                if n >= 2:
                    pe.wait_ge(oT_ok, n - 1)
                if u < N_U0:
                    hh, o = u % 8, 64 * (u % 2)
                    for k in range(T):
                        v = z[:, k, ZV + HD * (hh // 4):ZV + HD * (hh // 4 + 1)] if u < N_GQA else vm[:, k, hh, :]
                        q = mm(ps[o:o + 64, o_bank(u), 0:SEQ], v, probT(u)[:, k * SEQ:(k + 1) * SEQ], k == 0, k == T - 1)
                else:
                    hh, t = divmod(u - N_U0, T)
                    o = 64 * (hh % 2)
                    for j, (g, k) in enumerate(((0, 0), (0, 1), (1, t), (2, t))):
                        q = mm(ps[o:o + 64, o_bank(u), t * P:(t + 1) * P], dv[:, g, k, hh * HD:(hh + 1) * HD],
                               probT(u)[:, j * P:(j + 1) * P], j == 0, j == 3)
                q.then_inc(pv_mm, 1)

            def attention(first, n):
                for i in range(n + 3):
                    if i < n:
                        scores(first + i)
                    if i >= 3:
                        values(first + i - 3)
                    if 2 <= i < n + 2:
                        transposes(first + i - 2)

            def ple(l, chunk_of):
                pe.wait_ge(p_in, 16 * (l + 1))
                for k in range(PK):
                    for t in range(T):
                        q = pe.transpose(ps[:, 4, k * SEQ + t * P:k * SEQ + (t + 1) * P], pe_rows[:, t, k * P:(k + 1) * P], ident)
                q.then_inc(p_tr, 1)
                pe.wait_ge(pT_ok, l + 1)
                pe.wait_ge(xT_ok, 4 * (3 * l + 2) + 4)
                w = chunk_of(0)
                for t in range(T):
                    for k in range(PK):
                        for half in range(2):
                            q = mm(ps[:, 2 * t + half, :], pT[:, k, t * P:(t + 1) * P],
                                   w[:, k, half * BANK:(half + 1) * BANK], k == 0, k == PK - 1)
                q.then_inc(chunk_used, 1)
                for a in range(2):
                    w = chunk_of(1 + a)
                    for t in range(T):
                        for k in range(4):
                            for half in range(2):
                                q = mm(ps[:, 4 + 2 * t + half, :], xT[:, 4 * a + k, t * P:(t + 1) * P],
                                       w[:, k, half * BANK:(half + 1) * BANK], a == 0 and k == 0, a == 1 and k == 3)
                        if a == 1 and (l or t == 0):
                            q.then_inc(pl_mm, 1)
                    if a == 0 or l == 0:
                        q.then_inc(chunk_used, 1)

            pe.wait_ge(tab_in, 16)
            pe.wait_ge(gain_in, 16 * 5)
            pe.transpose(ps[:, 7, 0:51], small, tab[0:51, 0:51]).then_inc(gt_tr, 1)
            pre(0)
            pe.wait_ge(xT_ok, 4)
            for n, (a, tiles) in enumerate(IN_TILES):
                arrived(pe, n)
                rows_by(n, tiles, ZW, 0, lhs_of(a), n == 0, n == 2, z_mm if n == 2 else None)
            for t in range(T):
                pe.wait_ge(z_ok, t + 1)
                if t == 0:
                    pe.wait_ge(xT_ok, 4)
                for k in range(3):
                    q = pe.transpose(ps[:, 6 + t, k * P:(k + 1) * P], z[:, t, ZCQ + k * P:ZCQ + (k + 1) * P], ident)
                q.then_inc(lat_tr, 1)
            pe.wait_ge(lat_ok, T)
            pe.wait_ge(z_ok, T)
            arrived(pe, C_UQ)
            rows_by(C_UQ, 2, MH * MQ, 0, lambda k, t: latT[:, k, t * P:(t + 1) * P], True, True, up_mm)
            arrived(pe, C_UKV)
            rows_by(C_UKV, 1, MH * 2 * HD, 4, lambda k, t: latT[:, 2, t * P:(t + 1) * P], True, True, up_mm)
            pe.wait_ge(qk_ok, 1)
            pe.wait_ge(up_ok, T)
            for t in range(T):
                for c in range(4):
                    q = pe.transpose(ps[:, t, c * P:(c + 1) * P], qr[:, t, c * P:(c + 1) * P], ident)
                q.then_inc(qk_tr, 1)
            for j in range(NKV):
                for t in range(T):
                    q = pe.transpose(ps[:, 2, (T * j + t) * P:(T * j + t + 1) * P], kr[:, t, j, :, :].rearrange("p u n -> p (u n)"), ident)
            q.then_inc(qk_tr, 1)
            pe.wait_ge(qkT_ok, 3)
            pe.wait_ge(up_ok, 2 * T)
            pe.wait_ge(mrow_ok, 1)
            for src, b0 in ((qm, 0), (km, 4)):
                for b in range(4):
                    for hh in (0, 1):
                        for t in range(T):
                            q = pe.transpose(ps[0:MQ, b0 + b, hh * SEQ + t * P:hh * SEQ + (t + 1) * P], src[:, t, 2 * b + hh, :], ident)
                    q.then_inc(m_tr, 1)
            pe.wait_ge(mqT_ok, 4)
            pe.wait_ge(mkT_ok, 4)
            attention(0, N_U0)
            pe.wait_ge(oT_ok, N_U0 // 2)
            for a in range(2):
                arrived(pe, C_ABOUT + a)
                rows_by(C_ABOUT + a, 4, D, 4, lhs_of(4 * a), a == 0, a == 1, y_ok if a == 1 else None)
            pre(1)
            pe.wait_ge(xT_ok, 4 * 1 + 4)
            for step, (kind, c) in enumerate(FFN):
                n = C_FFN + step
                arrived(pe, n)
                if kind == "d":
                    pe.wait_ge(f_h, 2 * c + 2)
                    w = chunk(n, FT, D)
                    for t in range(T):
                        for k in range(FT):
                            for half in range(2):
                                q = mm(ps[:, 4 + 2 * t + half, :], hT[:, c % 2, k, t * P:(t + 1) * P],
                                       w[:, k, half * BANK:(half + 1) * BANK], c == 0 and k == 0, c == NFC - 1 and k == FT - 1)
                        if c == NFC - 1 and t == 0:
                            q.then_inc(y_ok, 1)
                else:
                    if c:
                        pe.wait_ge(f_silu if kind == "g" else f_h, 2 * c)
                    w = chunk(n, KD, FC)
                    for f in range(FT):
                        for k in range(KD):
                            q = mm(ps[:, (0 if kind == "g" else 2) + f // 2, (f % 2) * SEQ:(f % 2 + 1) * SEQ],
                                   w[:, k, f * P:(f + 1) * P], xT[:, k, :], k == 0, k == KD - 1)
                        if f == 1:
                            q.then_inc(f_g if kind == "g" else f_u, 1)
                q.then_inc(chunk_used, 1)
            pre(2)

            def ple_chunk(i):
                arrived(pe, C_PLE0 + i)
                return chunk(C_PLE0 + i, (PK, 4, 4)[i], D)

            ple(0, ple_chunk)
            pre(3)
            pe.wait_ge(xT_ok, 4 * 3 + 4)
            for c in range(9):
                g, kind = divmod(c, 3)
                n = C_QKV + c
                arrived(pe, n)
                w = chunk(n, KD, FC)
                for t in range(T):
                    if c >= 2:
                        pe.wait_ge(dz_ok, 2 * c - 3 + t)
                    for k in range(KD):
                        q = mm(ps[:, 2 * (c % 2) + t, :], xT[:, k, t * P:(t + 1) * P], w[:, k, :], k == 0, k == KD - 1)
                    if t == 0:
                        q.then_inc(dz_mm, 1)
                q.then_inc(chunk_used, 1)
                if c and (c - 1) % 3 < 2:
                    qi = 2 * ((c - 1) // 3) + (c - 1) % 3
                    pe.wait_ge(dr_ok, qi + 1)
                    for t in range(T):
                        if qi >= 2:
                            pe.wait_ge(dT_ok, 2 * qi - 3 + t)
                        for k in range(4):
                            a = (qi % 2) * 512 + k * P
                            q = pe.transpose(ps[:, 4 + 2 * (qi % 2) + t, k * P:(k + 1) * P], xn[:, t, a:a + P], ident)
                        q.then_inc(d_tr, 1)
            pe.wait_ge(dz_ok, 18)
            pe.wait_ge(dT_ok, 12)
            attention(N_U0, T * DH)
            pe.wait_ge(oT_ok, N_U0 // 2 + DH // 2)
            arrived(pe, C_DOUT)
            rows_by(C_DOUT, 4, D, 4, lhs_of(0), True, True, y_ok)
            pre(4)
            pe.wait_ge(xT_ok, 4 * 4 + 4)
            pe.wait_ge(wr_in, 16)
            for t in range(T):
                for k in range(KD):
                    q = mm(ps[:, 4, t * NE:(t + 1) * NE], xT[:, k, t * P:(t + 1) * P], wr[:, k, :], k == 0, k == KD - 1)
            q.then_inc(r_mm, 1)
            pe.wait_ge(r_mask, 1)
            pe.wait_ge(moetab_in, 16)
            chose = [rt[:, 6, t * NE:(t + 1) * NE] for t in range(T)]
            mm(ps[:, 5, 0:NE], tri, chose[0], True, True)
            mm(ps[:, 5, NE:2 * NE], ones, chose[0], True, False)
            mm(ps[:, 5, NE:2 * NE], tri, chose[1], False, True)
            mm(ps[:, 5, 2 * NE:3 * NE], ones, chose[0], True, False)
            mm(ps[:, 5, 2 * NE:3 * NE], ones, chose[1], False, True).then_inc(r_pos, 1)
            pe.wait_ge(r_cnt, 1)
            big = pe.value_load(cnti[0:1, 0:1])

            def experts(blk):
                with pe.Fori(0, NE) as e:
                    r = e + rounds_before(blk)

                    def hidden_T(c):
                        pe.wait_ge(m_h, NFC * r + c + 1)
                        pe.wait_ge(m_ht, NFC * r + c)
                        for k in range(FT):
                            q = pe.transpose(ps[:, 2, k * P:(k + 1) * P], mh[:, c % 2, k * P:(k + 1) * P], ident)
                        q.then_inc(m_t, 1)

                    pe.wait_ge(m_sel, (NE + 1) * blk + e + 1)
                    pe.wait_ge(m_acc, 4 * r)
                    for half in range(2):
                        for k in range(4):
                            a = (4 * half + k) * P
                            for t in range(T):
                                q = mm(ps[:, 6 + half, k * P:(k + 1) * P], xn[:, t, a:a + P], sel[:, t, :], t == 0, t == T - 1)
                        q.then_inc(m_ga, 1)
                    for j, (kind, c) in enumerate(FFN):
                        n = C_MOE + j
                        if kind == "u" and c:
                            hidden_T(c - 1)
                        if kind == "d" and c == NFC - 1:
                            hidden_T(c)
                        arrived(pe, n, r)
                        if kind == "d":
                            pe.wait_ge(m_ht, NFC * r + c + 1)
                            if c == 0:
                                pe.wait_ge(m_ysb, 2 * r)
                            w = chunk(n, FT, D)
                            for half in range(2):
                                for k in range(FT):
                                    q = mm(ps[:, 4 + half, :], mhT[:, c % 2, k * P:(k + 1) * P],
                                           w[:, k, half * BANK:(half + 1) * BANK], c == 0 and k == 0, c == NFC - 1 and k == FT - 1)
                                if c == NFC - 1 and half == 0:
                                    q.then_inc(m_y, 1)
                        else:
                            if kind == "g" and c == 0:
                                pe.wait_ge(m_xg, 2 * r + 2)
                            pe.wait_ge(m_silu if kind == "g" else m_h, NFC * r + c)
                            w = chunk(n, KD, FC)
                            for k in range(KD):
                                q = mm(bank(0 if kind == "g" else 1), xg[:, k, :], w[:, k, :], k == 0, k == KD - 1)
                        q.then_inc(chunk_used, 1)
                        if (kind, c) == ("g", 1):
                            pe.wait_ge(m_sT, r)
                            for t in range(T):
                                q = pe.transpose(ps[:, 3, t * P:(t + 1) * P], selg[:, t, :], ident)
                            q.then_inc(m_st, 1)
                    pe.wait_ge(m_sT, r + 1)
                    for half in range(2):
                        pe.wait_ge(m_ysb, 2 * r + half + 1)
                        for t in range(T):
                            if half:
                                pe.wait_ge(m_acc, 4 * r + t + 1)
                            mm(bank(6 + t), selT[:, t, :], ysb[:, half * BANK:(half + 1) * BANK], True, True).then_inc(m_sc, 1)

            experts(0)
            with pe.If(big > P):
                experts(1)
            pre(5)

            def tail_chunk(i):
                pe.wait_ge(tail_in[i], 16)
                return chunk(C_MOE + i, (PK, 4, 4)[i], D)

            ple(1, tail_chunk)


def tables_of_shapes():
    f = np.float32
    tok = np.arange(SEQ).reshape(P, T)

    def angles(pos, dim, theta):
        inv = np.power(f(theta), -(np.arange(0, dim, 2, dtype=f) / f(dim)))
        a = pos.astype(f)[..., None] * inv
        return np.cos(a).astype(f), np.sin(a).astype(f)

    out = np.zeros((P, TAB_ALL), f)

    def put(at, v):
        v = np.asarray(v, f).reshape(P, -1)
        out[:, at:at + v.shape[1]] = v

    put(TAB["ident"][0], np.eye(P))
    cr, sr = angles(tok // 64, 32, 10000.0)
    cc, sc = angles(tok % 64, 32, 10000.0)
    put(TAB["axC"][0], np.concatenate([cr, cr, cc, cc], -1))
    put(TAB["axS"][0], np.concatenate([-sr, sr, -sc, sc], -1))
    for name, dim, theta in (("ml", MR, 10000.0), ("di", 16, 500000.0)):
        c, s = angles(tok, dim, theta)
        put(TAB[name + "C"][0], np.concatenate([c, c], -1))
        put(TAB[name + "S"][0], np.concatenate([-s, s], -1))
    put(TAB["rev"][0], np.tile(NE - np.arange(NE), (P, T)))
    i = np.arange(P)
    put(TAB_MOE, i[:, None] < i[None, :])
    put(TAB_MOE + P, np.ones((P, P)))
    put(TAB_MOE + 2 * P, np.tile(np.arange(2 * P), (P, 1)))
    for t in range(T):
        q = tok[:, t][:, None]
        keys = [np.abs(q - tok[:, k][None]) <= 64 for k in range(T)]
        keys += [(q - tok[:, t][None]) % dil == 0 for dil in (4, 16)]
        put(TAB_MASK + t * BANK, np.where(np.concatenate(keys, 1), 0.0, NEG))
    return out


INS = ["x", "p", "mix_pre_g", "mix_post_g", "ffn_pre_g", "ffn_post_g", "ple_w_proj", "ple_gate_norm_g",
       "ple_w_gate", "ple_post_g", "ab_w_in", "gqa_q_norm_g", "gqa_k_norm_g", "mla_q_norm_g", "mla_w_uq",
       "mla_kv_norm_g", "mla_w_ukv", "ab_w_out", "ffn_w_gate", "ffn_w_up", "ffn_w_down", "dil_w_qkv",
       "dil_w_out", "moe_w_router", "moe_w_gate", "moe_w_up", "moe_w_down"]


def kernel(**inputs):
    import concourse.bacc as bacc
    from concourse.bass_utils import run_bass_kernel_spmd

    nc = bacc.Bacc("TRN2", target_bir_lowering=False, num_devices=1)
    arrays, args = {}, []
    for name in INS:
        arrays["in_" + name] = np.ascontiguousarray(inputs[name])
    arrays["in_tables"] = tables_of_shapes()
    for name, a in arrays.items():
        args.append(nc.dram_tensor(name, a.shape, mybir.dt.from_np(a.dtype), kind="ExternalInput").ap())
    args.append(nc.dram_tensor("out_h", (1, SEQ, D), F32, kind="ExternalOutput").ap())
    hybrid_encoder(nc, *args)
    r = run_bass_kernel_spmd(nc, [arrays], core_ids=[0])
    return r.results[0]["out_h"]
```

```python
from contextlib import ExitStack

import numpy as np

import concourse.bass as bass
from concourse import mybir

P = 128
F32 = mybir.dt.float32
F32R = mybir.dt.float32r
I32 = mybir.dt.int32
U32 = mybir.dt.uint32
ACT = mybir.ActivationFunctionType
ALU = mybir.AluOpType
AX_X = mybir.AxisListType.X

SEQ, D = 256, 1024
T = SEQ // P
KD = D // P
EPS = 1e-6
NEG = -1e30
HD = 64
NQ, NKV = 8, 2
ZQ, ZK, ZV, ZCQ, ZCKV, ZKR, ZW = 0, 512, 640, 768, 1024, 1152, 1184
MH, MN, MR = 8, 64, 32
MQ = MN + MR
GQA_SCALE = HD ** -0.5
MLA_SCALE = MQ ** -0.5
FF = 3584
FC = 512
NFC = FF // FC
FT = FC // P
DH, DG = 8, 3
PD, PK = 256, 2
NE = 8
BANK = 512

SLOT, RAW, SPLIT = 2048, 6, 3
C_IN, N_IN = 0, KD
C_UQ = C_IN + N_IN
C_UKV = C_UQ + 1
C_ABOUT, N_ABOUT = C_UKV + 1, 4
C_FFN, N_FFN = C_ABOUT + N_ABOUT, 6 * NFC
C_PLE0, N_PLE = C_FFN + N_FFN, 5
C_QKV, N_QKV = C_PLE0 + N_PLE, 18
C_DOUT, N_DOUT = C_QKV + N_QKV, 2
C_MOE = C_DOUT + N_DOUT
assert N_FFN % RAW == 0 and N_FFN % SPLIT == 0
Z_BANKS = ((0, 384), (384, 768), (768, ZW))
MAX_OVER = 3
assert (MAX_OVER + 1) * (P + 1) > 2 * SEQ
JOBS = NE + MAX_OVER + 1


def ffn_order():
    order = [("g", 0), ("u", 0)]
    for c in range(1, NFC):
        order += [("g", c), ("u", c), ("d", c - 1)]
    order.append(("d", NFC - 1))
    return [(kind, c, half) for kind, c in order for half in range(2)]


FFN = ffn_order()
FFN_AT = {key: n for n, key in enumerate(FFN)}

TAB = {}
_w = 0
for _n, _c in (("ident", P), ("axC", T * HD), ("axS", T * HD), ("mlC", T * MR), ("mlS", T * MR),
               ("diC", T * 16), ("diS", T * 16), ("rev", T * NE)):
    TAB[_n] = (_w, _c)
    _w += _c
TAB_RES = _w
TAB_MOE = _w
TAB_MASK = TAB_MOE + 3 * P
TAB_ALL = TAB_MASK + T * BANK


def hybrid_encoder(nc, x, p, mix_pre_g, mix_post_g, ffn_pre_g, ffn_post_g, ple_w_proj, ple_gate_norm_g,
                   ple_w_gate, ple_post_g, ab_w_in, gqa_q_norm_g, gqa_k_norm_g, mla_q_norm_g, mla_w_uq,
                   mla_kv_norm_g, mla_w_ukv, ab_w_out, ffn_w_gate, ffn_w_up, ffn_w_down, dil_w_qkv,
                   dil_w_out, moe_w_router, moe_w_gate, moe_w_up, moe_w_down, tables, out):
    ctx = ExitStack()
    with ctx:
        def sb(name, shape, dt=F32):
            return ctx.enter_context(nc.sbuf_tensor(name, shape, dt))

        def sem(name):
            return ctx.enter_context(nc.semaphore(name))

        ps = ctx.enter_context(nc.psum_tensor("ps", [P, 8, BANK], F32))

        raw = sb("raw", [P, RAW, SLOT])
        whi = sb("whi", [P, SPLIT, SLOT], F32R)
        wlo = sb("wlo", [P, SPLIT, SLOT], F32R)
        h = sb("h", [P, T, D])
        xn = sb("xn", [P, T, D])
        xTh = sb("xTh", [P, KD, SEQ], F32R)
        xTl = sb("xTl", [P, KD, SEQ], F32R)
        gb = sb("gb", [P, 3, D])
        tab = sb("tab", [P, TAB_RES])
        gT = sb("gT", [P, 51])
        wr = sb("wr", [P, KD, NE])
        eps = sb("eps", [P, 1])
        ss = sb("ss", [P, T])
        ssl = sb("ssl", [P, T])
        rstd = sb("rstd", [P, T])
        prstd = sb("prstd", [P, T])
        hss = sb("hss", [P, T, 12])
        hrs = sb("hrs", [P, T, 12])
        smax = sb("smax", [P, 3, T])
        snm = sb("snm", [P, 3, T])
        ssum = sb("ssum", [P, 3, T])
        srec = sb("srec", [P, 3, T])
        rt = sb("rt", [P, 10, T * NE])
        rs = sb("rs", [P, 8, T])
        posm = sb("posm", [P, T, JOBS])
        gate = sb("gate", [P, T, JOBS])
        cnt8 = sb("cnt8", [P, 8])
        over8 = sb("over8", [P, 8])
        cidx = sb("cidx", [P, 8], U32)
        nover = sb("nover", [P, 1])
        noveri = sb("noveri", [P, 1], I32)
        ARENA, FR_ARENA = 10752, 4096
        arena = sb("arena", [P, ARENA])
        fr_arena = sb("fr_arena", [P, FR_ARENA], F32R)

        taken = [0, 0]

        def carve(n, reset=None, fr=0):
            if reset is not None:
                taken[fr] = reset
            a = taken[fr]
            taken[fr] += n
            assert taken[fr] <= (ARENA, FR_ARENA)[fr]
            return (arena, fr_arena)[fr][:, a:a + n]

        def table(name, *dims):
            a, n = TAB[name]
            return tab[:, a:a + n]

        ident = table("ident")

        xf = xn[:, :, :].rearrange("p t n -> p (t n)")
        xprod = carve(4 * BANK, 0).rearrange("p (q n) -> p q n", q=4)
        small = arena[0:51, 4096:4096 + P]
        zqk = carve(T * ZV, 0).rearrange("p (t n) -> p t n", t=T)
        zl = carve(T * (ZW - ZCQ)).rearrange("p (t n) -> p t n", t=T)
        zv = carve(T * NKV * HD).rearrange("p (t n) -> p t n", t=T)
        rows = carve(MH * MQ * T)
        qr = rows[:, 0:T * 512].rearrange("p (t n) -> p t n", t=T)
        kr = rows[:, T * 512:T * 768].rearrange("p (t j u n) -> p t j u n", t=T, j=NKV, u=2)
        km = rows.rearrange("p (t h n) -> p t h n", t=T, h=MH)
        qT = carve(4 * SEQ).rearrange("p (c n) -> p c n", c=4)
        kT = carve(NKV * SEQ).rearrange("p (c n) -> p c n", c=NKV)
        vm = carve(T * MH * HD).rearrange("p (t h n) -> p t h n", t=T, h=MH)
        qmT = carve(MH * SEQ).rearrange("p (h n) -> p h n", h=MH)
        probs0 = carve(3 * BANK).rearrange("p (b n) -> p b n", b=3)
        rot = carve(4 * T * HD).rearrange("p (i t n) -> p i t n", i=4, t=T)
        grow = carve(2 * HD).rearrange("p (i n) -> p i n", i=2)
        kmT = arena[:, 0:MH * SEQ].rearrange("p (h n) -> p h n", h=MH)
        assert MH * SEQ <= T * (ZV + ZW - ZCQ)
        lat = qmT[:, 0:3, :]
        latTh = carve(3 * SEQ, 0, 1).rearrange("p (k n) -> p k n", k=3)
        latTl = carve(3 * SEQ, None, 1).rearrange("p (k n) -> p k n", k=3)
        qm = xf[:, 0:T * MH * MQ].rearrange("p (t h n) -> p t h n", t=T, h=MH)
        mtmp = xf[:, T * MH * MQ:T * D]
        prT_buf = mtmp
        dq = carve(DG * 4 * SEQ, 0).rearrange("p (g c n) -> p g c n", g=DG, c=4)
        dk = carve(DG * 4 * SEQ).rearrange("p (g c n) -> p g c n", g=DG, c=4)
        dv = carve(DG * T * 512).rearrange("p (g t n) -> p g t n", g=DG, t=T)
        probs1 = carve(3 * BANK).rearrange("p (b n) -> p b n", b=3)
        dtmp = probs1
        mask = xn[:, :, 0:BANK]
        sg = carve(FT * SEQ, 0).rearrange("p (f n) -> p f n", f=FT)
        hp = carve(FT * SEQ).rearrange("p (f n) -> p f n", f=FT)
        hTh = carve(2 * FT * SEQ, 0, 1).rearrange("p (b f n) -> p b f n", b=2, f=FT)
        hTl = carve(2 * FT * SEQ, None, 1).rearrange("p (b f n) -> p b f n", b=2, f=FT)
        xgp = carve(KD * P, 0).rearrange("p (k n) -> p k n", k=KD)
        msg = carve(BANK)
        mh = carve(2 * BANK).rearrange("p (b n) -> p b n", b=2)
        ysb = carve(D)
        acc = carve(T * D).rearrange("p (t n) -> p t n", t=T)
        sel = carve(T * P).rearrange("p (t n) -> p t n", t=T)
        selg = carve(T * P).rearrange("p (t n) -> p t n", t=T)
        selT = carve(T * P).rearrange("p (t n) -> p t n", t=T)
        moetab = carve(3 * P)
        tri, ones, iota = (moetab[:, i * P:(i + 1) * P] for i in range(3))
        xr = carve(KD * SEQ).rearrange("p (k n) -> p k n", k=KD)
        xgh = carve(KD * P, 0, 1).rearrange("p (k n) -> p k n", k=KD)
        xgl = carve(KD * P, None, 1).rearrange("p (k n) -> p k n", k=KD)
        mhTh = carve(2 * BANK, None, 1).rearrange("p (b n) -> p b n", b=2)
        mhTl = carve(2 * BANK, None, 1).rearrange("p (b n) -> p b n", b=2)
        pe_rows = carve(T * PD, ARENA - T * PD).rearrange("p (t n) -> p t n", t=T)
        pTh = carve(PK * SEQ, 0, 1).rearrange("p (k n) -> p k n", k=PK)
        pTl = carve(PK * SEQ, None, 1).rearrange("p (k n) -> p k n", k=PK)

        tab_in = sem("tab_in")
        gain_in = sem("gain_in")
        grow_in = sem("grow_in")
        wr_in = sem("wr_in")
        x_in = sem("x_in")
        gb_in = [sem(f"gb_in{i}") for i in range(3)]
        mask_in = sem("mask_in")
        moetab_in = sem("moetab_in")
        p_in = sem("p_in")
        slot_in = [sem(f"slot_in{i}") for i in range(RAW)]
        whi_ok = sem("whi_ok")
        split_ok = sem("split_ok")
        chunk_used = sem("chunk_used")
        eps_ok = sem("eps_ok")
        acc_zero = sem("acc_zero")
        mqT_ok = sem("mqT_ok")
        mkT_ok = sem("mkT_ok")
        out_done = sem("out_done")
        dve_step = sem("dve_step")
        act_step = sem("act_step")
        gt_tr = sem("gt_tr")
        gt_ok = sem("gt_ok")
        rstd_ok = sem("rstd_ok")
        xn_ok = sem("xn_ok")
        xn_tr = sem("xn_tr")
        xp_ok = sem("xp_ok")
        xh_ok = sem("xh_ok")
        xT_ok = sem("xT_ok")
        lp_ok = sem("lp_ok")
        lh_ok = sem("lh_ok")
        oh_ok = sem("oh_ok")
        fp_ok = sem("fp_ok")
        fh_ok = sem("fh_ok")
        ph_ok = sem("ph_ok")
        m_xgp = sem("m_xgp")
        m_xgh = sem("m_xgh")
        m_hth = sem("m_hth")
        y_ok = sem("y_ok")
        ysq_ok = sem("ysq_ok")
        prstd_ok = sem("prstd_ok")
        h_ok = sem("h_ok")
        z_mm = sem("z_mm")
        z_ok = sem("z_ok")
        hss_ok = sem("hss_ok")
        hrs_ok = sem("hrs_ok")
        lat_tr = sem("lat_tr")
        lat_ok = sem("lat_ok")
        up_mm = sem("up_mm")
        up_ok = sem("up_ok")
        qk_ok = sem("qk_ok")
        qk_tr = sem("qk_tr")
        qkT_ok = sem("qkT_ok")
        mrow_ok = sem("mrow_ok")
        m_tr = sem("m_tr")
        mT_ok = sem("mT_ok")
        sc_mm = sem("sc_mm")
        sc_max = sem("sc_max")
        sc_exp = sem("sc_exp")
        pr_ok = sem("pr_ok")
        pr_tr = sem("pr_tr")
        prT_ok = sem("prT_ok")
        pv_mm = sem("pv_mm")
        oT_ok = sem("oT_ok")
        f_g = sem("f_g")
        f_silu = sem("f_silu")
        f_u = sem("f_u")
        f_h = sem("f_h")
        p_tr = sem("p_tr")
        pT_ok = sem("pT_ok")
        pl_mm = sem("pl_mm")
        pl_exp = sem("pl_exp")
        dz_mm = sem("dz_mm")
        dz_ok = sem("dz_ok")
        dr_ok = sem("dr_ok")
        d_tr = sem("d_tr")
        dT_ok = sem("dT_ok")
        r_mm = sem("r_mm")
        r_ev = sem("r_ev")
        r_mask = sem("r_mask")
        r_gap = sem("r_gap")
        r_eg = sem("r_eg")
        r_pos = sem("r_pos")
        r_cnt = sem("r_cnt")
        m_sel = sem("m_sel")
        m_ga = sem("m_ga")
        m_xg = sem("m_xg")
        m_st = sem("m_st")
        m_sT = sem("m_sT")
        m_silu = sem("m_silu")
        m_h = sem("m_h")
        m_t = sem("m_t")
        m_ht = sem("m_ht")
        m_y = sem("m_y")
        m_ysb = sem("m_ysb")
        m_sc = sem("m_sc")
        m_acc = sem("m_acc")

        def kt_rows(w):
            return w.rearrange("(k p) n -> p k n", p=P)

        chunks = []
        for a in range(N_IN):
            chunks.append((kt_rows(ab_w_in[0])[:, a:a + 1, :], 1, ZW))
        chunks.append((kt_rows(mla_w_uq[0]), 2, MH * MQ))
        chunks.append((kt_rows(mla_w_ukv[0]), 1, MH * 2 * HD))
        for a in range(N_ABOUT):
            chunks.append((kt_rows(ab_w_out[0])[:, 2 * a:2 * a + 2, :], 2, D))

        def ffn_source(kind, c, half, wg, wu, wd):
            if kind == "d":
                a = FT * c + 2 * half
                return wd[:, a:a + 2, :], 2, D
            return (wg if kind == "g" else wu)[:, 4 * half:4 * half + 4, FC * c:FC * (c + 1)], 4, FC

        dense = [kt_rows(w[0]) for w in (ffn_w_gate, ffn_w_up, ffn_w_down)]
        for kind, c, half in FFN:
            chunks.append(ffn_source(kind, c, half, *dense))

        def ple_source(l):
            return [(kt_rows(ple_w_proj[l]), PK, D)] + [(kt_rows(ple_w_gate[l])[:, 2 * a:2 * a + 2, :], 2, D) for a in range(4)]

        chunks += ple_source(0)
        for c in range(9):
            for half in range(2):
                chunks.append((kt_rows(dil_w_qkv[0])[:, 4 * half:4 * half + 4, FC * c:FC * (c + 1)], 4, FC))
        for a in range(N_DOUT):
            chunks.append((kt_rows(dil_w_out[0])[:, 2 * a:2 * a + 2, :], 2, D))
        assert len(chunks) == C_MOE


        def load(eng, n, source, tiles, width, rounds=0):
            if n >= RAW:
                eng.wait_ge(split_ok, n - RAW + 1 + N_FFN * rounds)
            dst = raw[:, n % RAW, 0:tiles * width].rearrange("p (k n) -> p k n", k=tiles)
            eng.dma_start(dst, source).then_inc(slot_in[n % RAW], 16)

        def width_of(n):
            return chunks[n][1] * chunks[n][2] if n < C_MOE else SLOT

        def chunk_hi(act, n, rounds=0):
            act.wait_ge(slot_in[n % RAW], 16 * (n // RAW + 1) + 16 * (N_FFN // RAW) * rounds)
            if n >= SPLIT:
                act.wait_ge(chunk_used, n - SPLIT + 1 + N_FFN * rounds)
            w = width_of(n)
            act.activation(whi[:, n % SPLIT, 0:w], raw[:, n % RAW, 0:w], ACT.Copy).then_inc(whi_ok, 1)

        def chunk_lo(dve, n, rounds=0):
            dve.wait_ge(whi_ok, n + 1 + N_FFN * rounds)
            w = width_of(n)
            dve.tensor_tensor(wlo[:, n % SPLIT, 0:w], raw[:, n % RAW, 0:w], whi[:, n % SPLIT, 0:w].bitcast(F32),
                              ALU.subtract).then_inc(split_ok, 1)

        def chunk(pe, n, tiles, width, rounds=0):
            pe.wait_ge(split_ok, n + 1 + N_FFN * rounds)
            return [w[:, n % SPLIT, 0:tiles * width].rearrange("p (k n) -> p k n", k=tiles) for w in (whi, wlo)]

        class Ahead:

            def __init__(self, split, eng):
                self.split, self.eng, self.next = split, eng, 0

            def __call__(self, n):
                while self.next <= n:
                    self.split(self.eng, self.next)
                    self.next += 1

        def used(eng, n, rounds=0):
            eng.wait_ge(chunk_used, n + 1 + N_FFN * rounds)

        Y_BEFORE = [0, 1, 2, 4, 5, 7]
        Y_CHUNK = {0: C_FFN - 1, 1: C_PLE0 - 1, 3: C_MOE - 1}

        def output_ready(eng, j, t):
            if j in Y_CHUNK and t:
                used(eng, Y_CHUNK[j])
            else:
                eng.wait_ge(y_ok, Y_BEFORE[j] + t + 1)

        def first_or_used(eng, s, count, n, second):
            if second:
                used(eng, n)
            else:
                eng.wait_ge(s, count)

        def gates_ready(eng, l, t):
            if l == 0 and t:
                used(eng, C_QKV - 1)
            else:
                eng.wait_ge(pl_mm, 2 * l - (1 if l else 0) + t + 1)

        def hidden_used(eng, r, c):
            used(eng, C_MOE - 1 if c < 2 else C_MOE + FFN_AT["d", c - 2, 1], r)

        def of(x, n):
            return x.unsqueeze(2).to_broadcast([P, x.shape[1], n])

        def bank(b, n=BANK):
            return ps[:, b, 0:n]

        def pair(b):
            return ps[:, b:b + 2, :].rearrange("p b n -> p (b n)")

        GAIN = {"mix": 0, "ffn": 16, "ple": 32, "mla": 48}
        PRE = [("mix", 0), ("ffn", 0), ("ple", 0), ("mix", 1), ("ffn", 1), ("ple", 1)]
        N_GQA, N_U0, N_U = NQ, NQ + MH, NQ + MH + T * DH
        S_BANK, T_BANK = (0, 1, 6), (2, 3)

        def probs(u):
            return (probs0 if u < N_U0 else probs1)[:, u % 3, :]

        def oT_before(u):
            return u // 2 if u < N_U0 else N_U0 // 2 + (u - N_U0) // 4

        def o_bank(u):
            return 4 + oT_before(u) % 2

        block = ctx.enter_context(nc.Block())

        @block.sync
        def _(sp):
            sp.dma_start(h[:, :, :], x.rearrange("b (p t) d -> p t (b d)", t=T)).then_inc(x_in, 16)
            for n, (source, tiles, width) in enumerate(chunks):
                load(sp, n, source, tiles, width)

            experts_w = [w.rearrange("a e (k p) n -> (a e) p k n", p=P) for w in (moe_w_gate, moe_w_up, moe_w_down)]

            def expert_loads(e, r):
                for j, (kind, c, half) in enumerate(FFN):
                    source = ffn_source(kind, c, half, *[w[e] for w in experts_w])
                    load(sp, C_MOE + j, *source, r)

            with sp.Fori(0, NE) as e:
                expert_loads(e, e)
            sp.wait_ge(r_cnt, 2)
            over = sp.value_load(noveri[0:1, 0:1], min_val=0, max_val=MAX_OVER)
            with sp.Fori(0, MAX_OVER) as j:
                with sp.If(over > j):
                    e = sp.value_load(cidx[0:1, bass.ds(j, 1)], min_val=0, max_val=NE - 1)
                    expert_loads(e, j + NE)
            for i, source in enumerate(ple_source(1)):
                load(sp, C_MOE + i, *source, over + NE)
            for t in range(T):
                sp.wait_ge(h_ok, 2 * 5 + t + 1)
                sp.dma_start(out.rearrange("b (p t) d -> p t (b d)", t=T)[:, t, :], h[:, t, :]).then_inc(out_done, 16)
            sp.wait_ge(out_done, 16 * T)

        @block.gpsimd
        def _(pool):
            def rows_of(vec, n):
                return vec.to_broadcast([P, n])

            for vec, a in ((mix_pre_g, 0), (ffn_pre_g, 16), (ple_gate_norm_g, 32)):
                pool.dma_start(small[a:a + 16, :], vec.rearrange("i (k n) -> (i k) n", n=P)).then_inc(gain_in, 16)
            pool.dma_start(small[48:50, :], mla_q_norm_g.rearrange("i (k n) -> (i k) n", n=P)).then_inc(gain_in, 16)
            pool.dma_start(small[50:51, :], mla_kv_norm_g).then_inc(gain_in, 16)
            pool.dma_start(tab[:, :], tables[:, 0:TAB_RES]).then_inc(tab_in, 16)
            pool.dma_start(grow[:, 0, :], rows_of(gqa_q_norm_g, HD)).then_inc(grow_in, 16)
            pool.dma_start(grow[:, 1, :], rows_of(gqa_k_norm_g, HD)).then_inc(grow_in, 16)
            for n, g in enumerate((mix_post_g, ffn_post_g, ple_post_g)):
                pool.dma_start(gb[:, n, :], rows_of(g[0:1, :], D)).then_inc(gb_in[n], 16)
            pool.dma_start(wr[:, :, :], kt_rows(moe_w_router[0])).then_inc(wr_in, 16)
            pool.wait_ge(oT_ok, N_U0 // 2)
            pool.dma_start(pe_rows, p[0, 0].rearrange("(p t) n -> p t n", t=T)).then_inc(p_in, 16)
            pool.wait_ge(h_ok, 2 * 3)
            for n, g in enumerate((mix_post_g, ffn_post_g, ple_post_g)):
                pool.dma_start(gb[:, n, :], rows_of(g[1:2, :], D)).then_inc(gb_in[n], 16)
            pool.wait_ge(d_tr, 10)
            pool.dma_start(mask, tables[:, TAB_MASK:TAB_ALL].rearrange("p (t n) -> p t n", t=T)).then_inc(mask_in, 16)
            pool.wait_ge(oT_ok, N_U0 // 2 + DH // 2)
            pool.dma_start(moetab, tables[:, TAB_MOE:TAB_MASK]).then_inc(moetab_in, 16)
            pool.dma_start(pe_rows, p[1, 0].rearrange("(p t) n -> p t n", t=T)).then_inc(p_in, 16)
            pool.memset(acc, 0.0).then_inc(acc_zero, 1)

        @block.scalar
        def _(act):
            steps = [0]

            def link(ins):
                steps[0] += 1
                ins.then_inc(act_step, 1)
                act.wait_ge(act_step, steps[0])

            def copy(out, in_, scale=1.0):
                return act.activation(out, in_, ACT.Copy, scale=scale)

            def scales(out, total, width, ok, inputs_ok=None):
                link(act.activation(ssl[:, :], total, ACT.Ln, bias=eps[:, 0:1], scale=1.0 / width))
                act.activation(out, ssl[:, :], ACT.Exp, scale=-0.5).then_inc(ok, 1)

            ahead = Ahead(chunk_hi, act)

            def upper(out, in_, ok):
                copy(out, in_).then_inc(ok, 1)

            def pre(i):
                for t in range(T):
                    if i == 0:
                        act.wait_ge(x_in, 16)
                    else:
                        act.wait_ge(h_ok, 2 * (i - 1) + t + 1)
                    q = act.activation(xn[:, t, :], h[:, t, :], ACT.Square, accum_out=ss[:, t:t + 1])
                link(q)
                scales(rstd[:, :], ss[:, :], D, rstd_ok)
                if i == 4:
                    return
                for q in range(4):
                    t, half = divmod(q, 2)
                    act.wait_ge(xp_ok, 4 * (i - (i > 4)) + q + 1)
                    upper(xTh[:, 4 * half:4 * half + 4, t * P:(t + 1) * P],
                          xprod[:, q, :].rearrange("p (k n) -> p k n", k=4), xh_ok)

            def post(j, y):
                for t in range(T):
                    output_ready(act, j, t)
                    act.activation(arena[:, t * D:(t + 1) * D], y(t), ACT.Square, accum_out=ss[:, t:t + 1]).then_inc(ysq_ok, 1)
                act.wait_ge(ysq_ok, 2 * j + 2)
                scales(prstd[:, :], ss[:, :], D, prstd_ok)

            def exps(u):
                act.wait_ge(sc_max, u + 1)
                if u < N_U0:
                    if u >= 3:
                        act.wait_ge(pr_tr, u - 2)
                    s = GQA_SCALE if u < N_GQA else MLA_SCALE
                    for t in range(T):
                        last = act.activation(probs(u)[:, t * SEQ:(t + 1) * SEQ],
                                              ps[:, S_BANK[u % 3], t * SEQ:(t + 1) * SEQ], ACT.Exp,
                                              bias=snm[:, u % 3, t:t + 1], scale=s, accum_out=ssum[:, u % 3, t:t + 1])
                else:
                    last = act.activation(probs(u), probs(u), ACT.Exp, bias=snm[:, u % 3, 0:1],
                                          accum_out=ssum[:, u % 3, 0:1])
                last.then_inc(sc_exp, 1)

            def prT(u):
                act.wait_ge(pr_tr, u + 1)
                act.wait_ge(pv_mm, u)
                copy(prT_buf, bank(T_BANK[u % 2])).then_inc(prT_ok, 1)

            def attention(first, n, per):
                for i in range(n + 3):
                    if i < n:
                        exps(first + i)
                    if 2 <= i < n + 2:
                        prT(first + i - 2)
                    if i >= 3 and (i - 3) % per == per - 1:
                        u = first + i - 3
                        act.wait_ge(pv_mm, u + 1)
                        upper(xTh[:, (u - first) // per, :], bank(o_bank(u), SEQ), oh_ok)

            def ple(l):
                for t in range(T):
                    gates_ready(act, l, t)
                    act.activation(xn[:, t, :], pair(4 + 2 * t), ACT.Exp, scale=-1.0).then_inc(pl_exp, 1)

            act.wait_ge(eps_ok, 1)
            pre(0)
            ahead(C_UQ + 1)
            for t in range(T):
                first_or_used(act, z_mm, 1, C_UQ - 1, t)
                zb = ps[:, 3 * t:3 * t + 3, :]
                copy(zqk[:, t, 0:384], zb[:, 0, 0:384])
                copy(zqk[:, t, 384:ZV], zb[:, 1, 0:ZV - 384])
                copy(zv[:, t, :], zb[:, 1, ZV - 384:384])
                copy(zl[:, t, :], zb[:, 2, 0:ZW - ZCQ]).then_inc(z_ok, 1)
            act.wait_ge(z_ok, T)
            for t in range(T):
                act.activation(xf[:, 1280:1536], zl[:, t, 0:256], ACT.Square, accum_out=hss[:, t, 10:11])
                q = act.activation(xf[:, 1536:1664], zl[:, t, 256:384], ACT.Square, accum_out=hss[:, t, 11:12])
                link(q)
            for t in range(T):
                act.wait_ge(lp_ok, t + 1)
                upper(latTh[:, :, t * P:(t + 1) * P], lat[:, :, t * P:(t + 1) * P], lh_ok)
            act.wait_ge(hss_ok, 1)
            for a, b, width in ((0, 10, HD), (10, 11, 256), (11, 12, 128)):
                q = act.activation(hrs[:, :, a:b], hss[:, :, a:b], ACT.Ln, bias=eps[:, 0:1], scale=1.0 / width)
            link(q)
            act.activation(hrs[:, :, :], hrs[:, :, :], ACT.Exp, scale=-0.5).then_inc(hrs_ok, 1)
            act.wait_ge(hrs_ok, 1)
            ahead(C_UQ + 2)
            for t in range(T):
                first_or_used(act, up_mm, 1, C_UQ, t)
                copy(qm[:, t, :, :].rearrange("p h n -> p (h n)").rearrange("p (b n) -> p b n", b=2),
                     ps[:, 2 * t:2 * t + 2, 0:384], hrs[:, t, 10:11]).then_inc(up_ok, 1)
            ahead(C_UKV + 2)
            act.wait_ge(qk_tr, 3)
            for t in range(T):
                first_or_used(act, up_mm, 2, C_UKV, t)
                kv = pair(4 + 2 * t).rearrange("p (h n) -> p h n", h=MH)
                copy(km[:, t, :, 0:MN], kv[:, :, 0:MN], hrs[:, t, 11:12])
                copy(vm[:, t, :, :], kv[:, :, MN:], hrs[:, t, 11:12]).then_inc(up_ok, 1)
            ahead(C_UKV + 3)
            for b in range(4):
                act.wait_ge(m_tr, b + 1)
                copy(qmT[0:MQ, 2 * b:2 * b + 2, :].rearrange("p h n -> p (h n)"), ps[0:MQ, b, :]).then_inc(mqT_ok, 1)
            attention(0, N_U0, 2)
            ahead(C_FFN + 1)
            post(0, lambda t: pair(4 + 2 * t))
            ahead(C_FFN + 2)
            pre(1)
            for s, (kind, c, half) in enumerate(FFN):
                n = C_FFN + s
                ahead(n + 2)
                if kind == "g" and half:
                    for b in range(2):
                        first_or_used(act, f_g, c + 1, n, b)
                        if c:
                            act.wait_ge(fp_ok, 2 * c - 1 + b)
                        act.activation(sg[:, 2 * b:2 * b + 2, :].rearrange("p f n -> p (f n)"), bank(b),
                                       ACT.Silu).then_inc(f_silu, 1)
                if kind == "u" and half:
                    if c >= 2:
                        used(act, C_FFN + FFN_AT["d", c - 2, 1])
                    for b in range(2):
                        act.wait_ge(fp_ok, 2 * c + b + 1)
                        upper(hTh[:, c % 2, 2 * b:2 * b + 2, :], hp[:, 2 * b:2 * b + 2, :], fh_ok)
            post(1, lambda t: pair(4 + 2 * t))
            ahead(C_PLE0 + 2)
            pre(2)
            act.wait_ge(p_tr, 1)
            upper(pTh.rearrange("p k n -> p (k n)"), bank(4), ph_ok)
            ahead(C_QKV + 1)
            ple(0)
            post(2, lambda t: xn[:, t, :])
            ahead(C_QKV + 2)
            pre(3)
            for c in range(9):
                g, kind = divmod(c, 3)
                n = C_QKV + 2 * c + 1
                ahead(n + 2)
                for t in range(T):
                    first_or_used(act, dz_mm, c + 1, n, t)
                    src = bank(2 * (c % 2) + t)
                    if kind == 2:
                        copy(dv[:, g, t, :], src).then_inc(dz_ok, 1)
                    else:
                        qi = 2 * g + kind
                        if qi >= 2:
                            act.wait_ge(d_tr, 2 * qi - 2)
                        copy(xn[:, t, (qi % 2) * 512:(qi % 2) * 512 + 512], src).then_inc(dz_ok, 1)
            attention(N_U0, T * DH, 4)
            post(3, lambda t: pair(4 + 2 * t))
            ahead(C_MOE + 1)
            pre(4)
            act.wait_ge(r_gap, 1)
            act.activation(rs[:, 5, :], rs[:, 4, :], ACT.Exp).then_inc(r_eg, 1)

            def gathered_hi(r):
                for half in range(2):
                    act.wait_ge(m_xgp, 2 * r + half + 1)
                    upper(xgh[:, 4 * half:4 * half + 4, :], xgp[:, 4 * half:4 * half + 4, :], m_xgh)

            def hidden_hi(r, c):
                act.wait_ge(m_t, r * NFC + c + 1)
                hidden_used(act, r, c)
                upper(mhTh[:, c % 2, :], bank(2), m_hth)

            def expert(r):
                for j, (kind, c, half) in enumerate(FFN):
                    chunk_hi(act, C_MOE + j + 2, r)
                    if (kind, half) == ("g", 1):
                        used(act, C_MOE + j, r)
                        act.wait_ge(m_h, r * NFC + c)
                        act.activation(msg, bank(0), ACT.Silu).then_inc(m_silu, 1)
                    if (kind, half) == ("u", 0) and c:
                        hidden_hi(r, c - 1)
                    if (kind, c, half) == ("d", NFC - 2, 1):
                        hidden_hi(r, NFC - 1)
                for half in range(2):
                    if half:
                        used(act, C_MOE + N_FFN - 1, r)
                    else:
                        act.wait_ge(m_y, r + 1)
                    act.wait_ge(m_sc, r * 4)
                    copy(ysb[:, half * BANK:(half + 1) * BANK], bank(4 + half)).then_inc(m_ysb, 1)
                gathered_hi(r + 1)

            act.wait_ge(r_cnt, 2)
            over = act.value_load(noveri[0:1, 0:1], min_val=0, max_val=MAX_OVER)
            gathered_hi(0)
            with act.Fori(0, NE) as e:
                expert(e)
            with act.Fori(0, MAX_OVER) as j:
                with act.If(over > j):
                    expert(j + NE)
            post(4, lambda t: acc[:, t, :])
            pre(5)
            act.wait_ge(p_tr, 2)
            upper(pTh.rearrange("p k n -> p (k n)"), bank(4), ph_ok)
            for i in range(2, N_PLE):
                chunk_hi(act, C_MOE + i, over + NE)
            ple(1)
            post(5, lambda t: xn[:, t, :])

        @block.vector
        def _(dve):
            steps = [0]

            def link(ins):
                steps[0] += 1
                ins.then_inc(dve_step, 1)
                dve.wait_ge(dve_step, steps[0])

            ahead = Ahead(chunk_lo, dve)

            def lower(out, whole, hi, ok):
                dve.tensor_tensor(out, whole, hi.bitcast(F32), ALU.subtract).then_inc(ok, 1)

            def pre(i):
                kind, l = PRE[i]
                dve.wait_ge(rstd_ok, i + 1)
                for t in range(T):
                    dve.tensor_scalar(xn[:, t, :], h[:, t, :], rstd[:, t:t + 1], None, ALU.mult).then_inc(xn_ok, 1)

                def rest(q):
                    t, half = divmod(q, 2)
                    dve.wait_ge(xh_ok, 4 * (i - (i > 4)) + q + 1)
                    at = (slice(None), slice(4 * half, 4 * half + 4), slice(t * P, (t + 1) * P))
                    lower(xTl[at], xprod[:, q, :].rearrange("p (k n) -> p k n", k=4), xTh[at], xT_ok)

                for q in range(4):
                    t, half = divmod(q, 2)
                    dve.wait_ge(xn_tr, 4 * i + q + 1)
                    a = GAIN[kind] + KD * l + 4 * half
                    to = xprod[:, q, :].rearrange("p (k n) -> p k n", k=4)
                    if i == 4:
                        to = xr[:, 4 * half:4 * half + 4, t * P:(t + 1) * P]
                    dve.tensor_tensor(to, bank(q).rearrange("p (k n) -> p k n", k=4),
                                      of(gT[:, a:a + 4], P), ALU.mult).then_inc(xT_ok if i == 4 else xp_ok, 1)
                    if q and i != 4:
                        rest(q - 1)
                if i != 4:
                    rest(3)

            def post(j, y):
                g, l = j % 3, j // 3
                dve.wait_ge(gb_in[g], 16 * (l + 1))
                for t in range(T):
                    dve.wait_ge(ysq_ok, 2 * j + t + 1)
                    q = dve.tensor_tensor(xn[:, t, :], y(t), gb[:, g, :], ALU.mult)
                link(q)
                dve.wait_ge(prstd_ok, j + 1)
                for t in range(T):
                    dve.scalar_tensor_tensor(out=h[:, t, :], in0=xn[:, t, :], scalar=prstd[:, t:t + 1],
                                             in1=h[:, t, :], op0=ALU.mult, op1=ALU.add).then_inc(h_ok, 1)

            def rotate(out, rows_, cos, sin, half, a, b):
                dve.tensor_tensor(a, rows_, cos, ALU.mult)
                lo, hi = slice(0, half), slice(half, 2 * half)
                dve.tensor_tensor(b[..., lo], rows_[..., hi], sin[..., lo], ALU.mult)
                link(dve.tensor_tensor(b[..., hi], rows_[..., lo], sin[..., hi], ALU.mult))
                return dve.tensor_tensor(out, a, b, ALU.add)

            def maxes(u):
                dve.wait_ge(sc_mm, u + 1)
                b = u % 3
                if u < N_U0:
                    s = GQA_SCALE if u < N_GQA else MLA_SCALE
                    link(dve.tensor_reduce(smax[:, b, :], bank(S_BANK[b]).rearrange("p (t n) -> p t n", t=T), AX_X, ALU.max))
                    dve.tensor_scalar(snm[:, b, :], smax[:, b, :], -s, None, ALU.mult).then_inc(sc_max, 1)
                else:
                    if u >= N_U0 + 3:
                        dve.wait_ge(pr_tr, u - 2)
                    link(dve.tensor_tensor_reduce(out=probs(u), in0=bank(S_BANK[b]), in1=mask[:, u % T, :],
                                                  scale=HD ** -0.5, scalar=-3e38, op0=ALU.add, op1=ALU.max,
                                                  accum_out=smax[:, b, 0:1]))
                    dve.tensor_scalar(snm[:, b, 0:1], smax[:, b, 0:1], -1.0, None, ALU.mult).then_inc(sc_max, 1)

            def normalise(u):
                b = u % 3
                dve.wait_ge(sc_exp, u + 1)
                n = T if u < N_U0 else 1
                link(dve.reciprocal(srec[:, b, 0:n], ssum[:, b, 0:n]))
                w = BANK // n
                for t in range(n):
                    q = dve.tensor_scalar(probs(u)[:, t * w:(t + 1) * w], probs(u)[:, t * w:(t + 1) * w],
                                          srec[:, b, t:t + 1], None, ALU.mult)
                q.then_inc(pr_ok, 1)

            def attention(first, n, per):
                for i in range(n + 3):
                    if i < n:
                        maxes(first + i)
                    if 1 <= i <= n:
                        normalise(first + i - 1)
                    if i >= 3 and (i - 3) % per == per - 1:
                        u = first + i - 3
                        dve.wait_ge(oh_ok, oT_before(u) + 1)
                        tile = (u - first) // per
                        lower(xTl[:, tile, :], bank(o_bank(u), SEQ), xTh[:, tile, :], oT_ok)

            def ple(l):
                dve.wait_ge(ph_ok, l + 1)
                lower(pTl.rearrange("p k n -> p (k n)"), bank(4), pTh.rearrange("p k n -> p (k n)"), pT_ok)
                if l == 0:
                    ahead(C_QKV + 1)
                else:
                    for i in range(2, N_PLE):
                        chunk_lo(dve, C_MOE + i, over + NE)
                for t in range(T):
                    dve.wait_ge(pl_exp, 2 * l + t + 1)
                    link(dve.tensor_scalar(xn[:, t, :], xn[:, t, :], 1.0, None, ALU.add))
                    link(dve.reciprocal(xn[:, t, :], xn[:, t, :]))
                    dve.tensor_tensor(xn[:, t, :], pair(2 * t), xn[:, t, :], ALU.mult).then_inc(y_ok, 1)

            dve.memset(eps[:, :], EPS).then_inc(eps_ok, 1)
            dve.memset(posm[:, :, JOBS - 1:], -1.0)
            dve.memset(gate[:, :, JOBS - 1:], 0.0)
            dve.wait_ge(gt_tr, 1)
            link(dve.tensor_copy(gT[:, :], bank(7, 51)))
            dve.wait_ge(tab_in, 16)
            dve.wait_ge(grow_in, 32)
            axC = table("axC").rearrange("p (t n) -> p t n", t=T)
            axS = table("axS").rearrange("p (t a f n) -> p t a f n", t=T, a=2, f=2)
            for i in range(2):
                dve.tensor_tensor(rot[:, 2 * i, :, :], axC, grow[:, i:i + 1, :].to_broadcast([P, T, HD]), ALU.mult)
                rv = rot[:, 2 * i + 1, :, :].rearrange("p t (a f n) -> p t a f n", a=2, f=2)
                gv = grow[:, i, :].rearrange("p (a f n) -> p a f n", a=2, f=2)
                for t in range(T):
                    for f in range(2):
                        q = dve.tensor_tensor(rv[:, t, :, f, :], axS[:, t, :, f, :], gv[:, :, 1 - f, :], ALU.mult)
            link(q)
            pre(0)
            ahead(C_UQ + 1)
            for t in range(T):
                dve.wait_ge(lat_tr, t + 1)
                dve.tensor_tensor(lat[:, :, t * P:(t + 1) * P], bank(6 + t, 3 * P).rearrange("p (k n) -> p k n", k=3),
                                  of(gT[:, 48:51], P), ALU.mult).then_inc(lp_ok, 1)
            dve.wait_ge(z_ok, T)
            sq = xf[:, 0:T * ZV].rearrange("p (t n) -> p t n", t=T)
            link(dve.tensor_tensor(sq, zqk, zqk, ALU.mult))
            for t in range(T):
                q = dve.tensor_reduce(hss[:, t, 0:10], sq[:, t, :].rearrange("p (h n) -> p h n", h=10), AX_X, ALU.add)
            q.then_inc(hss_ok, 1)
            for t in range(T):
                dve.wait_ge(lh_ok, t + 1)
                at = (slice(None), slice(None), slice(t * P, (t + 1) * P))
                lower(latTl[at], lat[at], latTh[at], lat_ok)
            ahead(C_UQ + 2)
            dve.wait_ge(hss_ok, 1)
            sa, sb_ = probs0[:, 0, :], probs0[:, 1, :]
            for t in range(T):
                for first, heads, i in ((ZQ, NQ, 0), (ZK, NKV, 1)):
                    n = heads * HD
                    src = zqk[:, t, first:first + n]
                    v5 = "p (h a f n) -> p h a f n"
                    cos = rot[:, 2 * i, t:t + 1, :].to_broadcast([P, heads, HD])
                    sinv = rot[:, 2 * i + 1, t, :].rearrange("p (a f n) -> p a f n", a=2, f=2)
                    s5 = src.rearrange(v5, h=heads, a=2, f=2)
                    b5 = sb_[:, 0:n].rearrange(v5, h=heads, a=2, f=2)
                    dve.tensor_tensor(sa[:, 0:n].rearrange("p (h n) -> p h n", h=heads),
                                      src.rearrange("p (h n) -> p h n", h=heads), cos, ALU.mult)
                    for f in range(2):
                        q = dve.tensor_tensor(b5[:, :, :, f, :], s5[:, :, :, 1 - f, :],
                                              sinv[:, :, f, :].unsqueeze(1).to_broadcast([P, heads, 2, 16]), ALU.mult)
                    link(q)
                    link(dve.tensor_tensor(sa[:, 0:n], sa[:, 0:n], sb_[:, 0:n], ALU.add))
                    if t == 0 and i == 0:
                        dve.wait_ge(hrs_ok, 1)
                    a3 = sa[:, 0:n].rearrange("p (h n) -> p h n", h=heads)
                    sc = of(hrs[:, t, (0, NQ)[i]:(NQ, NQ + NKV)[i]], HD)
                    if i == 0:
                        link(dve.tensor_tensor(qr[:, t, :].rearrange("p (h n) -> p h n", h=heads), a3, sc, ALU.mult))
                    else:
                        for u in range(2):
                            q = dve.tensor_tensor(kr[:, t, :, u, :], a3, sc, ALU.mult)
                        link(q)
            dve.sem_inc(qk_ok, 1)
            ahead(C_UKV + 2)
            for t in range(T):
                dve.wait_ge(qk_tr, t + 1)
                dve.tensor_copy(qT[:, :, t * P:(t + 1) * P], bank(t).rearrange("p (c n) -> p c n", c=4)).then_inc(qkT_ok, 1)
            dve.wait_ge(qk_tr, 3)
            dve.tensor_copy(kT.rearrange("p j n -> p (j n)"), bank(2)).then_inc(qkT_ok, 1)
            mlC = table("mlC").rearrange("p (t n) -> p t n", t=T)
            mlS = table("mlS").rearrange("p (t n) -> p t n", t=T)
            dve.wait_ge(up_ok, T)
            hb = [P, T, MH, MR]
            ma, mb = mtmp[:, 0:512].rearrange("p (t h n) -> p t h n", t=T, h=MH), probs0[:, 2, :].rearrange("p (t h n) -> p t h n", t=T, h=MH)
            link(rotate(qm[:, :, :, MN:], qm[:, :, :, MN:], mlC.unsqueeze(2).to_broadcast(hb),
                        mlS.unsqueeze(2).to_broadcast(hb), MR // 2, ma, mb))
            ka, kb = (sa[:, i * 64:(i + 1) * 64].rearrange("p (t n) -> p t n", t=T) for i in range(2))
            kro = sa[:, 128:192].rearrange("p (t n) -> p t n", t=T)
            link(rotate(kro, zl[:, :, ZKR - ZCQ:], mlC, mlS, MR // 2, ka, kb))
            dve.tensor_copy(km[:, :, :, MN:], kro.unsqueeze(2).to_broadcast(hb)).then_inc(mrow_ok, 1)
            ahead(C_UKV + 3)
            for b in range(4):
                dve.wait_ge(m_tr, 4 + b + 1)
                dve.tensor_copy(kmT[0:MQ, 2 * b:2 * b + 2, :].rearrange("p h n -> p (h n)"), ps[0:MQ, 4 + b, :]).then_inc(mkT_ok, 1)
            attention(0, N_U0, 2)
            ahead(C_FFN + 1)
            post(0, lambda t: pair(4 + 2 * t))
            ahead(C_FFN + 2)
            pre(1)
            for s, (kind, c, half) in enumerate(FFN):
                n = C_FFN + s
                ahead(n + 2)
                if kind == "u" and half:
                    for b in range(2):
                        dve.wait_ge(f_silu, 2 * c + b + 1)
                        first_or_used(dve, f_u, c + 1, n, b)
                        if c:
                            dve.wait_ge(f_h, 2 * c)
                        dve.tensor_tensor(hp[:, 2 * b:2 * b + 2, :].rearrange("p f n -> p (f n)"),
                                          sg[:, 2 * b:2 * b + 2, :].rearrange("p f n -> p (f n)"),
                                          bank(2 + b), ALU.mult).then_inc(fp_ok, 1)
                    for b in range(2):
                        dve.wait_ge(fh_ok, 2 * c + b + 1)
                        at = (slice(None), c % 2, slice(2 * b, 2 * b + 2), slice(None))
                        lower(hTl[at], hp[:, 2 * b:2 * b + 2, :], hTh[at], f_h)
            post(1, lambda t: pair(4 + 2 * t))
            ahead(C_PLE0 + 2)
            pre(2)
            ple(0)
            post(2, lambda t: xn[:, t, :])
            ahead(C_QKV + 2)
            pre(3)
            dC = table("diC").rearrange("p (t n) -> p t n", t=T).unsqueeze(2).to_broadcast([P, T, DH, 16])
            dS = table("diS").rearrange("p (t n) -> p t n", t=T).unsqueeze(2).to_broadcast([P, T, DH, 16])
            da, db = (dtmp[:, i, 0:256].rearrange("p (t h n) -> p t h n", t=T, h=DH) for i in range(2))

            def dil_T(qi):
                g, kind = divmod(qi, 2)
                for t in range(T):
                    dve.wait_ge(d_tr, 2 * qi + t + 1)
                    dve.tensor_copy((dq, dk)[kind][:, g, :, t * P:(t + 1) * P],
                                    bank(4 + 2 * (qi % 2) + t).rearrange("p (c n) -> p c n", c=4)).then_inc(dT_ok, 1)

            for c in range(9):
                g, kind = divmod(c, 3)
                ahead(C_QKV + 2 * c + 3)
                if kind < 2:
                    qi = 2 * g + kind
                    dve.wait_ge(dz_ok, 2 * c + 2)
                    rw = xn[:, :, (qi % 2) * 512:(qi % 2) * 512 + 512].rearrange("p t (h n) -> p t h n", h=DH)[:, :, :, 0:16]
                    q = rotate(rw, rw, dC, dS, 8, da, db)
                    link(q)
                    dve.sem_inc(dr_ok, 1)
                if c and (c - 1) % 3 < 2:
                    dil_T(2 * ((c - 1) // 3) + (c - 1) % 3)
            dve.wait_ge(mask_in, 16)
            attention(N_U0, T * DH, 4)
            post(3, lambda t: pair(4 + 2 * t))
            ahead(C_MOE + 1)
            pre(4)

            def R(i):
                return rt[:, i, :].rearrange("p (t n) -> p t n", t=T)

            def each(v):
                return v.unsqueeze(2).to_broadcast([P, T, NE])

            rev = table("rev").rearrange("p (t n) -> p t n", t=T)
            dve.wait_ge(r_mm, 1)
            link(dve.tensor_copy(rt[:, 0, :], bank(4, T * NE)))

            def largest(logits, top, eq, best, onehot):
                link(dve.tensor_reduce(rs[:, top, :], R(logits), AX_X, ALU.max))
                link(dve.tensor_tensor(R(eq), R(logits), each(rs[:, top, :]), ALU.is_equal))
                link(dve.tensor_tensor(R(eq), R(eq), rev, ALU.mult))
                link(dve.tensor_reduce(rs[:, best, :], R(eq), AX_X, ALU.max))
                link(dve.tensor_tensor(R(onehot), R(eq), each(rs[:, best, :]), ALU.is_equal))

            largest(0, 0, 1, 1, 2)
            link(dve.scalar_tensor_tensor(out=rt[:, 3, :], in0=rt[:, 2, :], scalar=-3e38, in1=rt[:, 0, :],
                                          op0=ALU.mult, op1=ALU.add))
            largest(3, 2, 4, 3, 5)
            dve.tensor_tensor(rs[:, 4, :], rs[:, 2, :], rs[:, 0, :], ALU.subtract).then_inc(r_gap, 1)
            dve.tensor_tensor(rt[:, 6, :], rt[:, 2, :], rt[:, 5, :], ALU.add).then_inc(r_mask, 1)
            dve.wait_ge(r_eg, 1)
            link(dve.tensor_scalar(rs[:, 6, :], rs[:, 5, :], 1.0, None, ALU.add))
            link(dve.reciprocal(rs[:, 7, :], rs[:, 6, :]))
            link(dve.tensor_tensor(rs[:, 1, :], rs[:, 5, :], rs[:, 7, :], ALU.mult))
            dve.tensor_tensor(R(7), R(2), each(rs[:, 7, :]), ALU.mult)
            link(dve.tensor_tensor(R(8), R(5), each(rs[:, 1, :]), ALU.mult))
            link(dve.tensor_tensor(gate[:, :, 0:NE], R(7), R(8), ALU.add))
            dve.wait_ge(r_pos, 1)
            counts = ps[:, 5, T * NE:(T + 1) * NE]
            link(dve.scalar_tensor_tensor(out=rt[:, 9, :], in0=bank(5, T * NE), scalar=1.0, in1=rt[:, 6, :],
                                          op0=ALU.add, op1=ALU.mult))
            link(dve.tensor_scalar(posm[:, :, 0:NE], R(9), -1.0, None, ALU.add))
            link(dve.tensor_copy(over8[:, :], counts))
            link(dve.max(cnt8[:, :], over8[:, :]))
            dve.max_index(cidx[:, :], cnt8[:, :], over8[:, :]).then_inc(r_cnt, 1)
            dve.wait_ge(r_cnt, 1)
            link(dve.tensor_scalar(over8[:, :], cnt8[:, :], float(P), None, ALU.is_gt))
            link(dve.tensor_reduce(nover[:, :], over8[:, :], AX_X, ALU.add))
            dve.tensor_copy(noveri[:, :], nover[:, :]).then_inc(r_cnt, 1)
            dve.wait_ge(r_cnt, 2)
            over = dve.value_load(noveri[0:1, 0:1], min_val=0, max_val=MAX_OVER)
            for j in range(MAX_OVER):
                e = dve.value_load(cidx[0:1, j:j + 1], min_val=0, max_val=NE - 1)
                dve.tensor_scalar(posm[:, :, NE + j:NE + j + 1], posm[:, :, bass.ds(e, 1)], float(-P), None, ALU.add)
                q = dve.tensor_copy(gate[:, :, NE + j:NE + j + 1], gate[:, :, bass.ds(e, 1)])
            link(q)
            dve.wait_ge(moetab_in, 16)
            dve.wait_ge(acc_zero, 1)

            def select(r):
                dve.wait_ge(m_ga, r * 2)
                dve.wait_ge(m_st, r)
                for t in range(T):
                    at, w = posm[:, t, bass.ds(r, 1)], gate[:, t, bass.ds(r, 1)]
                    dve.tensor_scalar(sel[:, t, :], iota, at, None, ALU.is_equal)
                    q = dve.tensor_scalar(selg[:, t, :], iota, at, w, ALU.is_equal, ALU.mult)
                q.then_inc(m_sel, 1)

            def gathered(r):
                for half in range(2):
                    dve.wait_ge(m_ga, r * 2 + half + 1)
                    dve.wait_ge(m_xg, r * 2)
                    a = GAIN["ffn"] + KD + 4 * half
                    dve.tensor_tensor(xgp[:, 4 * half:4 * half + 4, :], bank(6 + half).rearrange("p (k n) -> p k n", k=4),
                                      of(gT[:, a:a + 4], P), ALU.mult).then_inc(m_xgp, 1)
                for half in range(2):
                    dve.wait_ge(m_xgh, r * 2 + half + 1)
                    at = (slice(None), slice(4 * half, 4 * half + 4), slice(None))
                    lower(xgl[at], xgp[at], xgh[at], m_xg)

            def hidden_lo(r, c):
                dve.wait_ge(m_hth, r * NFC + c + 1)
                lower(mhTl[:, c % 2, :], bank(2), mhTh[:, c % 2, :], m_ht)

            def expert(r):
                for j, (kind, c, half) in enumerate(FFN):
                    chunk_lo(dve, C_MOE + j + 2, r)
                    if (kind, half) == ("u", 0) and c:
                        hidden_lo(r, c - 1)
                    if (kind, half) == ("u", 1):
                        dve.wait_ge(m_silu, r * NFC + c + 1)
                        used(dve, C_MOE + j, r)
                        dve.wait_ge(m_t, r * NFC + max(c - 1, 0))
                        dve.tensor_tensor(mh[:, c % 2, :], msg, bank(1), ALU.mult).then_inc(m_h, 1)
                        if c == 1:
                            dve.wait_ge(m_st, r + 1)
                            dve.wait_ge(m_sc, r * 4)
                            dve.tensor_copy(selT.rearrange("p t n -> p (t n)"), bank(3, T * P)).then_inc(m_sT, 1)
                        if c == 3:
                            select(r + 1)
                    if (kind, c, half) == ("d", NFC - 2, 1):
                        hidden_lo(r, NFC - 1)
                gathered(r + 1)
                for half in range(2):
                    for t in range(T):
                        dve.wait_ge(m_sc, r * 4 + 2 * half + t + 1)
                        dve.wait_ge(m_acc, r * 4)
                        part = acc[:, t, half * BANK:(half + 1) * BANK]
                        dve.tensor_tensor(part, bank(3 - t), part, ALU.add).then_inc(m_acc, 1)

            def first_selection():
                for t in range(T):
                    dve.tensor_scalar(sel[:, t, :], iota, posm[:, t, 0:1], None, ALU.is_equal)
                    q = dve.tensor_scalar(selg[:, t, :], iota, posm[:, t, 0:1], gate[:, t, 0:1], ALU.is_equal, ALU.mult)
                q.then_inc(m_sel, 1)

            first_selection()
            gathered(0)
            with dve.Fori(0, NE) as e:
                expert(e)
            with dve.Fori(0, MAX_OVER) as j:
                with dve.If(over > j):
                    expert(j + NE)
            dve.wait_ge(m_acc, (over + NE) * 4)
            dve.sem_inc(y_ok, 2)
            post(4, lambda t: acc[:, t, :])
            pre(5)
            ple(1)
            post(5, lambda t: xn[:, t, :])

        @block.tensor
        def _(pe):
            def mm(out_, lhsT, rhs, start, stop):
                return pe.matmul(out_, lhsT, rhs, start=start, stop=stop)

            def pre(i):
                for t in range(T):
                    pe.wait_ge(xn_ok, 2 * i + t + 1)
                    for half in range(2):
                        for k in range(4):
                            a = (4 * half + k) * P
                            q = pe.transpose(ps[:, 2 * t + half, k * P:(k + 1) * P], xn[:, t, a:a + P], ident)
                        q.then_inc(xn_tr, 1)

            def mm3(out_, lhsT, rhs, start, stop):
                (lh, ll), (rh, rl) = lhsT, rhs
                pe.matmul(out_, lh, rl, start=start, stop=False, skip_group_check=True)
                pe.matmul(out_, lh, rh, start=False, stop=False, skip_group_check=True)
                return pe.matmul(out_, ll, rh, start=False, stop=stop, skip_group_check=True)

            def at(parts, *index):
                return tuple(x[(slice(None),) + index] for x in parts)

            def rows_by(n, tiles, width, banks, b0, lhs, first, last, done=None):
                w = chunk(pe, n, tiles, width)
                for t in range(T):
                    for j, (a, b) in enumerate(banks):
                        for k in range(tiles):
                            q = mm3(ps[:, b0 + len(banks) * t + j, 0:b - a], lhs(k, t), at(w, k, slice(a, b)),
                                    first and k == 0, last and k == tiles - 1)
                    if done is not None and t == 0:
                        q.then_inc(done, 1)
                q.then_inc(chunk_used, 1)

            xT = (xTh, xTl)
            HALVES = ((0, BANK), (BANK, D))

            def lhs_of(base):
                return lambda k, t: at(xT, base + k, slice(t * P, (t + 1) * P))

            def scores(u):
                b = u % 3
                if u >= 3:
                    pe.wait_ge(sc_exp, u - 2)
                if u < N_U0:
                    hh, o = u % 8, 64 * (u % 2)
                    for t in range(T):
                        cols = slice(t * P, (t + 1) * P)
                        if u < N_GQA:
                            l_, r_ = qT[o:o + 64, hh // 2, cols], kT[o:o + 64, hh // 4, :]
                        else:
                            l_, r_ = qmT[0:MQ, hh, cols], kmT[0:MQ, hh, :]
                        q = mm(ps[:, S_BANK[b], t * SEQ:(t + 1) * SEQ], l_, r_, True, True)
                else:
                    hh, t = divmod(u - N_U0, T)
                    o, own = 64 * (hh % 2), slice(t * P, (t + 1) * P)
                    for g in range(DG):
                        a, b_ = ((0, SEQ), (SEQ, SEQ + P), (SEQ + P, BANK))[g]
                        q = mm(ps[:, S_BANK[b], a:b_], dq[o:o + 64, g, hh // 2, own],
                               dk[o:o + 64, g, hh // 2, :] if g == 0 else dk[o:o + 64, g, hh // 2, own], True, True)
                q.then_inc(sc_mm, 1)

            def transposes(u):
                pe.wait_ge(pr_ok, u + 1)
                if u >= 2:
                    pe.wait_ge(prT_ok, u - 1)
                for a in range(4):
                    to = a if u >= N_U0 else 2 * (a % 2) + a // 2
                    q = pe.transpose(ps[:, T_BANK[u % 2], to * P:(to + 1) * P], probs(u)[:, a * P:(a + 1) * P], ident)
                q.then_inc(pr_tr, 1)

            def values(u):
                pe.wait_ge(prT_ok, u + 1)
                n = oT_before(u)
                if n >= 2:
                    pe.wait_ge(oT_ok, n - 1)
                if u < N_U0:
                    hh, o = u % 8, 64 * (u % 2)
                    for k in range(T):
                        v = zv[:, k, HD * (hh // 4):HD * (hh // 4 + 1)] if u < N_GQA else vm[:, k, hh, :]
                        q = mm(ps[o:o + 64, o_bank(u), 0:SEQ], v, prT_buf[:, k * SEQ:(k + 1) * SEQ], k == 0, k == T - 1)
                else:
                    hh, t = divmod(u - N_U0, T)
                    o = 64 * (hh % 2)
                    for j, (g, k) in enumerate(((0, 0), (0, 1), (1, t), (2, t))):
                        q = mm(ps[o:o + 64, o_bank(u), t * P:(t + 1) * P], dv[:, g, k, hh * HD:(hh + 1) * HD],
                               prT_buf[:, j * P:(j + 1) * P], j == 0, j == 3)
                q.then_inc(pv_mm, 1)

            def attention(first, n):
                for i in range(n + 3):
                    if i < n:
                        scores(first + i)
                    if i >= 3:
                        values(first + i - 3)
                    if 2 <= i < n + 2:
                        transposes(first + i - 2)

            def ple(l, n0, rounds=0):
                pe.wait_ge(p_in, 16 * (l + 1))
                for k in range(PK):
                    for t in range(T):
                        q = pe.transpose(ps[:, 4, k * SEQ + t * P:k * SEQ + (t + 1) * P], pe_rows[:, t, k * P:(k + 1) * P], ident)
                q.then_inc(p_tr, 1)
                pe.wait_ge(pT_ok, l + 1)
                pe.wait_ge(xT_ok, 4 * (3 * l + 2) + 4)
                w = chunk(pe, n0, PK, D, rounds)
                for t in range(T):
                    for j, (a, b) in enumerate(HALVES):
                        for k in range(PK):
                            q = mm3(ps[:, 2 * t + j, :], at((pTh, pTl), k, slice(t * P, (t + 1) * P)),
                                    at(w, k, slice(a, b)), k == 0, k == PK - 1)
                q.then_inc(chunk_used, 1)
                for i in range(4):
                    w = chunk(pe, n0 + 1 + i, 2, D, rounds)
                    for t in range(T):
                        for j, (a, b) in enumerate(HALVES):
                            for k in range(2):
                                q = mm3(ps[:, 4 + 2 * t + j, :], at(xT, 2 * i + k, slice(t * P, (t + 1) * P)),
                                        at(w, k, slice(a, b)), i == 0 and k == 0, i == 3 and k == 1)
                        if i == 3 and (l or t == 0):
                            q.then_inc(pl_mm, 1)
                    if i < 3 or l == 0:
                        q.then_inc(chunk_used, 1)

            pe.wait_ge(tab_in, 16)
            pe.wait_ge(gain_in, 16 * 5)
            pe.transpose(ps[:, 7, 0:51], small, tab[0:51, 0:51]).then_inc(gt_tr, 1)
            pre(0)
            pe.wait_ge(xT_ok, 4)
            for n in range(N_IN):
                rows_by(n, 1, ZW, Z_BANKS, 0, lhs_of(n), n == 0, n == N_IN - 1, z_mm if n == N_IN - 1 else None)
            for t in range(T):
                pe.wait_ge(z_ok, t + 1)
                for k in range(3):
                    q = pe.transpose(ps[:, 6 + t, k * P:(k + 1) * P], zl[:, t, k * P:(k + 1) * P], ident)
                q.then_inc(lat_tr, 1)
            pe.wait_ge(lat_ok, T)
            lat_parts = (latTh, latTl)
            rows_by(C_UQ, 2, MH * MQ, ((0, 384), (384, 768)), 0, lambda k, t: at(lat_parts, k, slice(t * P, (t + 1) * P)),
                    True, True, up_mm)
            rows_by(C_UKV, 1, MH * 2 * HD, HALVES, 4, lambda k, t: at(lat_parts, 2, slice(t * P, (t + 1) * P)),
                    True, True, up_mm)
            pe.wait_ge(qk_ok, 1)
            pe.wait_ge(up_ok, T)
            for t in range(T):
                for c in range(4):
                    q = pe.transpose(ps[:, t, c * P:(c + 1) * P], qr[:, t, c * P:(c + 1) * P], ident)
                q.then_inc(qk_tr, 1)
            for j in range(NKV):
                for t in range(T):
                    q = pe.transpose(ps[:, 2, (T * j + t) * P:(T * j + t + 1) * P], kr[:, t, j, :, :].rearrange("p u n -> p (u n)"), ident)
            q.then_inc(qk_tr, 1)
            pe.wait_ge(qkT_ok, 3)
            pe.wait_ge(up_ok, 2 * T)
            pe.wait_ge(mrow_ok, 1)
            for src, b0 in ((qm, 0), (km, 4)):
                for b in range(4):
                    for hh in (0, 1):
                        for t in range(T):
                            q = pe.transpose(ps[0:MQ, b0 + b, hh * SEQ + t * P:hh * SEQ + (t + 1) * P], src[:, t, 2 * b + hh, :], ident)
                    q.then_inc(m_tr, 1)
            pe.wait_ge(mqT_ok, 4)
            pe.wait_ge(mkT_ok, 4)
            attention(0, N_U0)
            pe.wait_ge(oT_ok, N_U0 // 2)
            for a in range(N_ABOUT):
                rows_by(C_ABOUT + a, 2, D, HALVES, 4, lhs_of(2 * a), a == 0, a == N_ABOUT - 1, y_ok if a == N_ABOUT - 1 else None)
            pre(1)
            pe.wait_ge(xT_ok, 4 * 1 + 4)
            for step, (kind, c, half) in enumerate(FFN):
                n = C_FFN + step
                if kind == "d":
                    if half == 0:
                        pe.wait_ge(f_h, 2 * c + 2)
                    rows_by(n, 2, D, HALVES, 4, lambda k, t: at((hTh, hTl), c % 2, 2 * half + k, slice(t * P, (t + 1) * P)),
                            c == 0 and half == 0, c == NFC - 1 and half == 1,
                            y_ok if c == NFC - 1 and half == 1 else None)
                    continue
                if half == 0 and c:
                    pe.wait_ge(f_silu if kind == "g" else fp_ok, 2 * c)
                w = chunk(pe, n, 4, FC)
                for f in range(FT):
                    for k in range(4):
                        q = mm3(ps[:, (0 if kind == "g" else 2) + f // 2, (f % 2) * SEQ:(f % 2 + 1) * SEQ],
                                at(w, k, slice(f * P, (f + 1) * P)), at(xT, 4 * half + k),
                                half == 0 and k == 0 and f % 2 == 0, half == 1 and k == 3)
                    if f == 1 and half:
                        q.then_inc(f_g if kind == "g" else f_u, 1)
                q.then_inc(chunk_used, 1)
            pre(2)
            ple(0, C_PLE0)
            pre(3)
            pe.wait_ge(xT_ok, 4 * 3 + 4)
            for c in range(9):
                g, kind = divmod(c, 3)
                for half in range(2):
                    n = C_QKV + 2 * c + half
                    w = chunk(pe, n, 4, FC)
                    for t in range(T):
                        if c >= 2 and half == 0:
                            pe.wait_ge(dz_ok, 2 * c - 3 + t)
                        for k in range(4):
                            q = mm3(ps[:, 2 * (c % 2) + t, :], at(xT, 4 * half + k, slice(t * P, (t + 1) * P)),
                                    at(w, k, slice(0, FC)), half == 0 and k == 0, half == 1 and k == 3)
                        if t == 0 and half:
                            q.then_inc(dz_mm, 1)
                    q.then_inc(chunk_used, 1)
                if c and (c - 1) % 3 < 2:
                    qi = 2 * ((c - 1) // 3) + (c - 1) % 3
                    pe.wait_ge(dr_ok, qi + 1)
                    for t in range(T):
                        if qi >= 2:
                            pe.wait_ge(dT_ok, 2 * qi - 3 + t)
                        for k in range(4):
                            a = (qi % 2) * 512 + k * P
                            q = pe.transpose(ps[:, 4 + 2 * (qi % 2) + t, k * P:(k + 1) * P], xn[:, t, a:a + P], ident)
                        q.then_inc(d_tr, 1)
            pe.wait_ge(dz_ok, 18)
            pe.wait_ge(dT_ok, 12)
            attention(N_U0, T * DH)
            pe.wait_ge(oT_ok, N_U0 // 2 + DH // 2)
            for a in range(N_DOUT):
                rows_by(C_DOUT + a, 2, D, HALVES, 4, lhs_of(2 * a), a == 0, a == N_DOUT - 1, y_ok if a == N_DOUT - 1 else None)
            pre(4)
            pe.wait_ge(xT_ok, 4 * 4 + 4)
            pe.wait_ge(wr_in, 16)
            for t in range(T):
                for k in range(KD):
                    q = mm(ps[:, 4, t * NE:(t + 1) * NE], xr[:, k, t * P:(t + 1) * P], wr[:, k, :], k == 0, k == KD - 1)
            q.then_inc(r_mm, 1)
            pe.wait_ge(r_mask, 1)
            pe.wait_ge(moetab_in, 16)
            chose = [rt[:, 6, t * NE:(t + 1) * NE] for t in range(T)]
            mm(ps[:, 5, 0:NE], tri, chose[0], True, True)
            mm(ps[:, 5, NE:2 * NE], ones, chose[0], True, False)
            mm(ps[:, 5, NE:2 * NE], tri, chose[1], False, True)
            mm(ps[:, 5, 2 * NE:3 * NE], ones, chose[0], True, False)
            mm(ps[:, 5, 2 * NE:3 * NE], ones, chose[1], False, True).then_inc(r_pos, 1)
            pe.wait_ge(r_cnt, 2)
            over = pe.value_load(noveri[0:1, 0:1], min_val=0, max_val=MAX_OVER)

            def gather(r):
                pe.wait_ge(m_sel, r + 1)
                pe.wait_ge(m_xgp, r * 2)
                for half in range(2):
                    for k in range(4):
                        a = (4 * half + k) * P
                        for t in range(T):
                            q = mm(ps[:, 6 + half, k * P:(k + 1) * P], xn[:, t, a:a + P], sel[:, t, :], t == 0, t == T - 1)
                    q.then_inc(m_ga, 1)

            def hidden_T(r, c):
                pe.wait_ge(m_h, r * NFC + c + 1)
                pe.wait_ge(m_ht, r * NFC + c)
                if c == 0:
                    pe.wait_ge(m_acc, r * 4)
                for k in range(FT):
                    q = pe.transpose(ps[:, 2, k * P:(k + 1) * P], mh[:, c % 2, k * P:(k + 1) * P], ident)
                q.then_inc(m_t, 1)

            def expert(r):
                for j, (kind, c, half) in enumerate(FFN):
                    n = C_MOE + j
                    if (kind, half) == ("u", 0) and c:
                        hidden_T(r, c - 1)
                    if (kind, c, half) == ("d", NFC - 2, 1):
                        hidden_T(r, NFC - 1)
                    if kind == "d":
                        w = chunk(pe, n, 2, D, r)
                        if half == 0:
                            pe.wait_ge(m_ht, r * NFC + c + 1)
                        if c == 0 and half == 0:
                            pe.wait_ge(m_ysb, r * 2)
                        for j2, (a, b) in enumerate(HALVES):
                            for k in range(2):
                                q = mm3(ps[:, 4 + j2, :], at((mhTh, mhTl), c % 2, slice((2 * half + k) * P, (2 * half + k + 1) * P)),
                                        at(w, k, slice(a, b)), c == 0 and half == 0 and k == 0,
                                        c == NFC - 1 and half == 1 and k == 1)
                            if c == NFC - 1 and half == 1 and j2 == 0:
                                q.then_inc(m_y, 1)
                    else:
                        w = chunk(pe, n, 4, FC, r)
                        if half == 0:
                            if (kind, c) == ("g", 0):
                                pe.wait_ge(m_xg, r * 2 + 2)
                            pe.wait_ge(m_silu if kind == "g" else m_h, r * NFC + c)
                        for k in range(4):
                            q = mm3(bank(0 if kind == "g" else 1), at((xgh, xgl), 4 * half + k), at(w, k, slice(0, FC)),
                                    half == 0 and k == 0, half == 1 and k == 3)
                    q.then_inc(chunk_used, 1)
                    if (kind, c, half) == ("g", 1, 1):
                        pe.wait_ge(m_sT, r)
                        pe.wait_ge(m_acc, r * 4)
                        for t in range(T):
                            q = pe.transpose(ps[:, 3, t * P:(t + 1) * P], selg[:, t, :], ident)
                        q.then_inc(m_st, 1)
                gather(r + 1)
                pe.wait_ge(m_sT, r + 1)
                pe.wait_ge(m_ht, r * NFC + NFC)
                for half in range(2):
                    pe.wait_ge(m_ysb, r * 2 + half + 1)
                    for t in range(T):
                        if half:
                            pe.wait_ge(m_acc, r * 4 + t + 1)
                        mm(bank(3 - t), selT[:, t, :], ysb[:, half * BANK:(half + 1) * BANK], True, True).then_inc(m_sc, 1)

            gather(0)
            with pe.Fori(0, NE) as e:
                expert(e)
            with pe.Fori(0, MAX_OVER) as j:
                with pe.If(over > j):
                    expert(j + NE)
            pre(5)
            ple(1, C_MOE, over + NE)


def tables_of_shapes():
    f = np.float32
    tok = np.arange(SEQ).reshape(P, T)

    def angles(pos, dim, theta):
        inv = np.power(f(theta), -(np.arange(0, dim, 2, dtype=f) / f(dim)))
        a = pos.astype(f)[..., None] * inv
        return np.cos(a).astype(f), np.sin(a).astype(f)

    out = np.zeros((P, TAB_ALL), f)

    def put(at, v):
        v = np.asarray(v, f).reshape(P, -1)
        out[:, at:at + v.shape[1]] = v

    put(TAB["ident"][0], np.eye(P))
    cr, sr = angles(tok // 64, 32, 10000.0)
    cc, sc = angles(tok % 64, 32, 10000.0)
    put(TAB["axC"][0], np.concatenate([cr, cr, cc, cc], -1))
    put(TAB["axS"][0], np.concatenate([-sr, sr, -sc, sc], -1))
    for name, dim, theta in (("ml", MR, 10000.0), ("di", 16, 500000.0)):
        c, s = angles(tok, dim, theta)
        put(TAB[name + "C"][0], np.concatenate([c, c], -1))
        put(TAB[name + "S"][0], np.concatenate([-s, s], -1))
    put(TAB["rev"][0], np.tile(NE - np.arange(NE), (P, T)))
    i = np.arange(P)
    put(TAB_MOE, i[:, None] < i[None, :])
    put(TAB_MOE + P, np.ones((P, P)))
    put(TAB_MOE + 2 * P, np.tile(np.arange(P), (P, 1)))
    for t in range(T):
        q = tok[:, t][:, None]
        keys = [np.abs(q - tok[:, k][None]) <= 64 for k in range(T)]
        keys += [(q - tok[:, t][None]) % dil == 0 for dil in (4, 16)]
        put(TAB_MASK + t * BANK, np.where(np.concatenate(keys, 1), 0.0, NEG))
    return out


INS = ["x", "p", "mix_pre_g", "mix_post_g", "ffn_pre_g", "ffn_post_g", "ple_w_proj", "ple_gate_norm_g",
       "ple_w_gate", "ple_post_g", "ab_w_in", "gqa_q_norm_g", "gqa_k_norm_g", "mla_q_norm_g", "mla_w_uq",
       "mla_kv_norm_g", "mla_w_ukv", "ab_w_out", "ffn_w_gate", "ffn_w_up", "ffn_w_down", "dil_w_qkv",
       "dil_w_out", "moe_w_router", "moe_w_gate", "moe_w_up", "moe_w_down"]


def kernel(**inputs):
    import concourse.bacc as bacc
    from concourse.bass_utils import run_bass_kernel_spmd

    nc = bacc.Bacc("TRN2", target_bir_lowering=False, num_devices=1)
    arrays, args = {}, []
    for name in INS:
        arrays["in_" + name] = np.ascontiguousarray(inputs[name])
    arrays["in_tables"] = tables_of_shapes()
    for name, a in arrays.items():
        args.append(nc.dram_tensor(name, a.shape, mybir.dt.from_np(a.dtype), kind="ExternalInput").ap())
    args.append(nc.dram_tensor("out_h", (1, SEQ, D), F32, kind="ExternalOutput").ap())
    hybrid_encoder(nc, *args)
    r = run_bass_kernel_spmd(nc, [arrays], core_ids=[0])
    return r.results[0]["out_h"]
```

```python
from contextlib import ExitStack

import numpy as np

import concourse.bass as bass
from concourse import mybir

P = 128
F32 = mybir.dt.float32
F32R = mybir.dt.float32r
I32 = mybir.dt.int32
ACT = mybir.ActivationFunctionType
ALU = mybir.AluOpType
AX_X = mybir.AxisListType.X

SEQ, D = 256, 1024
T = SEQ // P
KD = D // P
EPS = 1e-6
NEG = -1e30
HD = 64
NQ, NKV = 8, 2
ZQ, ZK, ZV, ZCQ, ZCKV, ZKR, ZW = 0, 512, 640, 768, 1024, 1152, 1184
MH, MN, MR = 8, 64, 32
MQ = MN + MR
GQA_SCALE = HD ** -0.5
MLA_SCALE = MQ ** -0.5
FF = 3584
FC = 512
NFC = FF // FC
FT = FC // P
DH, DG = 8, 3
PD, PK = 256, 2
NE = 8
BANK = 512

SLOT, RAW, SPLIT = 2048, 6, 3
C_IN, N_IN = 0, KD
C_UQ = C_IN + N_IN
C_UKV = C_UQ + 1
C_ABOUT, N_ABOUT = C_UKV + 1, 4
C_FFN, N_FFN = C_ABOUT + N_ABOUT, 6 * NFC
C_PLE0, N_PLE = C_FFN + N_FFN, 5
C_QKV, N_QKV = C_PLE0 + N_PLE, 18
C_DOUT, N_DOUT = C_QKV + N_QKV, 2
C_MOE = C_DOUT + N_DOUT
assert N_FFN % RAW == 0 and N_FFN % SPLIT == 0
Z_BANKS = ((0, 384), (384, 768), (768, ZW))
JOBS = NE + 1


def ffn_order():
    order = [("g", 0), ("u", 0)]
    for c in range(1, NFC):
        order += [("g", c), ("u", c), ("d", c - 1)]
    order.append(("d", NFC - 1))
    return [(kind, c, half) for kind, c in order for half in range(2)]


FFN = ffn_order()
FFN_AT = {key: n for n, key in enumerate(FFN)}

TAB = {}
_w = 0
for _n, _c in (("ident", P), ("axC", T * HD), ("axS", T * HD), ("mlC", T * MR), ("mlS", T * MR),
               ("diC", T * 16), ("diS", T * 16), ("rev", T * NE)):
    TAB[_n] = (_w, _c)
    _w += _c
TAB_RES = _w
TAB_MOE = _w
TAB_MASK = TAB_MOE + 3 * P
TAB_ALL = TAB_MASK + T * BANK


def hybrid_encoder(nc, x, p, mix_pre_g, mix_post_g, ffn_pre_g, ffn_post_g, ple_w_proj, ple_gate_norm_g,
                   ple_w_gate, ple_post_g, ab_w_in, gqa_q_norm_g, gqa_k_norm_g, mla_q_norm_g, mla_w_uq,
                   mla_kv_norm_g, mla_w_ukv, ab_w_out, ffn_w_gate, ffn_w_up, ffn_w_down, dil_w_qkv,
                   dil_w_out, moe_w_router, moe_w_gate, moe_w_up, moe_w_down, tables, out):
    ctx = ExitStack()
    with ctx:
        def sb(name, shape, dt=F32):
            return ctx.enter_context(nc.sbuf_tensor(name, shape, dt))

        def sem(name):
            return ctx.enter_context(nc.semaphore(name))

        ps = ctx.enter_context(nc.psum_tensor("ps", [P, 8, BANK], F32))

        raw = sb("raw", [P, RAW, SLOT])
        whi = sb("whi", [P, SPLIT, SLOT], F32R)
        wlo = sb("wlo", [P, SPLIT, SLOT], F32R)
        h = sb("h", [P, T, D])
        xn = sb("xn", [P, T, D])
        xTh = sb("xTh", [P, KD, SEQ], F32R)
        xTl = sb("xTl", [P, KD, SEQ], F32R)
        gb = sb("gb", [P, 3, D])
        tab = sb("tab", [P, TAB_RES])
        gT = sb("gT", [P, 51])
        wr = sb("wr", [P, KD, NE])
        eps = sb("eps", [P, 1])
        ss = sb("ss", [P, T])
        pss = sb("pss", [P, T])
        rstd = sb("rstd", [P, T])
        prstd = sb("prstd", [P, T])
        hss = sb("hss", [P, T, 12])
        hrs = sb("hrs", [P, T, 12])
        smax = sb("smax", [P, 3, T])
        snm = sb("snm", [P, 3, T])
        ssum = sb("ssum", [P, 3, T])
        srec = sb("srec", [P, 3, T])
        rt = sb("rt", [P, 10, T * NE])
        rs = sb("rs", [P, 8, T])
        posm = sb("posm", [P, T, JOBS])
        gate = sb("gate", [P, T, JOBS])
        full = sb("full", [P, NE])
        fulli = sb("fulli", [P, NE], I32)
        ARENA, FR_ARENA = 10752, 4096
        arena = sb("arena", [P, ARENA])
        fr_arena = sb("fr_arena", [P, FR_ARENA], F32R)

        taken = [0, 0]

        def carve(n, reset=None, fr=0):
            if reset is not None:
                taken[fr] = reset
            a = taken[fr]
            taken[fr] += n
            assert taken[fr] <= (ARENA, FR_ARENA)[fr]
            return (arena, fr_arena)[fr][:, a:a + n]

        def table(name, *dims):
            a, n = TAB[name]
            return tab[:, a:a + n]

        ident = table("ident")

        xf = xn[:, :, :].rearrange("p t n -> p (t n)")
        xprod = carve(4 * BANK, 0).rearrange("p (q n) -> p q n", q=4)
        small = arena[0:51, 4096:4096 + P]
        zqk = carve(T * ZV, 0).rearrange("p (t n) -> p t n", t=T)
        zl = carve(T * (ZW - ZCQ)).rearrange("p (t n) -> p t n", t=T)
        zv = carve(T * NKV * HD).rearrange("p (t n) -> p t n", t=T)
        rows = carve(MH * MQ * T)
        qr = rows[:, 0:T * 512].rearrange("p (t n) -> p t n", t=T)
        kr = rows[:, T * 512:T * 768].rearrange("p (t j u n) -> p t j u n", t=T, j=NKV, u=2)
        km = rows.rearrange("p (t h n) -> p t h n", t=T, h=MH)
        qT = carve(4 * SEQ).rearrange("p (c n) -> p c n", c=4)
        kT = carve(NKV * SEQ).rearrange("p (c n) -> p c n", c=NKV)
        vm = carve(T * MH * HD).rearrange("p (t h n) -> p t h n", t=T, h=MH)
        qmT = carve(MH * SEQ).rearrange("p (h n) -> p h n", h=MH)
        probs0 = carve(3 * BANK).rearrange("p (b n) -> p b n", b=3)
        rot = carve(4 * T * HD).rearrange("p (i t n) -> p i t n", i=4, t=T)
        grow = carve(2 * HD).rearrange("p (i n) -> p i n", i=2)
        kmT = arena[:, 0:MH * SEQ].rearrange("p (h n) -> p h n", h=MH)
        assert MH * SEQ <= T * (ZV + ZW - ZCQ)
        lat = qmT[:, 0:3, :]
        latTh = carve(3 * SEQ, 0, 1).rearrange("p (k n) -> p k n", k=3)
        latTl = carve(3 * SEQ, None, 1).rearrange("p (k n) -> p k n", k=3)
        qm = xf[:, 0:T * MH * MQ].rearrange("p (t h n) -> p t h n", t=T, h=MH)
        mtmp = xf[:, T * MH * MQ:T * D]
        prT_buf = mtmp
        dq = carve(DG * 4 * SEQ, 0).rearrange("p (g c n) -> p g c n", g=DG, c=4)
        dk = carve(DG * 4 * SEQ).rearrange("p (g c n) -> p g c n", g=DG, c=4)
        dv = carve(DG * T * 512).rearrange("p (g t n) -> p g t n", g=DG, t=T)
        probs1 = carve(3 * BANK).rearrange("p (b n) -> p b n", b=3)
        dtmp = probs1
        mask = xn[:, :, 0:BANK]
        sg = carve(FT * SEQ, 0).rearrange("p (f n) -> p f n", f=FT)
        hp = carve(FT * SEQ).rearrange("p (f n) -> p f n", f=FT)
        hTh = carve(2 * FT * SEQ, 0, 1).rearrange("p (b f n) -> p b f n", b=2, f=FT)
        hTl = carve(2 * FT * SEQ, None, 1).rearrange("p (b f n) -> p b f n", b=2, f=FT)
        xgp = carve(KD * P, 0).rearrange("p (k n) -> p k n", k=KD)
        msg = carve(BANK)
        mh = carve(2 * BANK).rearrange("p (b n) -> p b n", b=2)
        ysb = carve(D)
        acc = carve(T * D).rearrange("p (t n) -> p t n", t=T)
        sel = carve(T * P).rearrange("p (t n) -> p t n", t=T)
        selg = carve(T * P).rearrange("p (t n) -> p t n", t=T)
        selT = carve(T * P).rearrange("p (t n) -> p t n", t=T)
        moetab = carve(3 * P)
        tri, ones, iota = (moetab[:, i * P:(i + 1) * P] for i in range(3))
        xr = carve(KD * SEQ).rearrange("p (k n) -> p k n", k=KD)
        xgh = carve(KD * P, 0, 1).rearrange("p (k n) -> p k n", k=KD)
        xgl = carve(KD * P, None, 1).rearrange("p (k n) -> p k n", k=KD)
        mhTh = carve(2 * BANK, None, 1).rearrange("p (b n) -> p b n", b=2)
        mhTl = carve(2 * BANK, None, 1).rearrange("p (b n) -> p b n", b=2)
        pe_rows = carve(T * PD, ARENA - T * PD).rearrange("p (t n) -> p t n", t=T)
        pTh = carve(PK * SEQ, FT * SEQ, 1).rearrange("p (k n) -> p k n", k=PK)
        pTl = carve(PK * SEQ, None, 1).rearrange("p (k n) -> p k n", k=PK)

        tab_in = sem("tab_in")
        gain_in = sem("gain_in")
        more_gain_in = sem("more_gain_in")
        grow_in = sem("grow_in")
        wr_in = sem("wr_in")
        x_in = [sem(f"x_in{t}") for t in range(T)]
        gb_in = [sem(f"gb_in{i}") for i in range(3)]
        mask_in = sem("mask_in")
        moetab_in = sem("moetab_in")
        p_in = sem("p_in")
        slot_in = [sem(f"slot_in{i}") for i in range(RAW)]
        whi_ok = sem("whi_ok")
        split_ok = sem("split_ok")
        chunk_used = sem("chunk_used")
        acc_zero = sem("acc_zero")
        out_done = sem("out_done")
        dve_step = sem("dve_step")
        act_step = sem("act_step")
        eps_ok = sem("eps_ok")
        gains_tr = sem("gains_tr")
        rstd_ok = sem("rstd_ok")
        xn_ok = sem("xn_ok")
        xn_tr = sem("xn_tr")
        xp_ok = sem("xp_ok")
        xh_ok = sem("xh_ok")
        xT_ok = sem("xT_ok")
        y_ok = sem("y_ok")
        ysq_ok = sem("ysq_ok")
        prstd_ok = sem("prstd_ok")
        h_ok = sem("h_ok")
        z_mm = sem("z_mm")
        z_ok = sem("z_ok")
        zl_ok = sem("zl_ok")
        lat_tr = sem("lat_tr")
        lat_gained = sem("lat_gained")
        lat_hi = sem("lat_hi")
        lat_split = sem("lat_split")
        hss_ok = sem("hss_ok")
        hrs_ok = sem("hrs_ok")
        up_mm = sem("up_mm")
        up_ok = sem("up_ok")
        qk_ok = sem("qk_ok")
        qk_tr = sem("qk_tr")
        qkT_ok = sem("qkT_ok")
        mrow_ok = sem("mrow_ok")
        mla_tr = sem("mla_tr")
        mqT_ok = sem("mqT_ok")
        mkT_ok = sem("mkT_ok")
        sc_mm = sem("sc_mm")
        sc_max = sem("sc_max")
        sc_exp = sem("sc_exp")
        pr_ok = sem("pr_ok")
        pr_tr = sem("pr_tr")
        prT_ok = sem("prT_ok")
        pv_mm = sem("pv_mm")
        oT_hi = sem("oT_hi")
        oT_ok = sem("oT_ok")
        ffn_gate_mm = sem("ffn_gate_mm")
        ffn_silu = sem("ffn_silu")
        ffn_up_mm = sem("ffn_up_mm")
        ffn_hidden = sem("ffn_hidden")
        ffn_hidden_hi = sem("ffn_hidden_hi")
        ffn_hidden_split = sem("ffn_hidden_split")
        emb_tr = sem("emb_tr")
        emb_hi = sem("emb_hi")
        emb_split = sem("emb_split")
        emb_gate_mm = sem("emb_gate_mm")
        emb_gate = sem("emb_gate")
        dil_mm = sem("dil_mm")
        dil_rows_ok = sem("dil_rows_ok")
        dil_rotated = sem("dil_rotated")
        dil_tr = sem("dil_tr")
        dil_T_ok = sem("dil_T_ok")
        logits_mm = sem("logits_mm")
        chosen_ok = sem("chosen_ok")
        gap_ok = sem("gap_ok")
        gap_exp = sem("gap_exp")
        places_mm = sem("places_mm")
        full_ok = sem("full_ok")
        moe_sel_ok = sem("moe_sel_ok")
        moe_gather_mm = sem("moe_gather_mm")
        moe_rows_ok = sem("moe_rows_ok")
        moe_rows_hi = sem("moe_rows_hi")
        moe_rows_split = sem("moe_rows_split")
        moe_selT_tr = sem("moe_selT_tr")
        moe_selT_ok = sem("moe_selT_ok")
        moe_silu = sem("moe_silu")
        moe_hidden = sem("moe_hidden")
        moe_hidden_tr = sem("moe_hidden_tr")
        moe_hidden_hi = sem("moe_hidden_hi")
        moe_hidden_split = sem("moe_hidden_split")
        moe_y_mm = sem("moe_y_mm")
        moe_y_ok = sem("moe_y_ok")
        moe_scatter_mm = sem("moe_scatter_mm")
        moe_added = sem("moe_added")

        def kt_rows(w):
            return w.rearrange("(k p) n -> p k n", p=P)

        chunks = []
        for a in range(N_IN):
            chunks.append((kt_rows(ab_w_in[0])[:, a:a + 1, :], 1, ZW))
        chunks.append((kt_rows(mla_w_uq[0]), 2, MH * MQ))
        chunks.append((kt_rows(mla_w_ukv[0]), 1, MH * 2 * HD))
        for a in range(N_ABOUT):
            chunks.append((kt_rows(ab_w_out[0])[:, 2 * a:2 * a + 2, :], 2, D))

        def ffn_source(kind, c, half, wg, wu, wd):
            if kind == "d":
                a = FT * c + 2 * half
                return wd[:, a:a + 2, :], 2, D
            return (wg if kind == "g" else wu)[:, 4 * half:4 * half + 4, FC * c:FC * (c + 1)], 4, FC

        dense = [kt_rows(w[0]) for w in (ffn_w_gate, ffn_w_up, ffn_w_down)]
        for kind, c, half in FFN:
            chunks.append(ffn_source(kind, c, half, *dense))

        def ple_source(l):
            return [(kt_rows(ple_w_proj[l]), PK, D)] + [(kt_rows(ple_w_gate[l])[:, 2 * a:2 * a + 2, :], 2, D) for a in range(4)]

        chunks += ple_source(0)
        for c in range(9):
            for half in range(2):
                chunks.append((kt_rows(dil_w_qkv[0])[:, 4 * half:4 * half + 4, FC * c:FC * (c + 1)], 4, FC))
        for a in range(N_DOUT):
            chunks.append((kt_rows(dil_w_out[0])[:, 2 * a:2 * a + 2, :], 2, D))
        assert len(chunks) == C_MOE


        def load(eng, n, source, tiles, width, rounds=0):
            if n >= RAW:
                eng.wait_ge(split_ok, n - RAW + 1 + N_FFN * rounds)
            dst = raw[:, n % RAW, 0:tiles * width].rearrange("p (k n) -> p k n", k=tiles)
            eng.dma_start(dst, source).then_inc(slot_in[n % RAW], 16)

        def width_of(n):
            return chunks[n][1] * chunks[n][2] if n < C_MOE else SLOT

        def chunk_hi(act, n, rounds=0):
            act.wait_ge(slot_in[n % RAW], 16 * (n // RAW + 1) + 16 * (N_FFN // RAW) * rounds)
            if n >= SPLIT:
                act.wait_ge(chunk_used, n - SPLIT + 1 + N_FFN * rounds)
            w = width_of(n)
            act.activation(whi[:, n % SPLIT, 0:w], raw[:, n % RAW, 0:w], ACT.Copy).then_inc(whi_ok, 1)

        def chunk_lo(dve, n, rounds=0):
            dve.wait_ge(whi_ok, n + 1 + N_FFN * rounds)
            w = width_of(n)
            dve.tensor_tensor(wlo[:, n % SPLIT, 0:w], raw[:, n % RAW, 0:w], whi[:, n % SPLIT, 0:w].bitcast(F32),
                              ALU.subtract).then_inc(split_ok, 1)

        def chunk(pe, n, tiles, width, rounds=0):
            pe.wait_ge(split_ok, n + 1 + N_FFN * rounds)
            return [w[:, n % SPLIT, 0:tiles * width].rearrange("p (k n) -> p k n", k=tiles) for w in (whi, wlo)]

        class Ahead:

            def __init__(self, split, eng):
                self.split, self.eng, self.next = split, eng, 0

            def __call__(self, n):
                while self.next <= n:
                    self.split(self.eng, self.next)
                    self.next += 1

        def used(eng, n, rounds=0):
            eng.wait_ge(chunk_used, n + 1 + N_FFN * rounds)

        Y_BEFORE = [0, 1, 2, 4, 5, 7]
        Y_CHUNK = {0: C_FFN - 1, 1: C_PLE0 - 1, 3: C_MOE - 1}

        def product(i, q):
            t, half = divmod(q, 2)
            if i == 4:
                return xr[:, 4 * half:4 * half + 4, t * P:(t + 1) * P]
            return xprod[:, q, :].rearrange("p (k n) -> p k n", k=4)

        def output_ready(eng, j, t):
            if j in Y_CHUNK and t:
                used(eng, Y_CHUNK[j])
            else:
                eng.wait_ge(y_ok, Y_BEFORE[j] + t + 1)

        def first_or_used(eng, s, count, n, second, rounds=0):
            if second:
                used(eng, n, rounds)
            else:
                eng.wait_ge(s, count)

        def gates_ready(eng, l, t):
            if l == 0 and t:
                used(eng, C_QKV - 1)
            else:
                eng.wait_ge(emb_gate_mm, 2 * l - (1 if l else 0) + t + 1)

        def hidden_used(eng, r, c):
            used(eng, C_MOE - 1 if c < 2 else C_MOE + FFN_AT["d", c - 2, 1], r)

        def of(x, n):
            return x.unsqueeze(2).to_broadcast([P, x.shape[1], n])

        def bank(b, n=BANK):
            return ps[:, b, 0:n]

        def pair(b):
            return ps[:, b:b + 2, :].rearrange("p b n -> p (b n)")

        GAIN = {"mix": 0, "ffn": 16, "ple": 32, "mla": 48}
        PRE_BANK = (4, 4, 4, 4, 0, 4)
        PRE = [("mix", 0), ("ffn", 0), ("ple", 0), ("mix", 1), ("ffn", 1), ("ple", 1)]
        N_GQA, N_U0 = NQ, NQ + MH
        SCATTER_BANK = (3, 5)
        S_BANK, T_BANK = (0, 1, 6), (2, 3)

        def probs(u):
            return (probs0 if u < N_U0 else probs1)[:, u % 3, :]

        def oT_before(u):
            return u // 2 if u < N_U0 else N_U0 // 2 + (u - N_U0) // 4

        def o_bank(u):
            return 4 + oT_before(u) % 2

        block = ctx.enter_context(nc.Block())

        @block.sync
        def _(sp):
            for t in range(T):
                sp.dma_start(h[:, t, :], x.rearrange("b (p t) d -> p t (b d)", t=T)[:, t, :]).then_inc(x_in[t], 16)
                if t == 0:
                    sp.dma_start(tab[:, :], tables[:, 0:TAB_RES]).then_inc(tab_in, 16)
            for n, (source, tiles, width) in enumerate(chunks):
                load(sp, n, source, tiles, width)

            experts_w = [w.rearrange("a e (k p) n -> (a e) p k n", p=P) for w in (moe_w_gate, moe_w_up, moe_w_down)]

            def expert_loads(e, r):
                for j, (kind, c, half) in enumerate(FFN):
                    source = ffn_source(kind, c, half, *[w[e] for w in experts_w])
                    load(sp, C_MOE + j, *source, r)

            with sp.Fori(0, NE) as e:
                expert_loads(e, e)
            for i, source in enumerate(ple_source(1)):
                load(sp, C_MOE + i, *source, NE)
            for t in range(T):
                sp.wait_ge(h_ok, 2 * 5 + t + 1)
                sp.dma_start(out.rearrange("b (p t) d -> p t (b d)", t=T)[:, t, :], h[:, t, :]).then_inc(out_done, 16)
            sp.wait_ge(out_done, 16 * T)

        @block.gpsimd
        def _(pool):
            def rows_of(vec, n):
                return vec.to_broadcast([P, n])

            pool.dma_start(small[32:48, :], ple_gate_norm_g.rearrange("i (k n) -> (i k) n", n=P)).then_inc(more_gain_in, 16)
            pool.dma_start(small[48:50, :], mla_q_norm_g.rearrange("i (k n) -> (i k) n", n=P)).then_inc(more_gain_in, 16)
            pool.dma_start(small[50:51, :], mla_kv_norm_g).then_inc(more_gain_in, 16)
            pool.dma_start(grow[:, 0, :], rows_of(gqa_q_norm_g, HD)).then_inc(grow_in, 16)
            pool.dma_start(grow[:, 1, :], rows_of(gqa_k_norm_g, HD)).then_inc(grow_in, 16)
            pool.wait_ge(z_mm, 1)
            for n, g in enumerate((mix_post_g, ffn_post_g, ple_post_g)):
                pool.dma_start(gb[:, n, :], rows_of(g[0:1, :], D)).then_inc(gb_in[n], 16)
            pool.dma_start(wr[:, :, :], kt_rows(moe_w_router[0])).then_inc(wr_in, 16)
            pool.wait_ge(oT_ok, N_U0 // 2)
            pool.dma_start(pe_rows, p[0, 0].rearrange("(p t) n -> p t n", t=T)).then_inc(p_in, 16)
            pool.wait_ge(h_ok, 2 * 3)
            for n, g in enumerate((mix_post_g, ffn_post_g, ple_post_g)):
                pool.dma_start(gb[:, n, :], rows_of(g[1:2, :], D)).then_inc(gb_in[n], 16)
            pool.wait_ge(dil_tr, 10)
            pool.dma_start(mask, tables[:, TAB_MASK:TAB_ALL].rearrange("p (t n) -> p t n", t=T)).then_inc(mask_in, 16)
            pool.wait_ge(oT_ok, N_U0 // 2 + DH // 2)
            pool.dma_start(moetab, tables[:, TAB_MOE:TAB_MASK]).then_inc(moetab_in, 16)
            pool.dma_start(pe_rows, p[1, 0].rearrange("(p t) n -> p t n", t=T)).then_inc(p_in, 16)
            pool.memset(acc, 0.0).then_inc(acc_zero, 1)

        @block.scalar
        def _(act):
            def copy(out, in_, scale=1.0):
                return act.activation(out, in_, ACT.Copy, scale=scale)

            steps = [0]

            def link(ins):
                steps[0] += 1
                ins.then_inc(act_step, 1)
                act.wait_ge(act_step, steps[0])

            def mean_square(scratch, rows, mean):
                return act.activation(scratch, rows, ACT.Square, scale=rows.shape[-1] ** -0.5, accum_out=mean)

            def inverse_root(out, mean, ok):
                link(act.activation(out, mean, ACT.Ln, bias=eps[:, 0:1]))
                act.activation(out, out, ACT.Exp, scale=-0.5).then_inc(ok, 1)

            ahead = Ahead(chunk_hi, act)

            def upper(out, in_, ok):
                copy(out, in_).then_inc(ok, 1)

            def pre(i):
                for t in range(T):
                    if i == 0:
                        act.wait_ge(x_in[t], 16)
                    else:
                        act.wait_ge(h_ok, 2 * (i - 1) + t + 1)
                    link(mean_square(xn[:, t, :], h[:, t, :], ss[:, t:t + 1]))
                    inverse_root(rstd[:, t:t + 1], ss[:, t:t + 1], rstd_ok)
                for q in range(4):
                    t, half = divmod(q, 2)
                    act.wait_ge(xp_ok, 4 * i + q + 1)
                    at = (slice(None), slice(4 * half, 4 * half + 4), slice(t * P, (t + 1) * P))
                    upper(xTh[at], product(i, q), xh_ok)

            def post(j, y):
                for t in range(T):
                    output_ready(act, j, t)
                    mean_square(arena[:, t * D:(t + 1) * D], y(t), pss[:, t:t + 1]).then_inc(ysq_ok, 1)
                    act.wait_ge(ysq_ok, 2 * j + t + 1)
                    inverse_root(prstd[:, t:t + 1], pss[:, t:t + 1], prstd_ok)

            def exps(u):
                act.wait_ge(sc_max, u + 1)
                if u < N_U0:
                    if u >= 3:
                        act.wait_ge(pr_tr, u - 2)
                    s = GQA_SCALE if u < N_GQA else MLA_SCALE
                    for t in range(T):
                        last = act.activation(probs(u)[:, t * SEQ:(t + 1) * SEQ],
                                              ps[:, S_BANK[u % 3], t * SEQ:(t + 1) * SEQ], ACT.Exp,
                                              bias=snm[:, u % 3, t:t + 1], scale=s, accum_out=ssum[:, u % 3, t:t + 1])
                else:
                    last = act.activation(probs(u), probs(u), ACT.Exp, bias=snm[:, u % 3, 0:1],
                                          accum_out=ssum[:, u % 3, 0:1])
                last.then_inc(sc_exp, 1)

            def prT(u):
                act.wait_ge(pr_tr, u + 1)
                act.wait_ge(pv_mm, u)
                copy(prT_buf, bank(T_BANK[u % 2])).then_inc(prT_ok, 1)

            def attention(first, n, per):
                for i in range(n + 4):
                    if 3 <= i < n + 3:
                        prT(first + i - 3)
                    if i < n:
                        exps(first + i)
                    if i >= 4 and (i - 4) % per == per - 1:
                        u = first + i - 4
                        act.wait_ge(pv_mm, u + 1)
                        upper(xTh[:, (u - first) // per, :], bank(o_bank(u), SEQ), oT_hi)

            def ple(l):
                act.preload_act_table_set("sigmoid_and_others")
                for t in range(T):
                    gates_ready(act, l, t)
                    act.activation(xn[:, t, :], pair(4 + 2 * t), ACT.Sigmoid).then_inc(emb_gate, 1)
                act.preload_act_table_set("natural_log_exp_and_others")

            def embedding_hi(l):
                act.wait_ge(emb_tr, l + 1)
                upper(pTh.rearrange("p k n -> p (k n)"), bank(0), emb_hi)

            def ffn_step(n0, s, kind, c, half, r, f0):
                if kind == "g" and half:
                    for b in range(2):
                        first_or_used(act, ffn_gate_mm, f0 * NFC + c + 1, n0 + s, b, r)
                        if c:
                            act.wait_ge(ffn_hidden, f0 * 2 * NFC + 2 * c - 1 + b)
                        act.activation(sg[:, 2 * b:2 * b + 2, :].rearrange("p f n -> p (f n)"), bank(b),
                                       ACT.Silu).then_inc(ffn_silu, 1)
                if kind == "u" and half:
                    if c >= 2:
                        used(act, n0 + FFN_AT["d", c - 2, 1], r)
                    for b in range(2):
                        act.wait_ge(ffn_hidden, f0 * 2 * NFC + 2 * c + b + 1)
                        upper(hTh[:, c % 2, 2 * b:2 * b + 2, :], hp[:, 2 * b:2 * b + 2, :], ffn_hidden_hi)

            for vec, a in ((mix_pre_g, 0), (ffn_pre_g, 16)):
                act.dma_start(small[a:a + 16, :], vec.rearrange("i (k n) -> (i k) n", n=P)).then_inc(gain_in, 16)
            for s in (moe_silu, moe_hidden_hi, moe_y_ok, moe_rows_hi):
                act.sem_inc(s, 1)
            act.preload_act_table_set("natural_log_exp_and_others")
            act.wait_ge(eps_ok, 1)
            pre(0)
            ahead(C_UQ + 1)
            for t in range(T):
                first_or_used(act, z_mm, 1, C_UQ - 1, t)
                zb = ps[:, 3 * t:3 * t + 3, :]
                copy(zl[:, t, :], zb[:, 2, 0:ZW - ZCQ]).then_inc(zl_ok, 1)
                copy(zqk[:, t, 0:384], zb[:, 0, 0:384])
                copy(zqk[:, t, 384:ZV], zb[:, 1, 0:ZV - 384])
                copy(zv[:, t, :], zb[:, 1, ZV - 384:384]).then_inc(z_ok, 1)
            for t in range(T):
                act.wait_ge(lat_gained, t + 1)
                upper(latTh[:, :, t * P:(t + 1) * P], lat[:, :, t * P:(t + 1) * P], lat_hi)
            act.wait_ge(z_ok, T)
            for t in range(T):
                mean_square(xf[:, 1280:1536], zl[:, t, 0:256], hss[:, t, 10:11])
                link(mean_square(xf[:, 1536:1664], zl[:, t, 256:384], hss[:, t, 11:12]))
            act.wait_ge(hss_ok, 1)
            inverse_root(hrs[:, :, :], hss[:, :, :], hrs_ok)
            act.wait_ge(hrs_ok, 1)
            ahead(C_UQ + 2)
            for t in range(T):
                first_or_used(act, up_mm, 1, C_UQ, t)
                copy(qm[:, t, :, :].rearrange("p h n -> p (h n)").rearrange("p (b n) -> p b n", b=2),
                     ps[:, 2 * t:2 * t + 2, 0:384], hrs[:, t, 10:11]).then_inc(up_ok, 1)
            ahead(C_UKV + 2)
            act.wait_ge(qk_tr, 3)
            for t in range(T):
                first_or_used(act, up_mm, 2, C_UKV, t)
                kv = pair(4 + 2 * t).rearrange("p (h n) -> p h n", h=MH)
                copy(km[:, t, :, 0:MN], kv[:, :, 0:MN], hrs[:, t, 11:12])
                copy(vm[:, t, :, :], kv[:, :, MN:], hrs[:, t, 11:12]).then_inc(up_ok, 1)
            ahead(C_UKV + 3)
            for b in range(4):
                act.wait_ge(mla_tr, b + 1)
                copy(qmT[0:MQ, 2 * b:2 * b + 2, :].rearrange("p h n -> p (h n)"), ps[0:MQ, b, :]).then_inc(mqT_ok, 1)
            attention(0, N_U0, 2)
            ahead(C_FFN + 1)
            post(0, lambda t: pair(4 + 2 * t))
            pre(1)
            act.preload_act_table(ACT.Silu)
            for s, step in enumerate(FFN):
                ahead(C_FFN + s + 2)
                ffn_step(C_FFN, s, *step, 0, 0)
                if step == ("d", NFC - 1, 0):
                    embedding_hi(0)
                    act.preload_act_table_set("natural_log_exp_and_others")
            post(1, lambda t: pair(4 + 2 * t))
            pre(2)
            ahead(C_QKV + 1)
            ple(0)
            post(2, lambda t: xn[:, t, :])
            pre(3)
            for c in range(9):
                g, kind = divmod(c, 3)
                n = C_QKV + 2 * c + 1
                ahead(n + 2)
                for t in range(T):
                    first_or_used(act, dil_mm, c + 1, n, t)
                    src = bank(2 * (c % 2) + t)
                    if kind == 2:
                        copy(dv[:, g, t, :], src).then_inc(dil_rows_ok, 1)
                    else:
                        qi = 2 * g + kind
                        if qi >= 2:
                            act.wait_ge(dil_tr, 2 * qi - 2)
                        copy(xn[:, t, (qi % 2) * 512:(qi % 2) * 512 + 512], src).then_inc(dil_rows_ok, 1)
            attention(N_U0, T * DH, 4)
            ahead(C_MOE + 1)
            post(3, lambda t: pair(4 + 2 * t))
            pre(4)
            act.wait_ge(gap_ok, 1)
            act.activation(rs[:, 5, :], rs[:, 4, :], ACT.Exp).then_inc(gap_exp, 1)

            def gathered_hi(r):
                for half in range(2):
                    act.wait_ge(moe_rows_ok, 2 * r + half + 2)
                    upper(xgh[:, 4 * half:4 * half + 4, :], xgp[:, 4 * half:4 * half + 4, :], moe_rows_hi)

            def hidden_hi(r, c):
                act.wait_ge(moe_hidden_tr, r * NFC + c + 2)
                hidden_used(act, r, c)
                upper(mhTh[:, c % 2, :], bank(2), moe_hidden_hi)

            def expert(r):
                for j, (kind, c, half) in enumerate(FFN):
                    chunk_hi(act, C_MOE + j + 2, r)
                    if (kind, half) == ("g", 1):
                        used(act, C_MOE + j, r)
                        act.wait_ge(moe_hidden, r * NFC + c + 1)
                        act.activation(msg, bank(0), ACT.Silu).then_inc(moe_silu, 1)
                    if (kind, half) == ("u", 0) and c:
                        hidden_hi(r, c - 1)
                    if (kind, c, half) == ("d", NFC - 2, 1):
                        hidden_hi(r, NFC - 1)
                for half in range(2):
                    if half:
                        used(act, C_MOE + N_FFN - 1, r)
                    else:
                        act.wait_ge(moe_y_mm, r + 2)
                    act.wait_ge(moe_scatter_mm, r * 4 + 1)
                    copy(ysb[:, half * BANK:(half + 1) * BANK], bank(4 + half)).then_inc(moe_y_ok, 1)
                for s in (ffn_silu, ffn_hidden_hi):
                    act.sem_inc(s, 2 * NFC)

            def full_expert(r):
                act.wait_ge(moe_rows_split, r * 2 + 3)
                for s, step in enumerate(FFN):
                    chunk_hi(act, C_MOE + s + 2, r)
                    ffn_step(C_MOE, s, *step, r, r + 1)
                act.sem_inc(moe_silu, NFC)
                act.sem_inc(moe_hidden_hi, NFC)
                act.sem_inc(moe_y_ok, 2)

            act.preload_act_table(ACT.Silu)
            gathered_hi(0)
            act.wait_ge(full_ok, 1)
            with act.Fori(0, NE) as e:
                many = act.value_load(fulli[0:1, bass.ds(e, 1)], min_val=0, max_val=1)
                with act.If(many > 0):
                    full_expert(e)
                with act.If(many < 1):
                    expert(e)
                with act.If(e < NE - 1):
                    gathered_hi(e + 1)
            act.wait_ge(moe_rows_split, 2 * NE + 1)
            embedding_hi(1)
            act.preload_act_table_set("natural_log_exp_and_others")
            post(4, lambda t: acc[:, t, :])
            pre(5)
            for i in range(2, N_PLE):
                chunk_hi(act, C_MOE + i, NE)
            ple(1)
            post(5, lambda t: xn[:, t, :])

        @block.vector
        def _(dve):
            steps = [0]

            def link(ins):
                steps[0] += 1
                ins.then_inc(dve_step, 1)
                dve.wait_ge(dve_step, steps[0])

            ahead = Ahead(chunk_lo, dve)

            def lower(out, whole, hi, ok):
                dve.tensor_tensor(out, whole, hi.bitcast(F32), ALU.subtract).then_inc(ok, 1)

            def pre(i, between=lambda: None):
                kind, l = PRE[i]
                for t in range(T):
                    dve.wait_ge(rstd_ok, 2 * i + t + 1)
                    dve.tensor_scalar(xn[:, t, :], h[:, t, :], rstd[:, t:t + 1], None, ALU.mult).then_inc(xn_ok, 1)
                between()

                def rest(q):
                    t, half = divmod(q, 2)
                    dve.wait_ge(xh_ok, 4 * i + q + 1)
                    at = (slice(None), slice(4 * half, 4 * half + 4), slice(t * P, (t + 1) * P))
                    lower(xTl[at], product(i, q), xTh[at], xT_ok)

                for q in range(4):
                    t, half = divmod(q, 2)
                    dve.wait_ge(xn_tr, 4 * i + q + 1)
                    a = GAIN[kind] + KD * l + 4 * half
                    dve.tensor_tensor(product(i, q), bank(PRE_BANK[i] + q).rearrange("p (k n) -> p k n", k=4),
                                      of(gT[:, a:a + 4], P), ALU.mult).then_inc(xp_ok, 1)
                    if q and i != 4:
                        rest(q - 1)
                if i == 4:
                    return rest
                rest(3)

            def post(j, y):
                g, l = j % 3, j // 3
                dve.wait_ge(gb_in[g], 16 * (l + 1))
                for t in range(T):
                    dve.wait_ge(ysq_ok, 2 * j + t + 1)
                    link(dve.tensor_tensor(xn[:, t, :], y(t), gb[:, g, :], ALU.mult))
                    dve.wait_ge(prstd_ok, 2 * j + t + 1)
                    dve.scalar_tensor_tensor(out=h[:, t, :], in0=xn[:, t, :], scalar=prstd[:, t:t + 1],
                                             in1=h[:, t, :], op0=ALU.mult, op1=ALU.add).then_inc(h_ok, 1)

            def rotate(out, rows_, cos, sin, half, a, b):
                dve.tensor_tensor(a, rows_, cos, ALU.mult)
                lo, hi = slice(0, half), slice(half, 2 * half)
                dve.tensor_tensor(b[..., lo], rows_[..., hi], sin[..., lo], ALU.mult)
                link(dve.tensor_tensor(b[..., hi], rows_[..., lo], sin[..., hi], ALU.mult))
                return dve.tensor_tensor(out, a, b, ALU.add)

            def maxes(u):
                dve.wait_ge(sc_mm, u + 1)
                b = u % 3
                if u < N_U0:
                    s = GQA_SCALE if u < N_GQA else MLA_SCALE
                    link(dve.tensor_reduce(smax[:, b, :], bank(S_BANK[b]).rearrange("p (t n) -> p t n", t=T), AX_X, ALU.max))
                    dve.tensor_scalar(snm[:, b, :], smax[:, b, :], -s, None, ALU.mult).then_inc(sc_max, 1)
                else:
                    if u >= N_U0 + 3:
                        dve.wait_ge(pr_tr, u - 2)
                    link(dve.tensor_tensor_reduce(out=probs(u), in0=bank(S_BANK[b]), in1=mask[:, u % T, :],
                                                  scale=HD ** -0.5, scalar=-3e38, op0=ALU.add, op1=ALU.max,
                                                  accum_out=smax[:, b, 0:1]))
                    dve.tensor_scalar(snm[:, b, 0:1], smax[:, b, 0:1], -1.0, None, ALU.mult).then_inc(sc_max, 1)

            def normalise(u):
                b = u % 3
                dve.wait_ge(sc_exp, u + 1)
                n = T if u < N_U0 else 1
                link(dve.reciprocal(srec[:, b, 0:n], ssum[:, b, 0:n]))
                w = BANK // n
                for t in range(n):
                    q = dve.tensor_scalar(probs(u)[:, t * w:(t + 1) * w], probs(u)[:, t * w:(t + 1) * w],
                                          srec[:, b, t:t + 1], None, ALU.mult)
                q.then_inc(pr_ok, 1)

            def attention(first, n, per):
                for i in range(n + 4):
                    if i < n:
                        maxes(first + i)
                    if 1 <= i <= n:
                        normalise(first + i - 1)
                    if i >= 4 and (i - 4) % per == per - 1:
                        u = first + i - 4
                        dve.wait_ge(oT_hi, oT_before(u) + 1)
                        tile = (u - first) // per
                        lower(xTl[:, tile, :], bank(o_bank(u), SEQ), xTh[:, tile, :], oT_ok)

            def embedding_lo(l):
                dve.wait_ge(emb_hi, l + 1)
                lower(pTl.rearrange("p k n -> p (k n)"), bank(0), pTh.rearrange("p k n -> p (k n)"), emb_split)

            def ple(l):
                if l == 0:
                    ahead(C_QKV + 1)
                else:
                    for i in range(2, N_PLE):
                        chunk_lo(dve, C_MOE + i, NE)
                for t in range(T):
                    dve.wait_ge(emb_gate, 2 * l + t + 1)
                    dve.tensor_tensor(xn[:, t, :], pair(2 * t), xn[:, t, :], ALU.mult).then_inc(y_ok, 1)

            def ffn_step(n0, s, kind, c, half, r, f0):
                if kind == "u" and half:
                    for b in range(2):
                        dve.wait_ge(ffn_silu, f0 * 2 * NFC + 2 * c + b + 1)
                        first_or_used(dve, ffn_up_mm, f0 * NFC + c + 1, n0 + s, b, r)
                        if c:
                            dve.wait_ge(ffn_hidden_split, f0 * 2 * NFC + 2 * c)
                        dve.tensor_tensor(hp[:, 2 * b:2 * b + 2, :].rearrange("p f n -> p (f n)"),
                                          sg[:, 2 * b:2 * b + 2, :].rearrange("p f n -> p (f n)"),
                                          bank(2 + b), ALU.mult).then_inc(ffn_hidden, 1)
                    for b in range(2):
                        dve.wait_ge(ffn_hidden_hi, f0 * 2 * NFC + 2 * c + b + 1)
                        at = (slice(None), c % 2, slice(2 * b, 2 * b + 2), slice(None))
                        lower(hTl[at], hp[:, 2 * b:2 * b + 2, :], hTh[at], ffn_hidden_split)

            for s in (moe_sel_ok, moe_rows_ok, moe_rows_split, moe_hidden, moe_hidden_split, moe_selT_ok, moe_added):
                dve.sem_inc(s, 1)
            dve.memset(eps[:, :], EPS).then_inc(eps_ok, 1)
            dve.memset(posm[:, :, JOBS - 1:], -1.0)
            dve.memset(gate[:, :, JOBS - 1:], 0.0)
            def gains():
                dve.wait_ge(gains_tr, 1)
                link(dve.tensor_copy(gT[:, :], bank(0, 51)))

            pre(0, gains)
            ahead(C_IN + 4)
            dve.wait_ge(tab_in, 16)
            dve.wait_ge(grow_in, 32)
            axC = table("axC").rearrange("p (t n) -> p t n", t=T)
            axS = table("axS").rearrange("p (t a f n) -> p t a f n", t=T, a=2, f=2)
            for i in range(2):
                dve.tensor_tensor(rot[:, 2 * i, :, :], axC, grow[:, i:i + 1, :].to_broadcast([P, T, HD]), ALU.mult)
                rv = rot[:, 2 * i + 1, :, :].rearrange("p t (a f n) -> p t a f n", a=2, f=2)
                gv = grow[:, i, :].rearrange("p (a f n) -> p a f n", a=2, f=2)
                for t in range(T):
                    for f in range(2):
                        q = dve.tensor_tensor(rv[:, t, :, f, :], axS[:, t, :, f, :], gv[:, :, 1 - f, :], ALU.mult)
            link(q)
            ahead(C_UQ + 1)
            for t in range(T):
                dve.wait_ge(lat_tr, t + 1)
                dve.tensor_tensor(lat[:, :, t * P:(t + 1) * P], bank(6 + t, 3 * P).rearrange("p (k n) -> p k n", k=3),
                                  of(gT[:, 48:51], P), ALU.mult).then_inc(lat_gained, 1)
            for t in range(T):
                dve.wait_ge(lat_hi, t + 1)
                at = (slice(None), slice(None), slice(t * P, (t + 1) * P))
                lower(latTl[at], lat[at], latTh[at], lat_split)
            dve.wait_ge(z_ok, T)
            sq = xf[:, 0:T * ZV].rearrange("p (t n) -> p t n", t=T)
            link(dve.tensor_tensor(sq, zqk, zqk, ALU.mult))
            for t in range(T):
                q = dve.tensor_reduce(hss[:, t, 0:10], sq[:, t, :].rearrange("p (h n) -> p h n", h=10), AX_X, ALU.add)
            link(q)
            dve.tensor_scalar(hss[:, :, 0:10], hss[:, :, 0:10], 1.0 / HD, None, ALU.mult).then_inc(hss_ok, 1)
            ahead(C_UQ + 2)
            sa, sb_ = probs0[:, 0, :], probs0[:, 1, :]
            for t in range(T):
                for first, heads, i in ((ZQ, NQ, 0), (ZK, NKV, 1)):
                    n = heads * HD
                    src = zqk[:, t, first:first + n]
                    v5 = "p (h a f n) -> p h a f n"
                    cos = rot[:, 2 * i, t:t + 1, :].to_broadcast([P, heads, HD])
                    sinv = rot[:, 2 * i + 1, t, :].rearrange("p (a f n) -> p a f n", a=2, f=2)
                    s5 = src.rearrange(v5, h=heads, a=2, f=2)
                    b5 = sb_[:, 0:n].rearrange(v5, h=heads, a=2, f=2)
                    dve.tensor_tensor(sa[:, 0:n].rearrange("p (h n) -> p h n", h=heads),
                                      src.rearrange("p (h n) -> p h n", h=heads), cos, ALU.mult)
                    for f in range(2):
                        q = dve.tensor_tensor(b5[:, :, :, f, :], s5[:, :, :, 1 - f, :],
                                              sinv[:, :, f, :].unsqueeze(1).to_broadcast([P, heads, 2, 16]), ALU.mult)
                    link(q)
                    link(dve.tensor_tensor(sa[:, 0:n], sa[:, 0:n], sb_[:, 0:n], ALU.add))
                    if t == 0 and i == 0:
                        dve.wait_ge(hrs_ok, 1)
                    a3 = sa[:, 0:n].rearrange("p (h n) -> p h n", h=heads)
                    sc = of(hrs[:, t, (0, NQ)[i]:(NQ, NQ + NKV)[i]], HD)
                    if i == 0:
                        link(dve.tensor_tensor(qr[:, t, :].rearrange("p (h n) -> p h n", h=heads), a3, sc, ALU.mult))
                    else:
                        for u in range(2):
                            q = dve.tensor_tensor(kr[:, t, :, u, :], a3, sc, ALU.mult)
                        link(q)
            dve.sem_inc(qk_ok, 1)
            ahead(C_UKV + 2)
            for t in range(T):
                dve.wait_ge(qk_tr, t + 1)
                dve.tensor_copy(qT[:, :, t * P:(t + 1) * P], bank(t).rearrange("p (c n) -> p c n", c=4)).then_inc(qkT_ok, 1)
            dve.wait_ge(qk_tr, 3)
            dve.tensor_copy(kT.rearrange("p j n -> p (j n)"), bank(2)).then_inc(qkT_ok, 1)
            mlC = table("mlC").rearrange("p (t n) -> p t n", t=T)
            mlS = table("mlS").rearrange("p (t n) -> p t n", t=T)
            dve.wait_ge(up_ok, T)
            hb = [P, T, MH, MR]
            ma, mb = (v.rearrange("p (t h n) -> p t h n", t=T, h=MH) for v in (mtmp[:, 0:512], probs0[:, 2, :]))
            link(rotate(qm[:, :, :, MN:], qm[:, :, :, MN:], mlC.unsqueeze(2).to_broadcast(hb),
                        mlS.unsqueeze(2).to_broadcast(hb), MR // 2, ma, mb))
            ka, kb = (sa[:, i * 64:(i + 1) * 64].rearrange("p (t n) -> p t n", t=T) for i in range(2))
            kro = sa[:, 128:192].rearrange("p (t n) -> p t n", t=T)
            link(rotate(kro, zl[:, :, ZKR - ZCQ:], mlC, mlS, MR // 2, ka, kb))
            dve.tensor_copy(km[:, :, :, MN:], kro.unsqueeze(2).to_broadcast(hb)).then_inc(mrow_ok, 1)
            ahead(C_UKV + 3)
            for b in range(4):
                dve.wait_ge(mla_tr, 4 + b + 1)
                dve.tensor_copy(kmT[0:MQ, 2 * b:2 * b + 2, :].rearrange("p h n -> p (h n)"), ps[0:MQ, 4 + b, :]).then_inc(mkT_ok, 1)
            attention(0, N_U0, 2)
            ahead(C_FFN + 1)
            post(0, lambda t: pair(4 + 2 * t))
            pre(1)
            for s, step in enumerate(FFN):
                ahead(C_FFN + s + 2)
                ffn_step(C_FFN, s, *step, 0, 0)
                if step == ("d", NFC - 1, 0):
                    embedding_lo(0)
            post(1, lambda t: pair(4 + 2 * t))
            pre(2)
            ple(0)
            post(2, lambda t: xn[:, t, :])
            pre(3)
            dC = table("diC").rearrange("p (t n) -> p t n", t=T).unsqueeze(2).to_broadcast([P, T, DH, 16])
            dS = table("diS").rearrange("p (t n) -> p t n", t=T).unsqueeze(2).to_broadcast([P, T, DH, 16])
            da, db = (dtmp[:, i, 0:256].rearrange("p (t h n) -> p t h n", t=T, h=DH) for i in range(2))

            def dil_T(qi):
                g, kind = divmod(qi, 2)
                for t in range(T):
                    dve.wait_ge(dil_tr, 2 * qi + t + 1)
                    dve.tensor_copy((dq, dk)[kind][:, g, :, t * P:(t + 1) * P],
                                    bank(4 + 2 * (qi % 2) + t).rearrange("p (c n) -> p c n", c=4)).then_inc(dil_T_ok, 1)

            for c in range(9):
                g, kind = divmod(c, 3)
                ahead(C_QKV + 2 * c + 3)
                if kind < 2:
                    qi = 2 * g + kind
                    dve.wait_ge(dil_rows_ok, 2 * c + 2)
                    rw = xn[:, :, (qi % 2) * 512:(qi % 2) * 512 + 512].rearrange("p t (h n) -> p t h n", h=DH)[:, :, :, 0:16]
                    q = rotate(rw, rw, dC, dS, 8, da, db)
                    link(q)
                    dve.sem_inc(dil_rotated, 1)
                if c and (c - 1) % 3 < 2:
                    dil_T(2 * ((c - 1) // 3) + (c - 1) % 3)
            dve.wait_ge(mask_in, 16)
            attention(N_U0, T * DH, 4)
            ahead(C_MOE + 1)
            post(3, lambda t: pair(4 + 2 * t))
            rest = pre(4)

            def R(i):
                return rt[:, i, :].rearrange("p (t n) -> p t n", t=T)

            def each(v):
                return v.unsqueeze(2).to_broadcast([P, T, NE])

            rev = table("rev").rearrange("p (t n) -> p t n", t=T)
            dve.wait_ge(logits_mm, 1)
            link(dve.tensor_copy(rt[:, 0, :], bank(4, T * NE)))

            def largest(logits, top, eq, best, onehot):
                link(dve.tensor_reduce(rs[:, top, :], R(logits), AX_X, ALU.max))
                link(dve.tensor_tensor(R(eq), R(logits), each(rs[:, top, :]), ALU.is_equal))
                link(dve.tensor_tensor(R(eq), R(eq), rev, ALU.mult))
                link(dve.tensor_reduce(rs[:, best, :], R(eq), AX_X, ALU.max))
                link(dve.tensor_tensor(R(onehot), R(eq), each(rs[:, best, :]), ALU.is_equal))

            largest(0, 0, 1, 1, 2)
            link(dve.scalar_tensor_tensor(out=rt[:, 3, :], in0=rt[:, 2, :], scalar=-3e38, in1=rt[:, 0, :],
                                          op0=ALU.mult, op1=ALU.add))
            largest(3, 2, 4, 3, 5)
            dve.tensor_tensor(rs[:, 4, :], rs[:, 2, :], rs[:, 0, :], ALU.subtract).then_inc(gap_ok, 1)
            dve.tensor_tensor(rt[:, 6, :], rt[:, 2, :], rt[:, 5, :], ALU.add).then_inc(chosen_ok, 1)
            dve.wait_ge(gap_exp, 1)
            link(dve.tensor_scalar(rs[:, 6, :], rs[:, 5, :], 1.0, None, ALU.add))
            link(dve.reciprocal(rs[:, 7, :], rs[:, 6, :]))
            link(dve.tensor_tensor(rs[:, 1, :], rs[:, 5, :], rs[:, 7, :], ALU.mult))
            dve.tensor_tensor(R(7), R(2), each(rs[:, 7, :]), ALU.mult)
            link(dve.tensor_tensor(R(8), R(5), each(rs[:, 1, :]), ALU.mult))
            link(dve.tensor_tensor(gate[:, :, 0:NE], R(7), R(8), ALU.add))
            dve.wait_ge(places_mm, 1)
            counts = ps[:, 5, T * NE:(T + 1) * NE]
            link(dve.scalar_tensor_tensor(out=rt[:, 9, :], in0=bank(5, T * NE), scalar=1.0, in1=rt[:, 6, :],
                                          op0=ALU.add, op1=ALU.mult))
            link(dve.tensor_scalar(posm[:, :, 0:NE], R(9), -1.0, None, ALU.add))
            link(dve.tensor_scalar(full[:, :], counts, float(P), None, ALU.is_gt))
            dve.tensor_copy(fulli[:, :], full[:, :]).then_inc(full_ok, 1)
            dve.wait_ge(moetab_in, 16)
            dve.wait_ge(acc_zero, 1)

            def select(r):
                dve.wait_ge(moe_gather_mm, r * 2 + 1)
                dve.wait_ge(moe_selT_tr, r + 1)
                for t in range(T):
                    at, w = posm[:, t, bass.ds(r, 1)], gate[:, t, bass.ds(r, 1)]
                    dve.tensor_scalar(sel[:, t, :], iota, at, None, ALU.is_equal)
                    q = dve.tensor_scalar(selg[:, t, :], iota, at, w, ALU.is_equal, ALU.mult)
                q.then_inc(moe_sel_ok, 1)

            def gathered(r):
                for half in range(2):
                    dve.wait_ge(moe_gather_mm, r * 2 + half + 2)
                    dve.wait_ge(moe_rows_split, r * 2 + 1)
                    a = GAIN["ffn"] + KD + 4 * half
                    dve.tensor_tensor(xgp[:, 4 * half:4 * half + 4, :], bank(6 + half).rearrange("p (k n) -> p k n", k=4),
                                      of(gT[:, a:a + 4], P), ALU.mult).then_inc(moe_rows_ok, 1)
                    dve.wait_ge(moe_rows_hi, r * 2 + half + 2)
                    at = (slice(None), slice(4 * half, 4 * half + 4), slice(None))
                    lower(xgl[at], xgp[at], xgh[at], moe_rows_split)

            def hidden_lo(r, c):
                dve.wait_ge(moe_hidden_hi, r * NFC + c + 2)
                lower(mhTl[:, c % 2, :], bank(2), mhTh[:, c % 2, :], moe_hidden_split)

            def expert(r):
                for j, (kind, c, half) in enumerate(FFN):
                    chunk_lo(dve, C_MOE + j + 2, r)
                    if (kind, half) == ("u", 0) and c:
                        hidden_lo(r, c - 1)
                    if (kind, half) == ("u", 1):
                        dve.wait_ge(moe_silu, r * NFC + c + 2)
                        used(dve, C_MOE + j, r)
                        dve.wait_ge(moe_hidden_tr, r * NFC + max(c, 1))
                        dve.tensor_tensor(mh[:, c % 2, :], msg, bank(1), ALU.mult).then_inc(moe_hidden, 1)
                        if c == 1:
                            dve.wait_ge(moe_selT_tr, r + 2)
                            dve.wait_ge(moe_scatter_mm, r * 4 + 1)
                            dve.tensor_copy(selT.rearrange("p t n -> p (t n)"), bank(3, T * P)).then_inc(moe_selT_ok, 1)
                        if c == 3:
                            select(r + 1)
                    if (kind, c, half) == ("d", NFC - 2, 1):
                        hidden_lo(r, NFC - 1)
                with dve.If(r < NE - 1):
                    gathered(r + 1)
                for half in range(2):
                    for t in range(T):
                        dve.wait_ge(moe_scatter_mm, r * 4 + 2 * half + t + 2)
                        dve.wait_ge(moe_added, r * 4 + 1)
                        part = acc[:, t, half * BANK:(half + 1) * BANK]
                        dve.tensor_tensor(part, bank(SCATTER_BANK[half] - t), part, ALU.add).then_inc(moe_added, 1)
                for s in (ffn_hidden, ffn_hidden_split):
                    dve.sem_inc(s, 2 * NFC)

            def full_expert(r):
                for s, step in enumerate(FFN):
                    chunk_lo(dve, C_MOE + s + 2, r)
                    ffn_step(C_MOE, s, *step, r, r + 1)
                    if step == ("u", 3, 1):
                        select(r + 1)
                dve.wait_ge(moe_added, r * 4 + 1)
                for t in range(T):
                    if t:
                        used(dve, C_MOE + N_FFN - 1, r)
                    else:
                        dve.wait_ge(moe_y_mm, r + 2)
                    dve.scalar_tensor_tensor(out=acc[:, t, :], in0=pair(6 - 2 * t), scalar=gate[:, t, bass.ds(r, 1)],
                                             in1=acc[:, t, :], op0=ALU.mult, op1=ALU.add).then_inc(moe_added, 2)
                dve.sem_inc(moe_hidden, NFC)
                dve.sem_inc(moe_hidden_split, NFC)
                dve.sem_inc(moe_selT_ok, 1)
                with dve.If(r < NE - 1):
                    gathered(r + 1)

            def first_selection():
                for t in range(T):
                    dve.tensor_scalar(sel[:, t, :], iota, posm[:, t, 0:1], None, ALU.is_equal)
                    q = dve.tensor_scalar(selg[:, t, :], iota, posm[:, t, 0:1], gate[:, t, 0:1], ALU.is_equal, ALU.mult)
                q.then_inc(moe_sel_ok, 1)

            first_selection()
            for q in range(4):
                rest(q)
            gathered(0)
            dve.wait_ge(full_ok, 1)
            with dve.Fori(0, NE) as e:
                many = dve.value_load(fulli[0:1, bass.ds(e, 1)], min_val=0, max_val=1)
                with dve.If(many > 0):
                    full_expert(e)
                with dve.If(many < 1):
                    expert(e)
            dve.wait_ge(moe_added, NE * 4 + 1)
            dve.sem_inc(y_ok, 2)
            embedding_lo(1)
            post(4, lambda t: acc[:, t, :])
            pre(5)
            ple(1)
            post(5, lambda t: xn[:, t, :])

        @block.tensor
        def _(pe):
            def mm(out_, lhsT, rhs, start, stop):
                return pe.matmul(out_, lhsT, rhs, start=start, stop=stop)

            def pre(i):
                for t in range(T):
                    pe.wait_ge(xn_ok, 2 * i + t + 1)
                    for half in range(2):
                        for k in range(4):
                            a = (4 * half + k) * P
                            q = pe.transpose(ps[:, PRE_BANK[i] + 2 * t + half, k * P:(k + 1) * P], xn[:, t, a:a + P], ident)
                        q.then_inc(xn_tr, 1)

            def mm3(out_, lhsT, rhs, start, stop):
                (lh, ll), (rh, rl) = lhsT, rhs
                pe.matmul(out_, lh, rl, start=start, stop=False, skip_group_check=True)
                pe.matmul(out_, lh, rh, start=False, stop=False, skip_group_check=True)
                return pe.matmul(out_, ll, rh, start=False, stop=stop, skip_group_check=True)

            def at(parts, *index):
                return tuple(x[(slice(None),) + index] for x in parts)

            def normalised(i, t, k):
                pe.wait_ge(xT_ok, 4 * i + 2 * t + k // 4 + 1)

            def rows_by(n, tiles, width, banks, b0, lhs, first, last, done=None, r=0, b1=None):
                w = chunk(pe, n, tiles, width, r)
                starts = (b0, b0 + len(banks) if b1 is None else b1)
                for t in range(T):
                    for j, (a, b) in enumerate(banks):
                        for k in range(tiles):
                            q = mm3(ps[:, starts[t] + j, 0:b - a], lhs(k, t), at(w, k, slice(a, b)),
                                    first and k == 0, last and k == tiles - 1)
                    if done is not None and t == 0:
                        q.then_inc(done, 1)
                q.then_inc(chunk_used, 1)

            xT = (xTh, xTl)
            HALVES = ((0, BANK), (BANK, D))

            def lhs_of(base):
                return lambda k, t: at(xT, base + k, slice(t * P, (t + 1) * P))

            def scores(u):
                b = u % 3
                if u >= 3:
                    pe.wait_ge(sc_exp, u - 2)
                if u < N_U0:
                    hh, o = u % 8, 64 * (u % 2)
                    for t in range(T):
                        cols = slice(t * P, (t + 1) * P)
                        if u < N_GQA:
                            l_, r_ = qT[o:o + 64, hh // 2, cols], kT[o:o + 64, hh // 4, :]
                        else:
                            l_, r_ = qmT[0:MQ, hh, cols], kmT[0:MQ, hh, :]
                        q = mm(ps[:, S_BANK[b], t * SEQ:(t + 1) * SEQ], l_, r_, True, True)
                else:
                    hh, t = divmod(u - N_U0, T)
                    o, own = 64 * (hh % 2), slice(t * P, (t + 1) * P)
                    for g in range(DG):
                        a, b_ = ((0, SEQ), (SEQ, SEQ + P), (SEQ + P, BANK))[g]
                        q = mm(ps[:, S_BANK[b], a:b_], dq[o:o + 64, g, hh // 2, own],
                               dk[o:o + 64, g, hh // 2, :] if g == 0 else dk[o:o + 64, g, hh // 2, own], True, True)
                q.then_inc(sc_mm, 1)

            def transposes(u):
                pe.wait_ge(pr_ok, u + 1)
                if u >= 2:
                    pe.wait_ge(prT_ok, u - 1)
                for a in range(4):
                    to = a if u >= N_U0 else 2 * (a % 2) + a // 2
                    q = pe.transpose(ps[:, T_BANK[u % 2], to * P:(to + 1) * P], probs(u)[:, a * P:(a + 1) * P], ident)
                q.then_inc(pr_tr, 1)

            def values(u):
                pe.wait_ge(prT_ok, u + 1)
                n = oT_before(u)
                if n >= 2:
                    pe.wait_ge(oT_ok, n - 1)
                if u < N_U0:
                    hh, o = u % 8, 64 * (u % 2)
                    for k in range(T):
                        v = zv[:, k, HD * (hh // 4):HD * (hh // 4 + 1)] if u < N_GQA else vm[:, k, hh, :]
                        q = mm(ps[o:o + 64, o_bank(u), 0:SEQ], v, prT_buf[:, k * SEQ:(k + 1) * SEQ], k == 0, k == T - 1)
                else:
                    hh, t = divmod(u - N_U0, T)
                    o = 64 * (hh % 2)
                    for j, (g, k) in enumerate(((0, 0), (0, 1), (1, t), (2, t))):
                        q = mm(ps[o:o + 64, o_bank(u), t * P:(t + 1) * P], dv[:, g, k, hh * HD:(hh + 1) * HD],
                               prT_buf[:, j * P:(j + 1) * P], j == 0, j == 3)
                q.then_inc(pv_mm, 1)

            def attention(first, n):
                for i in range(n + 3):
                    if i < n:
                        scores(first + i)
                    if 2 <= i < n + 2:
                        transposes(first + i - 2)
                    if i >= 3:
                        values(first + i - 3)

            def embedding_T(l):
                pe.wait_ge(p_in, 16 * (l + 1))
                for k in range(PK):
                    for t in range(T):
                        q = pe.transpose(ps[:, 0, k * SEQ + t * P:k * SEQ + (t + 1) * P], pe_rows[:, t, k * P:(k + 1) * P], ident)
                q.then_inc(emb_tr, 1)

            def embedding(l, n0, rounds=0):
                pe.wait_ge(emb_split, l + 1)
                w = chunk(pe, n0, PK, D, rounds)
                for t in range(T):
                    for j, (a, b) in enumerate(HALVES):
                        for k in range(PK):
                            q = mm3(ps[:, 2 * t + j, :], at((pTh, pTl), k, slice(t * P, (t + 1) * P)),
                                    at(w, k, slice(a, b)), k == 0, k == PK - 1)
                q.then_inc(chunk_used, 1)

            def embedding_gate(l, n0, rounds=0):
                for i in range(4):
                    w = chunk(pe, n0 + 1 + i, 2, D, rounds)
                    for t in range(T):
                        if i == 0:
                            normalised(3 * l + 2, t, 4)
                        for j, (a, b) in enumerate(HALVES):
                            for k in range(2):
                                q = mm3(ps[:, 4 + 2 * t + j, :], at(xT, 2 * i + k, slice(t * P, (t + 1) * P)),
                                        at(w, k, slice(a, b)), i == 0 and k == 0, i == 3 and k == 1)
                        if i == 3 and (l or t == 0):
                            q.then_inc(emb_gate_mm, 1)
                    if i < 3 or l == 0:
                        q.then_inc(chunk_used, 1)

            def ffn_step(n0, s, kind, c, half, r, f0, banks, done):
                n = n0 + s
                if kind == "d":
                    if half == 0:
                        pe.wait_ge(ffn_hidden_split, f0 * 2 * NFC + 2 * c + 2)
                    rows_by(n, 2, D, HALVES, banks[0], lambda k, t: at((hTh, hTl), c % 2, 2 * half + k, slice(t * P, (t + 1) * P)),
                            c == 0 and half == 0, c == NFC - 1 and half == 1,
                            done if c == NFC - 1 and half == 1 else None, r, banks[1])
                    return
                if half == 0 and c:
                    pe.wait_ge(ffn_silu if kind == "g" else ffn_hidden, f0 * 2 * NFC + 2 * c)
                w = chunk(pe, n, 4, FC, r)
                for f in range(FT):
                    for k in range(4):
                        q = mm3(ps[:, (0 if kind == "g" else 2) + f // 2, (f % 2) * SEQ:(f % 2 + 1) * SEQ],
                                at(w, k, slice(f * P, (f + 1) * P)), at(xT, 4 * half + k),
                                half == 0 and k == 0 and f % 2 == 0, half == 1 and k == 3)
                    if f == 1 and half:
                        q.then_inc(ffn_gate_mm if kind == "g" else ffn_up_mm, 1)
                q.then_inc(chunk_used, 1)

            for s in (moe_gather_mm, moe_selT_tr, moe_hidden_tr, moe_y_mm, moe_scatter_mm):
                pe.sem_inc(s, 1)
            pe.wait_ge(tab_in, 16)
            pe.wait_ge(gain_in, 16 * 2)
            pe.wait_ge(more_gain_in, 16 * 3)
            pe.transpose(ps[:, 0, 0:51], small, tab[0:51, 0:51]).then_inc(gains_tr, 1)
            pre(0)
            def first_rows(n):
                def lhs(k, t):
                    if n % 4 == 0:
                        normalised(0, t, n)
                    return at(xT, n, slice(t * P, (t + 1) * P))
                return lhs

            for n in range(N_IN):
                rows_by(n, 1, ZW, Z_BANKS, 0, first_rows(n), n == 0, n == N_IN - 1, z_mm if n == N_IN - 1 else None)
            for t in range(T):
                pe.wait_ge(zl_ok, t + 1)
                for k in range(3):
                    q = pe.transpose(ps[:, 6 + t, k * P:(k + 1) * P], zl[:, t, k * P:(k + 1) * P], ident)
                q.then_inc(lat_tr, 1)
            pe.wait_ge(lat_split, T)
            lat_parts = (latTh, latTl)
            rows_by(C_UQ, 2, MH * MQ, ((0, 384), (384, 768)), 0, lambda k, t: at(lat_parts, k, slice(t * P, (t + 1) * P)),
                    True, True, up_mm)
            rows_by(C_UKV, 1, MH * 2 * HD, HALVES, 4, lambda k, t: at(lat_parts, 2, slice(t * P, (t + 1) * P)),
                    True, True, up_mm)
            pe.wait_ge(qk_ok, 1)
            pe.wait_ge(up_ok, T)
            for t in range(T):
                for c in range(4):
                    q = pe.transpose(ps[:, t, c * P:(c + 1) * P], qr[:, t, c * P:(c + 1) * P], ident)
                q.then_inc(qk_tr, 1)
            for j in range(NKV):
                for t in range(T):
                    q = pe.transpose(ps[:, 2, (T * j + t) * P:(T * j + t + 1) * P], kr[:, t, j, :, :].rearrange("p u n -> p (u n)"), ident)
            q.then_inc(qk_tr, 1)
            pe.wait_ge(qkT_ok, 3)
            pe.wait_ge(up_ok, 2 * T)
            pe.wait_ge(mrow_ok, 1)
            for src, b0 in ((qm, 0), (km, 4)):
                for b in range(4):
                    for hh in (0, 1):
                        for t in range(T):
                            q = pe.transpose(ps[0:MQ, b0 + b, hh * SEQ + t * P:hh * SEQ + (t + 1) * P], src[:, t, 2 * b + hh, :], ident)
                    q.then_inc(mla_tr, 1)
            pe.wait_ge(mqT_ok, 4)
            pe.wait_ge(mkT_ok, 4)
            attention(0, N_U0)
            pe.wait_ge(oT_ok, N_U0 // 2)
            for a in range(N_ABOUT):
                rows_by(C_ABOUT + a, 2, D, HALVES, 4, lhs_of(2 * a), a == 0, a == N_ABOUT - 1, y_ok if a == N_ABOUT - 1 else None)
            pre(1)
            for s, step in enumerate(FFN):
                if s < 2:
                    normalised(1, T - 1, 4 * s)
                if step == ("d", NFC - 1, 0):
                    pe.wait_ge(ffn_silu, 2 * NFC)
                    embedding_T(0)
                ffn_step(C_FFN, s, *step, 0, 0, (4, 6), y_ok)
            embedding(0, C_PLE0)
            pre(2)
            embedding_gate(0, C_PLE0)
            pre(3)
            for c in range(9):
                g, kind = divmod(c, 3)
                for half in range(2):
                    n = C_QKV + 2 * c + half
                    w = chunk(pe, n, 4, FC)
                    for t in range(T):
                        if c == 0:
                            normalised(3, t, 4 * half)
                        if c >= 2 and half == 0:
                            pe.wait_ge(dil_rows_ok, 2 * c - 3 + t)
                        for k in range(4):
                            q = mm3(ps[:, 2 * (c % 2) + t, :], at(xT, 4 * half + k, slice(t * P, (t + 1) * P)),
                                    at(w, k, slice(0, FC)), half == 0 and k == 0, half == 1 and k == 3)
                        if t == 0 and half:
                            q.then_inc(dil_mm, 1)
                    q.then_inc(chunk_used, 1)
                if c and (c - 1) % 3 < 2:
                    qi = 2 * ((c - 1) // 3) + (c - 1) % 3
                    pe.wait_ge(dil_rotated, qi + 1)
                    for t in range(T):
                        if qi >= 2:
                            pe.wait_ge(dil_T_ok, 2 * qi - 3 + t)
                        for k in range(4):
                            a = (qi % 2) * 512 + k * P
                            q = pe.transpose(ps[:, 4 + 2 * (qi % 2) + t, k * P:(k + 1) * P], xn[:, t, a:a + P], ident)
                        q.then_inc(dil_tr, 1)
            pe.wait_ge(dil_rows_ok, 18)
            pe.wait_ge(dil_T_ok, 12)
            attention(N_U0, T * DH)
            pe.wait_ge(oT_ok, N_U0 // 2 + DH // 2)
            for a in range(N_DOUT):
                rows_by(C_DOUT + a, 2, D, HALVES, 4, lhs_of(2 * a), a == 0, a == N_DOUT - 1, y_ok if a == N_DOUT - 1 else None)
            pre(4)
            pe.wait_ge(xp_ok, 4 * 4 + 4)
            pe.wait_ge(wr_in, 16)
            for t in range(T):
                for k in range(KD):
                    q = mm(ps[:, 4, t * NE:(t + 1) * NE], xr[:, k, t * P:(t + 1) * P], wr[:, k, :], k == 0, k == KD - 1)
            q.then_inc(logits_mm, 1)
            pe.wait_ge(chosen_ok, 1)
            pe.wait_ge(moetab_in, 16)
            chose = [rt[:, 6, t * NE:(t + 1) * NE] for t in range(T)]
            mm(ps[:, 5, 0:NE], tri, chose[0], True, True)
            mm(ps[:, 5, NE:2 * NE], ones, chose[0], True, False)
            mm(ps[:, 5, NE:2 * NE], tri, chose[1], False, True)
            mm(ps[:, 5, 2 * NE:3 * NE], ones, chose[0], True, False)
            mm(ps[:, 5, 2 * NE:3 * NE], ones, chose[1], False, True).then_inc(places_mm, 1)

            def gather(r):
                pe.wait_ge(moe_sel_ok, r + 2)
                pe.wait_ge(moe_rows_ok, r * 2 + 1)
                for half in range(2):
                    for k in range(4):
                        a = (4 * half + k) * P
                        for t in range(T):
                            q = mm(ps[:, 6 + half, k * P:(k + 1) * P], xn[:, t, a:a + P], sel[:, t, :], t == 0, t == T - 1)
                    q.then_inc(moe_gather_mm, 1)

            def hidden_T(r, c):
                pe.wait_ge(moe_hidden, r * NFC + c + 2)
                pe.wait_ge(moe_hidden_split, r * NFC + c + 1)
                if c == 0:
                    pe.wait_ge(moe_added, r * 4 + 1)
                for k in range(FT):
                    q = pe.transpose(ps[:, 2, k * P:(k + 1) * P], mh[:, c % 2, k * P:(k + 1) * P], ident)
                q.then_inc(moe_hidden_tr, 1)

            def expert(r):
                for j, (kind, c, half) in enumerate(FFN):
                    n = C_MOE + j
                    if (kind, half) == ("u", 0) and c:
                        hidden_T(r, c - 1)
                    if (kind, c, half) == ("d", NFC - 2, 1):
                        hidden_T(r, NFC - 1)
                    if kind == "d":
                        w = chunk(pe, n, 2, D, r)
                        if half == 0:
                            pe.wait_ge(moe_hidden_split, r * NFC + c + 2)
                        if c == 0 and half == 0:
                            pe.wait_ge(moe_y_ok, r * 2 + 1)
                        for j2, (a, b) in enumerate(HALVES):
                            for k in range(2):
                                q = mm3(ps[:, 4 + j2, :], at((mhTh, mhTl), c % 2, slice((2 * half + k) * P, (2 * half + k + 1) * P)),
                                        at(w, k, slice(a, b)), c == 0 and half == 0 and k == 0,
                                        c == NFC - 1 and half == 1 and k == 1)
                            if c == NFC - 1 and half == 1 and j2 == 0:
                                q.then_inc(moe_y_mm, 1)
                    else:
                        w = chunk(pe, n, 4, FC, r)
                        if (kind, c) == ("g", 0):
                            pe.wait_ge(moe_rows_split, r * 2 + half + 2)
                        if half == 0:
                            pe.wait_ge(moe_silu if kind == "g" else moe_hidden, r * NFC + c + 1)
                        for k in range(4):
                            q = mm3(bank(0 if kind == "g" else 1), at((xgh, xgl), 4 * half + k), at(w, k, slice(0, FC)),
                                    half == 0 and k == 0, half == 1 and k == 3)
                    q.then_inc(chunk_used, 1)
                    if (kind, c, half) == ("g", 1, 1):
                        pe.wait_ge(moe_selT_ok, r + 1)
                        pe.wait_ge(moe_added, r * 4 + 1)
                        for t in range(T):
                            q = pe.transpose(ps[:, 3, t * P:(t + 1) * P], selg[:, t, :], ident)
                        q.then_inc(moe_selT_tr, 1)
                with pe.If(r < NE - 1):
                    gather(r + 1)
                pe.wait_ge(moe_selT_ok, r + 2)
                pe.wait_ge(moe_hidden_split, r * NFC + NFC + 1)
                for half in range(2):
                    pe.wait_ge(moe_y_ok, r * 2 + half + 2)
                    for t in range(T):
                        mm(bank(SCATTER_BANK[half] - t), selT[:, t, :], ysb[:, half * BANK:(half + 1) * BANK],
                           True, True).then_inc(moe_scatter_mm, 1)
                for s in (ffn_gate_mm, ffn_up_mm):
                    pe.sem_inc(s, NFC)

            def full_expert(r):
                pe.sem_inc(moe_selT_tr, 1)
                pe.wait_ge(moe_silu, r * NFC + 1)
                pe.wait_ge(moe_hidden, r * NFC + 1)
                pe.wait_ge(moe_rows_split, r * 2 + 3)
                for s, (kind, c, half) in enumerate(FFN):
                    if (kind, c, half) == ("u", 0, 0):
                        pe.wait_ge(moe_hidden_split, r * NFC + 1)
                        pe.wait_ge(moe_added, r * 4 + 1)
                    if (kind, c, half) == ("d", 0, 0):
                        pe.wait_ge(moe_y_ok, r * 2 + 1)
                    ffn_step(C_MOE, s, kind, c, half, r, r + 1, (6, 4), moe_y_mm)
                pe.sem_inc(moe_hidden_tr, NFC)
                pe.sem_inc(moe_scatter_mm, 4)
                pe.wait_ge(moe_added, r * 4 + 3)
                with pe.If(r < NE - 1):
                    gather(r + 1)

            gather(0)
            pe.wait_ge(full_ok, 1)
            pe.wait_ge(xT_ok, 4 * 4 + 4)
            with pe.Fori(0, NE) as e:
                many = pe.value_load(fulli[0:1, bass.ds(e, 1)], min_val=0, max_val=1)
                with pe.If(many > 0):
                    full_expert(e)
                with pe.If(many < 1):
                    expert(e)
            embedding_T(1)
            pe.wait_ge(moe_added, NE * 4 + 1)
            embedding(1, C_MOE, NE)
            pre(5)
            embedding_gate(1, C_MOE, NE)


def tables_of_shapes():
    f = np.float32
    tok = np.arange(SEQ).reshape(P, T)

    def angles(pos, dim, theta):
        inv = np.power(f(theta), -(np.arange(0, dim, 2, dtype=f) / f(dim)))
        a = pos.astype(f)[..., None] * inv
        return np.cos(a).astype(f), np.sin(a).astype(f)

    out = np.zeros((P, TAB_ALL), f)

    def put(at, v):
        v = np.asarray(v, f).reshape(P, -1)
        out[:, at:at + v.shape[1]] = v

    put(TAB["ident"][0], np.eye(P))
    cr, sr = angles(tok // 64, 32, 10000.0)
    cc, sc = angles(tok % 64, 32, 10000.0)
    put(TAB["axC"][0], np.concatenate([cr, cr, cc, cc], -1))
    put(TAB["axS"][0], np.concatenate([-sr, sr, -sc, sc], -1))
    for name, dim, theta in (("ml", MR, 10000.0), ("di", 16, 500000.0)):
        c, s = angles(tok, dim, theta)
        put(TAB[name + "C"][0], np.concatenate([c, c], -1))
        put(TAB[name + "S"][0], np.concatenate([-s, s], -1))
    put(TAB["rev"][0], np.tile(NE - np.arange(NE), (P, T)))
    i = np.arange(P)
    put(TAB_MOE, i[:, None] < i[None, :])
    put(TAB_MOE + P, np.ones((P, P)))
    put(TAB_MOE + 2 * P, np.tile(np.arange(P), (P, 1)))
    for t in range(T):
        q = tok[:, t][:, None]
        keys = [np.abs(q - tok[:, k][None]) <= 64 for k in range(T)]
        keys += [(q - tok[:, t][None]) % dil == 0 for dil in (4, 16)]
        put(TAB_MASK + t * BANK, np.where(np.concatenate(keys, 1), 0.0, NEG))
    return out


INS = ["x", "p", "mix_pre_g", "mix_post_g", "ffn_pre_g", "ffn_post_g", "ple_w_proj", "ple_gate_norm_g",
       "ple_w_gate", "ple_post_g", "ab_w_in", "gqa_q_norm_g", "gqa_k_norm_g", "mla_q_norm_g", "mla_w_uq",
       "mla_kv_norm_g", "mla_w_ukv", "ab_w_out", "ffn_w_gate", "ffn_w_up", "ffn_w_down", "dil_w_qkv",
       "dil_w_out", "moe_w_router", "moe_w_gate", "moe_w_up", "moe_w_down"]


def kernel(**inputs):
    import concourse.bacc as bacc
    from concourse.bass_utils import run_bass_kernel_spmd

    nc = bacc.Bacc("TRN2", target_bir_lowering=False, num_devices=1)
    arrays, args = {}, []
    for name in INS:
        arrays["in_" + name] = np.ascontiguousarray(inputs[name])
    arrays["in_tables"] = tables_of_shapes()
    for name, a in arrays.items():
        args.append(nc.dram_tensor(name, a.shape, mybir.dt.from_np(a.dtype), kind="ExternalInput").ap())
    args.append(nc.dram_tensor("out_h", (1, SEQ, D), F32, kind="ExternalOutput").ap())
    hybrid_encoder(nc, *args)
    r = run_bass_kernel_spmd(nc, [arrays], core_ids=[0])
    return r.results[0]["out_h"]
```
